# Optimizing a Trainium2 kernel written in Bass

```python
import math
import jax, jax.numpy as jnp
from jax import lax
import numpy as np

D_MODEL = 2048
BATCH = 1
SEQ = 512
DEPTH = 1

CTX_LEN = 256
GRID_W = 64
S5_WIDTH = 1024
S5_GROUP = 16
S5_GROUPS = S5_WIDTH // S5_GROUP
S5_STATE = 64
HY_WIDTH = 1024
HY_BANDS = 16
HY_POS_DIM = 1 + 2 * HY_BANDS
HY_HIDDEN = 64
HY_DECAY_TARGET = 1e-2
HY_FAST_PCT = 0.3
HY_SLOW_PCT = 1.5
SHORT_CONV = 3
D_FF = -(-8 * D_MODEL // (3 * 256)) * 256
IN_COLS = S5_WIDTH + 3 * HY_WIDTH + 2 * D_MODEL
N_ADA = 6
EPS = 1e-6
DT_MIN = 1e-3
DT_MAX = 1e-1

kernel_name = "hybrid_s5_hyena_prefix_dit_block"

def rms_norm(x, g):
    xf = x.astype(jnp.float32)
    y = xf * lax.rsqrt(jnp.mean(xf * xf, axis=-1, keepdims=True) + EPS)
    return (y * g.astype(jnp.float32)).astype(x.dtype)

def modulate(x, g, shift, scale):
    return rms_norm(x, g) * (1.0 + scale[:, None, :]) + shift[:, None, :]

def sincos_2d(n_rows, dim):
    rows = jnp.repeat(jnp.arange(n_rows, dtype=jnp.float32), GRID_W)
    cols = jnp.tile(jnp.arange(GRID_W, dtype=jnp.float32), n_rows)
    quarter = dim // 4
    omega = 10000.0 ** (-jnp.arange(quarter, dtype=jnp.float32) / quarter)
    ar = rows[:, None] * omega
    ac = cols[:, None] * omega
    return jnp.concatenate([jnp.sin(ar), jnp.cos(ar), jnp.sin(ac), jnp.cos(ac)], axis=-1)

def linear_recurrence(e_i, e_j):
    a_i, b_i = e_i
    a_j, b_j = e_j
    return a_j * a_i, a_j * b_i + b_j

def s5_scan(u, a_re, a_im, log_dt, b_re, b_im, init, reverse):
    f32 = jnp.float32
    lam = lax.complex(a_re.astype(f32), a_im.astype(f32))
    lam_bar = jnp.exp(lam * jnp.exp(log_dt.astype(f32))[:, None])
    b_bar = ((lam_bar - 1.0) / lam)[:, :, None] * lax.complex(b_re.astype(f32), b_im.astype(f32))
    uf = u.astype(f32)
    bu = lax.complex(jnp.einsum("gph,blgh->blgp", b_bar.real, uf),
                     jnp.einsum("gph,blgh->blgp", b_bar.imag, uf))
    n = bu.shape[1]
    if init is not None:
        edge = n - 1 if reverse else 0
        bu = bu.at[:, edge].add(lam_bar * init)
    a = jnp.broadcast_to(lam_bar, (1, n) + lam_bar.shape)
    _, states = lax.associative_scan(linear_recurrence, (a, bu), reverse=reverse, axis=1)
    return states

def s5_states(u, lp, d, init, reverse):
    bsz, n, _ = u.shape
    ug = u.reshape(bsz, n, S5_GROUPS, S5_GROUP)
    return s5_scan(ug, lp["s5_a_re"][d], lp["s5_a_im"][d], lp["s5_log_dt"][d],
                   lp["s5_b_re"][d], lp["s5_b_im"][d], init, reverse)

def s5_readout(states, lp, d):
    f32 = jnp.float32
    return (jnp.einsum("ghp,blgp->blgh", lp["s5_c_re"][d].astype(f32), states.real)
            - jnp.einsum("ghp,blgp->blgh", lp["s5_c_im"][d].astype(f32), states.imag))

def centred_short_conv(u, w, b):
    n = u.shape[1]
    up = jnp.pad(u, ((0, 0), (1, 1), (0, 0)))
    return up[:, :n] * w[0] + up[:, 1:n + 1] * w[1] + up[:, 2:] * w[2] + b

def hyena_filters(n, lp):
    f32 = jnp.float32
    pos = jnp.arange(n, dtype=f32)
    t = pos / float(max(n - 1, 1))
    w = 2.0 * math.pi * pos / n
    bands = jnp.linspace(1e-4, HY_BANDS - 1, HY_BANDS, dtype=f32)
    feats = jnp.concatenate([t[:, None], jnp.cos(w[:, None] * bands), -jnp.sin(w[:, None] * bands)], axis=-1)
    h = jnp.sin(lp["hy_f1_freq"].astype(f32) * (feats @ lp["hy_f1_w"].astype(f32) + lp["hy_f1_b"].astype(f32)))
    h = jnp.sin(lp["hy_f2_freq"].astype(f32) * (h @ lp["hy_f2_w"].astype(f32) + lp["hy_f2_b"].astype(f32)))
    h = (h @ lp["hy_f3_w"].astype(f32)).reshape(n, 2, HY_WIDTH)
    window = jnp.exp(-t[:, None, None] * jnp.abs(lp["hy_decay"].astype(f32))[None])
    return h * window

def bidirectional_long_conv(u, h, bias):
    f32 = jnp.float32
    n = u.shape[1]
    h_fwd, h_bwd = h[:, 0], h[:, 1]
    taps = jnp.concatenate([h_fwd, jnp.zeros((1, HY_WIDTH), f32), h_bwd[:0:-1]], axis=0)
    kf = jnp.fft.rfft(taps, n=2 * n, axis=0)
    uf = jnp.fft.rfft(u.astype(f32), n=2 * n, axis=1)
    y = jnp.fft.irfft(uf * kf[None], n=2 * n, axis=1)[:, :n]
    return (y + u.astype(f32) * bias.astype(f32)).astype(u.dtype)

def hyena_branch(hy, lp):
    z = centred_short_conv(hy, lp["hy_conv_w"], lp["hy_conv_b"])
    x0, x1, v = jnp.split(z, 3, axis=-1)
    h = hyena_filters(hy.shape[1], lp)
    return x0 * bidirectional_long_conv(x1 * v, h, lp["hy_bias"])

def mixer_output(u, y_ssm, hy, gates, lp):
    y = (y_ssm.reshape(u.shape) + u.astype(jnp.float32) * lp["s5_d"].astype(jnp.float32)).astype(u.dtype)
    yg = jax.nn.gelu(y)
    glu_v, glu_g = jnp.split(yg @ lp["w_glu"], 2, axis=-1)
    branch_s5 = glu_v * jax.nn.sigmoid(glu_g)
    branch_hy = hyena_branch(hy, lp) @ lp["w_hy_out"]
    gate_s5, gate_hy = jnp.split(gates, 2, axis=-1)
    merged = jax.nn.sigmoid(gate_s5) * branch_s5 + jax.nn.sigmoid(gate_hy) * branch_hy
    return merged @ lp["w_out"]

def swiglu(h, w_in, w_out):
    a, b = jnp.split(h @ w_in, 2, axis=-1)
    return (jax.nn.silu(a) * b) @ w_out

def setup_inputs(seed: int = 0) -> dict:
    key = jax.random.key(seed)
    ks = iter(jax.random.split(key, 48))
    f32 = jnp.float32

    def nrm(shape, scale):
        return jax.random.normal(next(ks), shape, f32) * scale

    L, G, P, H = DEPTH, S5_GROUPS, S5_STATE, S5_GROUP
    n_idx = jnp.arange(P, dtype=f32)
    decay_base = jnp.linspace(math.log(HY_DECAY_TARGET) / HY_SLOW_PCT,
                              math.log(HY_DECAY_TARGET) / HY_FAST_PCT, HY_WIDTH, dtype=f32)
    return {
        "x": nrm((BATCH, SEQ, D_MODEL), 1.0),
        "c": nrm((BATCH, D_MODEL), 1.0),
        "ctx": nrm((BATCH, CTX_LEN, D_MODEL), 1.0),
        "c_ctx": nrm((D_MODEL,), 0.5),
        "w_ada": nrm((L, D_MODEL, N_ADA * D_MODEL), 0.2 * D_MODEL ** -0.5),
        "b_ada": nrm((L, N_ADA * D_MODEL), 0.01),
        "norm_mix": 1.0 + nrm((L, D_MODEL), 0.02),
        "w_in": nrm((L, D_MODEL, IN_COLS), D_MODEL ** -0.5),
        "s5_a_re": -0.5 + nrm((L, 2, G, P), 0.01),
        "s5_a_im": math.pi * n_idx + nrm((L, 2, G, P), 0.01),
        "s5_log_dt": jax.random.uniform(next(ks), (L, 2, G), f32, math.log(DT_MIN), math.log(DT_MAX)),
        "s5_b_re": nrm((L, 2, G, P, H), (2 * H) ** -0.5),
        "s5_b_im": nrm((L, 2, G, P, H), (2 * H) ** -0.5),
        "s5_c_re": nrm((L, 2, G, H, P), 0.5),
        "s5_c_im": nrm((L, 2, G, H, P), 0.5),
        "s5_d": nrm((L, S5_WIDTH), 1.0),
        "w_glu": nrm((L, S5_WIDTH, 2 * D_MODEL), S5_WIDTH ** -0.5),
        "hy_conv_w": nrm((L, SHORT_CONV, 3 * HY_WIDTH), 0.5),
        "hy_conv_b": nrm((L, 3 * HY_WIDTH), 0.01),
        "hy_f1_w": nrm((L, HY_POS_DIM, HY_HIDDEN), HY_POS_DIM ** -0.5),
        "hy_f1_b": nrm((L, HY_HIDDEN), 0.1),
        "hy_f1_freq": 1.0 + nrm((L, HY_HIDDEN), 0.02),
        "hy_f2_w": nrm((L, HY_HIDDEN, HY_HIDDEN), HY_HIDDEN ** -0.5),
        "hy_f2_b": nrm((L, HY_HIDDEN), 0.1),
        "hy_f2_freq": 1.0 + nrm((L, HY_HIDDEN), 0.02),
        "hy_f3_w": nrm((L, HY_HIDDEN, 2 * HY_WIDTH), 0.05 * HY_HIDDEN ** -0.5),
        "hy_decay": decay_base + nrm((L, 2, HY_WIDTH), 0.1),
        "hy_bias": nrm((L, HY_WIDTH), 1.0),
        "w_hy_out": nrm((L, HY_WIDTH, D_MODEL), HY_WIDTH ** -0.5),
        "w_out": nrm((L, D_MODEL, D_MODEL), D_MODEL ** -0.5),
        "norm_ffn": 1.0 + nrm((L, D_MODEL), 0.02),
        "w_ffn_in": nrm((L, D_MODEL, 2 * D_FF), D_MODEL ** -0.5),
        "w_ffn_out": nrm((L, D_FF, D_MODEL), D_FF ** -0.5),
        "norm_f": 1.0 + nrm((D_MODEL,), 0.02),
    }

def reference(x, c, ctx, c_ctx, w_ada, b_ada, norm_mix, w_in, s5_a_re, s5_a_im, s5_log_dt,
              s5_b_re, s5_b_im, s5_c_re, s5_c_im, s5_d, w_glu, hy_conv_w, hy_conv_b,
              hy_f1_w, hy_f1_b, hy_f1_freq, hy_f2_w, hy_f2_b, hy_f2_freq, hy_f3_w, hy_decay,
              hy_bias, w_hy_out, w_out, norm_ffn, w_ffn_in, w_ffn_out, norm_f):
    n_lat = x.shape[1]
    n_rows = n_lat // GRID_W
    x = x + sincos_2d(n_rows, D_MODEL).astype(x.dtype)[None]
    silu_c = jax.nn.silu(c)
    silu_cc = jax.nn.silu(c_ctx)[None]

    for l in range(DEPTH):
        lp = {
            "s5_a_re": s5_a_re[l], "s5_a_im": s5_a_im[l], "s5_log_dt": s5_log_dt[l],
            "s5_b_re": s5_b_re[l], "s5_b_im": s5_b_im[l],
            "s5_c_re": s5_c_re[l], "s5_c_im": s5_c_im[l],
            "s5_d": s5_d[l], "w_glu": w_glu[l],
            "hy_conv_w": hy_conv_w[l], "hy_conv_b": hy_conv_b[l],
            "hy_f1_w": hy_f1_w[l], "hy_f1_b": hy_f1_b[l], "hy_f1_freq": hy_f1_freq[l],
            "hy_f2_w": hy_f2_w[l], "hy_f2_b": hy_f2_b[l], "hy_f2_freq": hy_f2_freq[l],
            "hy_f3_w": hy_f3_w[l], "hy_decay": hy_decay[l], "hy_bias": hy_bias[l],
            "w_hy_out": w_hy_out[l], "w_out": w_out[l],
        }
        shift_mix, scale_mix, gate_mix, shift_ffn, scale_ffn, gate_ffn = jnp.split(
            silu_c @ w_ada[l] + b_ada[l], N_ADA, axis=-1)
        cshift_mix, cscale_mix, cgate_mix, cshift_ffn, cscale_ffn, cgate_ffn = jnp.split(
            silu_cc @ w_ada[l] + b_ada[l], N_ADA, axis=-1)

        h_c = modulate(ctx, norm_mix[l], cshift_mix, cscale_mix)
        u_c = h_c @ w_in[l][:, :S5_WIDTH]
        st_ctx_f = s5_states(u_c, lp, 0, None, False)
        st_ctx_b = s5_states(u_c, lp, 1, None, True)

        h_x = modulate(x, norm_mix[l], shift_mix, scale_mix)
        p_x = h_x @ w_in[l]
        u_x, hy_x, gates_x = jnp.split(p_x, [S5_WIDTH, S5_WIDTH + 3 * HY_WIDTH], axis=-1)
        y_x = (s5_readout(s5_states(u_x, lp, 0, st_ctx_f[:, -1], False), lp, 0)
               + s5_readout(s5_states(u_x, lp, 1, st_ctx_b[:, 0], True), lp, 1))
        x = x + gate_mix[:, None] * mixer_output(u_x, y_x, hy_x, gates_x, lp)
        x = x + gate_ffn[:, None] * swiglu(modulate(x, norm_ffn[l], shift_ffn, scale_ffn),
                                           w_ffn_in[l], w_ffn_out[l])

        if l < DEPTH - 1:
            hy_c, gates_c = jnp.split(h_c @ w_in[l][:, S5_WIDTH:], [3 * HY_WIDTH], axis=-1)
            y_c = s5_readout(st_ctx_f, lp, 0) + s5_readout(st_ctx_b, lp, 1)
            ctx = ctx + cgate_mix[:, None] * mixer_output(u_c, y_c, hy_c, gates_c, lp)
            ctx = ctx + cgate_ffn[:, None] * swiglu(modulate(ctx, norm_ffn[l], cshift_ffn, cscale_ffn),
                                                    w_ffn_in[l], w_ffn_out[l])

    return rms_norm(x, norm_f)


_drawn_inputs = setup_inputs


def setup_inputs(seed=0):
    import zlib

    import numpy as np

    out = dict(_drawn_inputs(seed))
    spreads = {}
    factors = {'ctx': 64.0,
     'c_ctx': 64.0,
     'b_ada': 8.0,
     'norm_mix': 8.0,
     's5_a_re': 64.0,
     's5_a_im': 34.408,
     's5_log_dt': 44.096,
     's5_b_re': 41.944,
     's5_b_im': 44.6,
     's5_c_re': 45.328,
     's5_c_im': 46.992,
     's5_d': 3.054,
     'hy_conv_b': 8.0,
     'hy_f1_w': 5.27,
     'hy_f1_b': 8.0,
     'hy_f1_freq': 8.0,
     'hy_f2_w': 4.817,
     'hy_f2_b': 8.0,
     'hy_f2_freq': 8.0,
     'hy_f3_w': 4.579,
     'hy_decay': 8.0,
     'norm_ffn': 64.0,
     'norm_f': 7.994}
    for name, (base, spread) in spreads.items():
        noise = np.random.default_rng([zlib.crc32(name.encode()), seed]).standard_normal(out[name].shape)
        drawn = base * np.exp(spread * noise) if base else spread * noise
        out[name] = __import__('jax').numpy.asarray(drawn.astype(out[name].dtype))
    for name, factor in factors.items():
        out[name] = (out[name] * factor).astype(out[name].dtype)
    return out
```

```python
import math
from contextlib import contextmanager

import numpy as np

import concourse.bass as bass
from concourse import mybir

P = 128
D = 2048
SEQ = 512
CTX = 256
GRID = 64
S5W = 1024
HYW = 1024
STATE = 64
GROUP = 16
HID = 64
BANDS = 16
POSD = 1 + 2 * BANDS
DFF = 5632
EPS = 1e-6

KT = D // P
ST = S5W // P
NPAIR = S5W // 32
NDQ = 2 * NPAIR
CH = 8
NC_CTX = CTX // CH
NC_LAT = SEQ // CH
NCH = NC_CTX + NC_LAT
UNIT = KT * P
QTILES = DFF // P // 4
UNIT2 = QTILES * P
N_ADA = 96
N_ADA0 = 32

U_IN = 0
U_TAB = 64
U_MRG = 68
U_OUT = 100
U_FFN = 116
U_QUARTER = 2 * QTILES + KT

V_NM, V_NF, V_NO, V_C, V_CC, V_BADA = 0, 16, 32, 48, 64, 80
V_CW, V_CB, V_HB, V_D4, V_NEGT, NVEC = 176, 248, 272, 280, 312, 316

F32 = mybir.dt.float32
F32R = mybir.dt.float32r
ALU = mybir.AluOpType
ACT = mybir.ActivationFunctionType
MUL, ADD, SUB = ALU.mult, ALU.add, ALU.subtract

MAGIC = 12582912.0
TWO_PI_1 = 6.28125
TWO_PI_2 = float(np.float32(np.round((2 * math.pi - TWO_PI_1) * 2.0 ** 20) / 2.0 ** 20))
TWO_PI_3 = float(np.float32(2 * math.pi - TWO_PI_1 - TWO_PI_2))
PI_SAFE = 3.1415925


class Chain:

    def __init__(self, eng, sem):
        self.eng, self.sem, self.base, self.k = eng, sem, 0, 0

    def mark(self, ins):
        ins.then_inc(self.sem, 1)
        self.k += 1

    def wait(self):
        self.eng.wait_ge(self.sem, self.base + self.k)

    def link(self, ins):
        self.mark(ins)
        self.wait()

    @contextmanager
    def loop(self, lo, hi, marks):
        start = self.base + self.k
        with self.eng.Fori(lo, hi) as i:
            self.base, self.k = start + (i - lo) * marks, 0
            yield i
            assert self.k == marks, (self.k, marks)
        self.base, self.k = start + (hi - lo) * marks, 0


def block_kernel(nc, vecs_d, w_ada_d, w_in_d, w_glu_d, w_hy_d, w_out_d, w_fi_d, w_fo_d, x_d, ctx_d,
                 s5a_d, s5b_d, s5c_d, f1w_d, f2w_d, f3w_d, fpar_d, decay_d, feats_d, postab_d,
                 tabs_d, ident_d, out_d, xp_d, gates_d, kf_d):
    kb = 1024
    base = (nc.sbuf_base + 63) // 64 * 64

    def at(name, off_kb, shape, dt=F32):
        return nc.alloc_sbuf_tensor_at(name, shape, dt, offset=base + int(off_kb * kb))

    raw = [at("w_raw0", 0, [P, UNIT]), at("w_raw1", 8, [P, UNIT])]
    hi = [at("w_hi0", 16, [P, UNIT], F32R), at("w_hi1", 32, [P, UNIT], F32R)]
    lo = [at("w_lo0", 24, [P, UNIT], F32R), at("w_lo1", 40, [P, UNIT], F32R)]
    small = 48
    vecs = at("vecs", small, [P, NVEC])
    o = small + 320 * 4 / kb
    silu_c = at("silu_c", o, [P, KT, 2]); o += 32 * 4 / kb
    mod_x = at("mod_x", o, [P, N_ADA]); o += N_ADA * 4 / kb
    mod_c = at("mod_c", o, [P, N_ADA0]); o += N_ADA0 * 4 / kb
    mul_x = at("mul_x", o, [P, KT]); o += KT * 4 / kb
    mul_c = at("mul_c", o, [P, KT]); o += KT * 4 / kb
    mul_f = at("mul_f", o, [P, KT]); o += 2 * KT * 4 / kb
    ident = at("ident", o, [P, P]); o += P * 4 / kb
    ones = at("ones", o, [P, P]); o += P * 4 / kb
    pow_at = o
    pow_c = at("pow_c", o, [P, 2, CH + 1, NDQ]); o += 2 * (CH + 1) * NDQ * 4 / kb
    pow_b = at("pow_b", o, [P, 2, CH, NDQ]); o += 2 * CH * NDQ * 4 / kb
    lam_rr = at("lam_rr", o, [P, 2, NDQ]); o += 2 * NDQ * 4 / kb
    lam_ii = at("lam_ii", o, [P, 2, NDQ]); o += 2 * NDQ * 4 / kb
    assert o <= 62, o
    tab_f = at("tab_f", 62, [P, 2, 4, 512])
    taps_s = at("taps_sum", 78, [P, 4, HYW])
    taps_d = at("taps_dif", 94, [P, 4, HYW])
    decay = at("decay", 110, [P, 2 * HYW])
    f3w = at("f3w", 118, [P, 2 * HYW])
    x_raw = at("x_raw", 126, [P, KT, SEQ])
    c_raw = at("c_raw", 158, [P, KT, CTX])
    ada0 = [at(f"ada0_{j}", 174 + 8 * j, [P, UNIT]) for j in range(4)]
    postab = at("postab", 0, [P, 8, 8 + GRID])
    sqr = [at(f"sqr{j}", 8 + 2 * j, [P, 512]) for j in range(2)]
    T = [at(f"tmp{j}", 16 + 2 * j, [P, 512]) for j in range(16)]
    h_hi = at("h_hi", 62, [P, KT, SEQ], F32R)
    h_lo = at("h_lo", 94, [P, KT, SEQ], F32R)
    hc_hi = at("hc_hi", 126, [P, KT, CTX], F32R)
    hc_lo = at("hc_lo", 142, [P, KT, CTX], F32R)
    gst = [at(f"gate_st{j}", 158 + 2 * j, [P, SEQ]) for j in range(2)]
    zx1 = at("zx1", 162, [P, SEQ])
    ada1 = [at(f"ada1_{j}", 166 + 8 * j, [P, UNIT]) for j in range(2)]
    u_ch = at("u_ch", 182, [P, ST, CTX + SEQ])
    uh = at("uh", 126, [P, ST, SEQ])
    x0z = at("x0z", 142, [P, ST, SEQ])
    X = at("states", 62, [P, NCH, 2, NDQ])
    s5b = at("s5b", 110, [P, NDQ, 2, GROUP])
    s5c = at("s5c", 118, [P, NDQ, 2, GROUP])
    U4 = at("u4", 158, [P, NPAIR, (CTX + SEQ) // 4])
    bbar = at("bbar", 182, [P, NDQ, 2, 32])
    BL = [at(f"b_lam{d}", 16 + 2 * d, [P, 2, CH, 32]) for d in range(2)]
    MT = [at(f"m_in{d}", 20 + 2 * d, [P, 4, P]) for d in range(2)]
    prod = [at(f"prod{j}", 24 + 1.25 * j, [P, 2, CH + 1, GROUP]) for j in range(4)]
    CL = [[at(f"c_lam{par}{d}", (30, 16)[par] + 2.5 * d, [P, 2, CH + 1, 32]) for d in range(2)] for par in range(2)]
    BB = [at(f"b_rep{d}", 35 + d, [P, 2, 4, 32]) for d in range(2)]
    TL = at("toeplitz", 38, [P, 2, CH, 32])
    rec = [at(f"rec{j}", 42 + 0.5 * j, [P, 2, NDQ]) for j in range(2)]
    XR = [at(f"states_back{j}", 43 + 0.5 * j, [P, 2, NC_LAT]) for j in range(2)]
    bt = [at(f"bt{j}", 24 + 2 * j, [P, NPAIR, GROUP]) for j in range(4)]
    y_ch = at("y_ch", 94, [P, ST, SEQ])
    yg_hi = at("yg_hi", 62, [P, ST, SEQ], F32R)
    yg_lo = at("yg_lo", 78, [P, ST, SEQ], F32R)
    uT_hi = at("uT_hi", 94, [P, 4, 512], F32R)
    uT_lo = at("uT_lo", 102, [P, 4, 512], F32R)
    tf_hi = at("tf_hi", 158, [P, 2, 4, 512], F32R)
    tf_lo = at("tf_lo", 174, [P, 2, 4, 512], F32R)
    tg_hi = at("tg_hi", 110, [P, 2, 4, 512], F32R)
    tg_lo = at("tg_lo", 190, [P, 2, 4, 512], F32R)
    Y_hi = at("Y_hi", 16, [P, 2, 4, 512], F32R)
    Y_lo = at("Y_lo", 32, [P, 2, 4, 512], F32R)
    kfr = [at(f"kf_in{j}", 8 + 4 * j, [P, 2, 512]) for j in range(2)]
    ct = [at(f"ct{j}", pow_at + 2 * j, [P, 512]) for j in range(4)]
    hyo_hi = at("hyo_hi", 126, [P, ST, SEQ], F32R)
    hyo_lo = at("hyo_lo", 142, [P, ST, SEQ], F32R)
    mg_hi = at("mg_hi", 94, [P, KT, SEQ], F32R)
    mg_lo = at("mg_lo", 158, [P, KT, SEQ], F32R)
    gT = [at(f"gates{j}", 190 + 4 * j, [P, 2, SEQ]) for j in range(2)]
    S0 = [at(f"mrg_a{j}", 198 + 2 * j, [P, SEQ]) for j in range(2)]
    S1 = [at(f"mrg_b{j}", 202 + 2 * j, [P, SEQ]) for j in range(2)]
    xacc = at("xacc", 126, [P, KT, SEQ])
    h2_hi = at("h2_hi", 62, [P, KT, SEQ], F32R)
    h2_lo = at("h2_lo", 94, [P, KT, SEQ], F32R)
    a_hi = at("act_hi", 158, [P, QTILES, SEQ], F32R)
    a_lo = at("act_lo", 180, [P, QTILES, SEQ], F32R)
    f_s = at("ffn_silu", 202, [P, SEQ])
    f_t = at("ffn_prod", 204, [P, SEQ])

    ps = [nc.alloc_psum_tensor(f"ps{j}", [P, 512], F32) for j in range(8)]

    fh = [at(f"fh{j}", 16 + 2 * j, [HID, SEQ]) for j in range(4)]
    lt = at("lam_tmp", 32.75, [P, 13, NDQ])
    s5a = at("s5a", 32, [P, 3, NDQ])
    feats = at("feats", 36, [POSD, SEQ])
    f1w = at("f1w", 38, [POSD, HID])
    f2w = at("f2w", 38.5, [HID, HID])
    fpar = at("fpar", 39, [HID, 4])
    pwt = at("pow_b_tmp", 39.5, [P, 2, CH, NPAIR])
    pw = at("pow_tmp", 42, [P, 2, CH + 1, NDQ])

    def sem(name):
        return nc.alloc_semaphore(name)

    s_vec, s_par, s_filt, s_tabf, s_x, s_ctx = (sem(n) for n in
        ("vec_loaded", "s5a_loaded", "filter_loaded", "tabf_loaded", "x_loaded", "ctx_loaded"))
    s_pos = sem("postab_loaded")
    ada0_in = [sem(f"ada0_loaded{j}") for j in range(4)]
    ada0_used, ada1_used = sem("ada0_used"), sem("ada1_used")
    ada1_in = [sem(f"ada1_loaded{j}") for j in range(2)]
    w_in = [sem(f"w_loaded{j}") for j in range(2)]
    w_hi, w_lo, w_used = sem("w_hi_ready"), sem("w_lo_ready"), sem("w_used")
    dch, ach, pch = sem("dve_chain"), sem("act_chain"), sem("pool_chain")
    s_silu = sem("silu_c_ready")
    s_mod = sem("mod_ready")
    ada0_ps, ada1_ps = sem("ada0_psum"), sem("ada1_psum")
    s_h1p, s_h1a, s_h1 = sem("filter_psum"), sem("filter_arg"), sem("filter_sin")
    f3_ps, f3_free, s_win, s_tap = sem("f3_psum"), sem("f3_free"), sem("window_ready"), sem("taps_ready")
    s_absd = sem("decay_abs")
    kf_ps, kf_free_a, kf_free_d = (sem(n) for n in ("kf_psum", "kf_evac_act", "kf_evac_dve"))
    kf_out = [sem(f"kf_stored{j}") for j in range(2)]
    lam_z, lam_s = sem("lam_arg"), sem("lam_sin")
    s_xp, s_xpo, s_sq, s_squ = sem("xp_ready"), sem("xp_stored"), sem("square_ready"), sem("square_used")
    s_var, s_sqrt = sem("var_ready"), sem("sqrt_ready")
    s_ss = sem("sumsq_psum")
    s_cmod, s_hv, s_hh, s_hl = sem("const_ready"), sem("h_ready"), sem("h_hi_ready"), sem("h_lo_ready")
    u_ps, u_fa, u_fd = sem("u_psum"), sem("u_evac_act"), sem("u_evac_dve")
    hy_ps, hy_free = sem("hy_psum"), sem("hy_free")
    g_ps, g_free, g_rd = sem("gate_psum"), sem("gate_free"), sem("gate_ready")
    g_st = [sem(f"gate_stored{j}") for j in range(2)]
    s_bc = sem("s5bc_loaded")
    u4a, u4d = sem("u4_act"), sem("u4_dve")
    bl_rd, bl_tr, mt_rd, xs_ps, xs_ev = (sem(n) for n in ("blam_ready", "blam_transposed", "m_in_ready", "x_psum", "x_stored"))
    rec_dn = sem("scan_done")
    cl_rd, bb_rd, l_ps, tl_a, tl_d, y_ps, y_ev = (sem(n) for n in
        ("clam_ready", "brep_ready", "taps_psum", "toepl_act", "toepl_dve", "y_psum", "y_stored"))
    ych, ycd, gel, ygh, ygl = (sem(n) for n in ("ych_act", "ych_dve", "gelu_ready", "yg_hi_ready", "yg_lo_ready"))
    tab_h, tab_l = sem("tab_hi_ready"), sem("tab_lo_ready")
    ut_ps, ut_h, ut_l = sem("uT_psum"), sem("uT_hi_ready"), sem("uT_lo_ready")
    pq_ps, pq_ev, k_in = sem("spec_psum"), sem("spec_free"), [sem(f"kf_in{j}") for j in range(2)]
    yv, yh, yl = sem("Y_ready"), sem("Y_hi_ready"), sem("Y_lo_ready")
    cv_ps, cv_free, ov, oh, ol = (sem(n) for n in ("conv_psum", "conv_free", "hyo_ready", "hyo_hi_ready", "hyo_lo_ready"))
    gt_in = [sem(f"gates_loaded{j}") for j in range(2)]
    m_gl, m_sg, m_hp, m_free, m_sum, m_hi, m_lo = (sem(n) for n in
        ("glu_psum", "glu_sigmoid", "hyout_psum", "merge_free", "merged_ready", "merged_hi_ready", "merged_lo_ready"))
    xa_in = [sem(f"xacc_loaded{j}") for j in range(4)]
    o_ps, o_free = sem("out_psum"), sem("out_free")
    s_acc = sem("acc_ready")
    s_hm = sem("h_scaled")
    fa_ps, fa_free, fb_ps, fb_free, ft_rd, fh_rd, fl_rd = (sem(n) for n in
        ("ffn_a_psum", "ffn_a_free", "ffn_b_psum", "ffn_b_free", "ffn_prod_ready", "ffn_hi_ready", "ffn_lo_ready"))
    fd_ps, fd_free = sem("ffn_out_psum"), sem("ffn_out_free")
    o_rd, s_out = sem("out_ready"), sem("out_stored")

    def halves(tensor, ri, idx0, idx1):
        return [tensor[64 * g:64 * g + 64, ri, idx0:idx1, 16 * g:16 * g + 16] for g in range(2)]

    gates_v = gates_d.rearrange("(g m) p t -> g m p t", g=2)

    with nc.Block() as block:
        @block.sync
        def _(sp):
            sp.dma_start(vecs[:, :], vecs_d).then_inc(s_vec, 16)
            sp.dma_start(ident[:, :], ident_d).then_inc(s_vec, 16)
            sp.dma_start(s5a[:, :, :], s5a_d).then_inc(s_par, 16)
            sp.dma_start(feats[:, :], feats_d).then_inc(s_filt, 16)
            sp.dma_start(f1w[:, :], f1w_d).then_inc(s_filt, 16)
            sp.dma_start(f2w[:, :], f2w_d).then_inc(s_filt, 16)
            sp.dma_start(fpar[:, :], fpar_d).then_inc(s_filt, 16)
            sp.dma_start(f3w[0:HID, :], f3w_d).then_inc(s_filt, 16)
            sp.dma_start(decay[:, :], decay_d.to_broadcast([P, 2 * HYW])).then_inc(s_filt, 16)
            for s in range(2):
                sp.dma_start(tab_f[:, s, :, :], tabs_d[s].rearrange("p (t k) -> p t k", t=4)).then_inc(s_tabf, 16)
            with sp.Fori(0, N_ADA0 // 4) as i:
                for j in range(4):
                    sp.wait_ge(ada0_used, 4 * i + j + 1)
                    sp.dma_start(ada0[j][:, :], w_ada_d[4 * i + j]).then_inc(ada0_in[j], 16)
            sp.wait_ge(s_xp, KT)
            sp.dma_start(raw[0][:, :], w_in_d[0]).then_inc(w_in[0], 16)
            sp.wait_ge(s_squ, 2 * KT + 2)
            sp.dma_start(raw[1][:, :], w_in_d[1]).then_inc(w_in[1], 16)
            with sp.Fori(1, 32) as i:
                for b in range(2):
                    sp.wait_ge(w_lo, 2 * i + b - 1)
                    sp.dma_start(raw[b][:, :], w_in_d[2 * i + b]).then_inc(w_in[b], 16)
            for s in range(4):
                sp.wait_ge(w_lo, U_TAB + s - 1)
                sp.dma_start(raw[s % 2][:, :], tabs_d[s]).then_inc(w_in[s % 2], 16)
            sp.wait_ge(w_lo, U_MRG)
            sp.dma_start(raw[0][:, :], w_glu_d[0]).then_inc(w_in[0], 16)
            for half in range(2):
                for f in range(4):
                    j = f % 2
                    if 4 * half + f >= 2:
                        sp.wait_ge(pq_ev, 4 * half + f - 1)
                    sp.dma_start(kfr[j][:, :, :],
                                 kf_d[f, :, :, 512 * half:512 * half + 512].rearrange("s p c -> p s c")
                                 ).then_inc(k_in[j], 16)
            sp.wait_ge(pq_ev, 8)
            sp.dma_start(raw[1][:, 0:1024], w_hy_d[0]).then_inc(w_in[1], 16)
            with sp.Fori(1, 16) as m:
                sp.wait_ge(w_lo, U_MRG + 2 * m - 1)
                sp.dma_start(raw[0][:, :], w_glu_d[m]).then_inc(w_in[0], 16)
                sp.wait_ge(w_lo, U_MRG + 2 * m)
                sp.dma_start(raw[1][:, 0:1024], w_hy_d[m]).then_inc(w_in[1], 16)
            with sp.Fori(0, 8) as i:
                for b in range(2):
                    sp.wait_ge(w_lo, U_OUT + 2 * i + b - 1)
                    sp.dma_start(raw[b][:, :], w_out_d[2 * i + b]).then_inc(w_in[b], 16)
            for q in range(4):
                n0 = U_FFN + U_QUARTER * q
                with sp.Fori(0, QTILES) as i:
                    for b in range(2):
                        sp.wait_ge(w_lo, n0 + 2 * i + b - 1)
                        sp.dma_start(raw[b][:, :], w_fi_d[2 * QTILES * q + 2 * i + b]).then_inc(w_in[b], 16)
                with sp.Fori(0, KT // 2) as i:
                    for b in range(2):
                        sp.wait_ge(w_lo, n0 + 2 * QTILES + 2 * i + b - 1)
                        sp.dma_start(raw[b][:, 0:UNIT2], w_fo_d[KT * q + 2 * i + b]).then_inc(w_in[b], 16)
            for g in range(4):
                sp.wait_ge(o_rd, 4 * (g + 1))
                sp.dma_start(out_d[4 * g:4 * g + 4].rearrange("k p t -> p k t"),
                             xacc[:, 4 * g:4 * g + 4, :]).then_inc(s_out, 16)
            sp.wait_ge(s_out, 64)

        @block.gpsimd
        def _(pool):
            pool.sem_inc(ada0_used, 4)
            for s, n in ((w_used, 2), (u_fa, 2), (u_fd, 2), (hy_free, 2), (g_free, 2), (m_free, 2), (o_free, 2),
                         (fa_free, 1), (fb_free, 1), (fd_free, 2), (s_squ, 2), (f3_free, 1),
                         (bl_tr, 2), (mt_rd, 2), (xs_ps, 2), (xs_ev, 2),
                         (l_ps, 1), (y_ps, 1), (tl_a, 1), (tl_d, 1), (y_ev, 1), (ft_rd, 1),
                         (g_st[0], 16), (g_st[1], 16)):
                pool.sem_inc(s, n)
            pool.memset(ones[:, :], 1.0).then_inc(s_cmod, 1)
            for g in range(4):
                pool.dma_start(x_raw[:, 4 * g:4 * g + 4, :], x_d[:, 4 * g:4 * g + 4, :]).then_inc(s_x, 16)
            pool.dma_start(postab[:, :, :], postab_d).then_inc(s_pos, 16)
            pool.dma_start(c_raw[:, :, :], ctx_d).then_inc(s_ctx, 16)
            for g in range(4):
                pool.wait_ge(s_xp, 4 * g + 4)
                pool.dma_start(xp_d[:, 4 * g:4 * g + 4, :], x_raw[:, 4 * g:4 * g + 4, :]).then_inc(s_xpo, 16)
            for st in range(8):
                f, cs = st // 2, st % 2
                pool.wait_ge(kf_free_a, st + 1)
                pool.wait_ge(kf_free_d, st + 1)
                for half in range(2):
                    pool.dma_start(kf_d[f, cs, :, 512 * half:512 * half + 512],
                                   T[12 + 2 * (st % 2) + half][:, :]).then_inc(kf_out[st % 2], 16)
            pool.wait_ge(s_hl, 2 * KT)
            pool.dma_start(ada1[0][:, :], w_ada_d[N_ADA0]).then_inc(ada1_in[0], 16)
            pool.dma_start(ada1[1][:, :], w_ada_d[N_ADA0 + 1]).then_inc(ada1_in[1], 16)
            with pool.Fori(1, 32) as i:
                for b in range(2):
                    pool.wait_ge(ada1_used, 2 * i + b - 1)
                    pool.dma_start(ada1[b][:, :], w_ada_d[N_ADA0 + 2 * i + b]).then_inc(ada1_in[b], 16)
            pool.wait_ge(ada1_used, 64)
            pool.wait_ge(g_ps, 32)
            pool.dma_start(s5b[:, :, :, :], s5b_d).then_inc(s_bc, 16)
            pool.dma_start(s5c[:, :, :, :], s5c_d).then_inc(s_bc, 16)
            pool.wait_ge(cv_ps, 8)
            for m in range(2):
                pool.dma_start(gT[m][:, :, :], gates_v[:, m].rearrange("g p t -> p g t")).then_inc(gt_in[m], 16)
            with pool.Fori(1, KT // 2) as i:
                for b in range(2):
                    m = 2 * i + b
                    pool.wait_ge(m_sum, m - 1)
                    pool.dma_start(gT[b][:, :, :],
                                   gates_v[:, bass.ds(m, 1)].rearrange("g o p t -> p (g o) t")
                                   ).then_inc(gt_in[b], 16)
            pool.wait_ge(m_hp, KT)
            for g in range(4):
                pool.dma_start(xacc[:, 4 * g:4 * g + 4, :], xp_d[:, 4 * g:4 * g + 4, :]).then_inc(xa_in[g], 16)

        @block.scalar
        def _(act):
            chain = Chain(act, ach)

            def split_hi(n, half, b, cols=UNIT):
                act.wait_ge(w_in[b], 16 * (half + 1))
                act.wait_ge(w_used, n + 1)
                act.activation(hi[b][:, 0:cols], raw[b][:, 0:cols], ACT.Copy).then_inc(w_hi, 1)

            act.wait_ge(s_vec, 32)
            act.activation(silu_c[:, :, 0], vecs[:, V_C:V_C + KT], ACT.Silu)
            act.activation(silu_c[:, :, 1], vecs[:, V_CC:V_CC + KT], ACT.Silu).then_inc(s_silu, 1)
            act.wait_ge(s_par, 16)
            act.activation(lt[:, 0, :], s5a[:, 2, :], ACT.Exp).then_inc(lam_s, 1)
            act.wait_ge(lam_z, 1)
            act.activation(lt[:, 3, :], lt[:, 1, :], ACT.Exp).then_inc(lam_s, 1)
            act.wait_ge(lam_z, 2)
            act.activation(lt[:, 7, :], lt[:, 5, :], ACT.Sin)
            act.activation(lt[:, 8, :], lt[:, 6, :], ACT.Sin).then_inc(lam_s, 1)
            act.wait_ge(s_h1a, 1)
            act.activation(fh[2][:, :], fh[0][:, :], ACT.Sin).then_inc(s_h1, 1)
            act.wait_ge(s_h1a, 2)
            act.activation(fh[3][:, :], fh[0][:, :], ACT.Sin).then_inc(s_h1, 1)
            act.wait_ge(s_absd, 1)
            for t in range(4):
                if t:
                    act.wait_ge(s_tap, t)
                for c in range(4):
                    act.activation(T[4 + c][:, :], decay[:, 512 * c:512 * c + 512], ACT.Exp,
                                   scale=vecs[:, V_NEGT + t:V_NEGT + t + 1]).then_inc(s_win, 1)
            for k in range(2 * KT):
                act.wait_ge(s_squ, k + 1)
                if k < KT:
                    act.wait_ge(s_xp, k + 1)
                    act.activation(sqr[k % 2][:, :], x_raw[:, k, :], ACT.Square).then_inc(s_sq, 1)
                else:
                    if k == KT:
                        act.wait_ge(s_ctx, 16)
                    act.activation(sqr[k % 2][:, 0:CTX], c_raw[:, k - KT, :], ACT.Square).then_inc(s_sq, 1)
            for st in range(8):
                act.wait_ge(kf_ps, st + 1)
                if st >= 2:
                    act.wait_ge(kf_out[st % 2], 32 * (st // 2))
                act.activation(T[12 + 2 * (st % 2)][:, :], ps[2 * (st % 2)][:, :], ACT.Copy).then_inc(kf_free_a, 1)
            for v, (a, b, w) in enumerate(((T[1], T[2], SEQ), (T[5], T[6], CTX))):
                act.wait_ge(s_var, v + 1)
                act.activation(b[:, 0:w], a[:, 0:w], ACT.Sqrt).then_inc(s_sqrt, 1)
            with act.Fori(0, KT // 2) as i:
                for b in range(2):
                    act.wait_ge(s_hv, 2 * i + b + 1)
                    act.activation(h_hi[:, 2 * i + b, :], T[8 + b][:, :], ACT.Copy).then_inc(s_hh, 1)
            act.wait_ge(s_xpo, 64)
            act.wait_ge(s_hl, KT)
            with act.Fori(0, KT // 2) as i:
                for b in range(2):
                    act.wait_ge(s_hv, KT + 2 * i + b + 1)
                    act.activation(hc_hi[:, 2 * i + b, :], T[8 + b][:, 0:CTX], ACT.Copy).then_inc(s_hh, 1)
            act.wait_ge(s_hl, 2 * KT)
            for j in range(2):
                act.wait_ge(kf_out[j], 128)
            split_hi(0, 0, 0)
            with act.Fori(0, 4) as i:
                for b in range(2):
                    split_hi(2 * i + b + 1, i + b, 1 - b)
                    act.wait_ge(u_ps, 2 * i + b + 1)
                    act.activation(u_ch[:, 2 * i + b, CTX:CTX + SEQ], ps[b][:, :], ACT.Copy).then_inc(u_fa, 1)
            with act.Fori(0, 12) as i:
                for b in range(2):
                    split_hi(8 + 2 * i + b + 1, 4 + i + b, 1 - b)
            def gate_tile(i, b):
                act.wait_ge(g_ps, 2 * i + b + 1)
                act.wait_ge(g_st[b], 16 * i + 16)
                act.activation(gst[b][:, :], ps[b][:, :], ACT.Sigmoid).then_inc(g_free, 1)
                act.wait_ge(g_free, 2 + 2 * i + b + 1)
                act.dma_start(gates_d[2 * i + b], gst[b][:, :]).then_inc(g_st[b], 16)

            with act.Fori(0, 15) as i:
                for b in range(2):
                    split_hi(32 + 2 * i + b + 1, 16 + i + b, 1 - b)
                    gate_tile(i, b)
            split_hi(63, 31, 1)
            gate_tile(15, 0)
            gate_tile(15, 1)
            for b in range(2):
                act.wait_ge(g_st[b], 16 * 17)
            act.wait_ge(ada1_used, 64)
            act.wait_ge(u_fd, 10)
            for q in range(4):
                for j in range(0, 4, 2):
                    ins = act.activation(U4[32 * j:32 * j + 32, q::4, :],
                                         u_ch[32 * q:32 * q + 32, :, j::4], ACT.Copy)
                ins.then_inc(u4a, 1)
            with act.Fori(0, NPAIR) as q:
                for d in range(2):
                    act.wait_ge(bl_tr, 2 * q + d + 3)
                    act.wait_ge(xs_ps, 2 * q + d + 1)
                    act.activation(MT[d][:, :, :].rearrange("p a b -> p (a b)"), ps[d][:, :],
                                   ACT.Copy).then_inc(mt_rd, 1)
                for d in range(2):
                    act.wait_ge(xs_ps, 2 * q + d + 3)
                    src = ps[2 + d][:, 0:2 * NCH].rearrange("p (r c) -> p c r", r=2)
                    dq = NPAIR * d + q
                    if d == 0:
                        act.activation(X[:, :, :, dq], src, ACT.Copy).then_inc(xs_ev, 1)
                    else:
                        act.activation(X[:, 0:NC_CTX, :, dq], src[:, NC_CTX - 1::-1, :], ACT.Copy)
                        act.activation(X[:, NC_CTX:NCH, :, dq], src[:, NCH - 1:NC_CTX - 1:-1, :],
                                       ACT.Copy).then_inc(xs_ev, 1)
            act.wait_ge(rec_dn, 1)

            def readout(q, par):
                act.wait_ge(l_ps, q + 1)
                act.activation(XR[par][:, :, ::-1], X[:, NC_CTX - 1:NCH - 1, :, NPAIR + q].rearrange("p c r -> p r c"),
                               ACT.Copy)
                for d in range(2):
                    ins = act.activation(BB[d][:, :, :, :],
                                         bbar[:, NPAIR * d + q, :, :].unsqueeze(2).to_broadcast([P, 2, 4, 32]),
                                         ACT.Copy)
                ins.then_inc(bb_rd, 1)
                act.wait_ge(l_ps, q + 2)
                for j in range(2):
                    for a in range(2):
                        o7 = 32 * (CH - 1 - 4 * a - j)
                        ins = act.activation(TL[32 * j:32 * j + 32, a, :, :].rearrange("p i h -> p (i h)"),
                                             ps[4][32 * j:32 * j + 32, o7:o7 + 256], ACT.Copy)
                ins.then_inc(tl_a, 1)

            with act.Fori(0, NPAIR // 2) as i:
                for par in range(2):
                    readout(2 * i + par, par)
            act.wait_ge(y_ev, NPAIR + 1)
            for q in range(4):
                for j in range(0, 4, 2):
                    ins = act.activation(y_ch[32 * q:32 * q + 32, :, j::4],
                                         U4[32 * j:32 * j + 32, q::4, CTX // 4:], ACT.Copy)
            ins.then_inc(ych, 1)
            act.wait_ge(ych, 1)
            act.wait_ge(ycd, 1)
            for g in range(2):
                act.activation(y_ch[:, 4 * g:4 * g + 4, :], y_ch[:, 4 * g:4 * g + 4, :],
                               ACT.Gelu_apprx_tanh).then_inc(gel, 1)
                act.wait_ge(gel, g + 1)
                act.activation(yg_hi[:, 4 * g:4 * g + 4, :], y_ch[:, 4 * g:4 * g + 4, :], ACT.Copy).then_inc(ygh, 1)
            for s in range(4):
                act.wait_ge(w_in[s % 2], 16 * (33 + s // 2))
                dst = (tf_hi, tg_hi)[s // 2][:, s % 2, :, :].rearrange("p a b -> p (a b)")
                act.activation(dst, raw[s % 2][:, :], ACT.Copy).then_inc(w_hi, 1)

            def transposed_u(half):
                for t in range(4):
                    act.wait_ge(ut_ps, 4 * half + t + 1)
                    act.activation(uT_hi[:, t, :], ps[t % 2][:, :], ACT.Copy).then_inc(ut_h, 1)

            def spectrum(half):
                for f in range(4):
                    for c in range(2):
                        act.wait_ge(yv, 8 * half + 2 * f + c + 1)
                        if half and f == 0 and c == 0:
                            act.wait_ge(cv_ps, 4)
                        act.activation(Y_hi[:, c, f, :], ct[2 + c][:, :], ACT.Copy).then_inc(yh, 1)

            def conv_out(half):
                for c in range(4):
                    i = 4 * half + c
                    act.wait_ge(ov, i + 1)
                    act.activation(hyo_hi[:, i, :], ct[1][:, :], ACT.Copy).then_inc(oh, 1)

            act.wait_ge(ygl, 2)
            transposed_u(0)
            spectrum(0)
            act.wait_ge(pq_ps, 4)
            transposed_u(1)
            conv_out(0)
            spectrum(1)
            conv_out(1)
            def merge(n, m, half, mm, last=False):
                split_hi(n + 1, half, 1, 1024)
                act.wait_ge(m_gl, m + 1)
                act.activation(S0[mm][:, :], ps[3 * mm + 1][:, :], ACT.Sigmoid).then_inc(m_sg, 1)
                split_hi(n + 2, half + 1, 0)
                act.wait_ge(m_sum, m + 1)
                act.activation(mg_hi[:, m, :], S1[mm][:, :], ACT.Copy).then_inc(m_hi, 1)

            split_hi(U_MRG, U_MRG // 2, 0)
            with act.Fori(0, KT // 2) as i:
                for mm in range(2):
                    merge(U_MRG + 4 * i + 2 * mm, 2 * i + mm, U_MRG // 2 + 2 * i + mm, mm)
            with act.Fori(0, KT // 2) as i:
                for b in range(2):
                    split_hi(U_OUT + 2 * i + b + 1, U_OUT // 2 + i + b, 1 - b)

            def sqrt_and_h(v):
                act.wait_ge(s_var, v + 1)
                act.activation(ct[3][:, :], ct[2][:, :], ACT.Sqrt).then_inc(s_sqrt, 1)

            sqrt_and_h(2)
            with act.Fori(0, KT // 2) as i:
                for b in range(2):
                    act.wait_ge(s_hv, 2 * KT + 2 * i + b + 1)
                    act.activation(h2_hi[:, 2 * i + b, :], ct[1 + b][:, :], ACT.Copy).then_inc(s_hh, 1)
            for q in range(4):
                n0, g0 = U_FFN + U_QUARTER * q, QTILES * q

                def pair(i, cols):
                    n, half = n0 + 2 * i, n0 // 2 + i
                    split_hi(n + 1, half, 1)
                    act.wait_ge(fa_ps, g0 + i + 1)
                    act.activation(f_s[:, :], ps[0][:, :], ACT.Silu).then_inc(fa_free, 1)
                    split_hi(n + 2, half + 1, 0, cols)
                    act.wait_ge(ft_rd, g0 + i + 2)
                    act.activation(a_hi[:, i, :], f_t[:, :], ACT.Copy).then_inc(fh_rd, 1)

                with act.Fori(0, QTILES - 1) as i:
                    pair(i, UNIT)
                pair(QTILES - 1, UNIT2)
                n1 = n0 + 2 * QTILES
                with act.Fori(0, KT // 2 - 1) as i:
                    for b in range(2):
                        split_hi(n1 + 2 * i + b + 1, n1 // 2 + i + b, 1 - b, UNIT2)
                split_hi(n1 + KT - 1, n1 // 2 + KT // 2 - 1, 1, UNIT2)
                if q < 3:
                    split_hi(n1 + KT, n1 // 2 + KT // 2, 0)
            sqrt_and_h(3)

        @block.vector
        def _(dve):
            chain = Chain(dve, dch)
            link, mark = chain.link, chain.mark
            tt, ts, stt = dve.tensor_tensor, dve.tensor_scalar, dve.scalar_tensor_tensor

            def split_lo(n, b, cols=UNIT):
                dve.wait_ge(w_hi, n + 1)
                tt(lo[b][:, 0:cols], raw[b][:, 0:cols], hi[b][:, 0:cols].bitcast(F32), SUB).then_inc(w_lo, 1)

            def reduce_angle(dst, k, src, shift):
                link(ts(k, src, 1.0 / (2 * math.pi), shift / (2 * math.pi), MUL, ADD))
                link(ts(k, k, MAGIC, MAGIC, ADD, SUB))
                link(stt(dst, k, -TWO_PI_1, src, MUL, ADD))
                link(stt(dst, k, -TWO_PI_2, dst, MUL, ADD))
                link(stt(dst, k, -TWO_PI_3, dst, MUL, ADD))
                link(ts(dst, dst, shift, PI_SAFE, ADD, ALU.min))
                return ts(dst, dst, -PI_SAFE, None, ALU.max)

            def rstd(v, sums, a, b, c, out, w):
                dve.wait_ge(s_ss, v + 1)
                link(ts(a, sums, 1.0 / D, EPS, MUL, ADD))
                dve.reciprocal(b, a).then_inc(s_var, 1)
                dve.wait_ge(s_sqrt, v + 1)
                link(tt(b, c, c, MUL))
                link(tt(b, b, a, MUL))
                link(ts(b, b, -0.5, 1.5, MUL, ADD))
                link(tt(out, b, c, MUL))

            a_re, a_im = s5a[:, 0, :], s5a[:, 1, :]
            L = [lt[:, j, :] for j in range(13)]
            dve.wait_ge(lam_s, 1)
            tt(L[1], a_re, L[0], MUL).then_inc(lam_z, 1)
            link(tt(L[2], a_im, L[0], MUL))
            link(reduce_angle(L[5], L[4], L[2], 0.0))
            reduce_angle(L[6], L[4], L[2], math.pi / 2).then_inc(lam_z, 1)
            dve.wait_ge(lam_s, 3)
            tt(lam_rr[:, 0, :], L[3], L[8], MUL)
            link(tt(lam_ii[:, 1, :], L[3], L[7], MUL))
            dve.tensor_copy(lam_rr[:, 1, :], lam_rr[:, 0, :])
            ts(lam_ii[:, 0, :], lam_ii[:, 1, :], -1.0, None, MUL)
            ts(L[9], lam_rr[:, 0, :], -1.0, None, ADD)
            tt(L[10], a_re, a_re, MUL)
            link(tt(L[11], a_im, a_im, MUL))
            link(tt(L[10], L[10], L[11], ADD))
            dve.reciprocal(L[10], L[10])
            tt(L[0], L[9], a_re, MUL)
            tt(L[1], lam_ii[:, 1, :], a_im, MUL)
            tt(L[2], lam_ii[:, 1, :], a_re, MUL)
            link(tt(L[3], L[9], a_im, MUL))
            tt(L[0], L[0], L[1], ADD)
            link(tt(L[2], L[2], L[3], SUB))
            tt(L[4], L[0], L[10], MUL)
            tt(L[5], L[0], L[10], MUL)
            link(tt(L[7], L[2], L[10], MUL))
            link(ts(L[6], L[7], -1.0, None, MUL))
            dve.memset(pw[:, 0, 0, :], 1.0)
            dve.memset(pw[:, 1, 0, :], 0.0)
            dve.tensor_copy(pw[:, 0, 1, :], lam_rr[:, 0, :])
            link(dve.tensor_copy(pw[:, 1, 1, :], lam_ii[:, 1, :]))
            tmp2 = lt[:, 9:11, :]
            for k in range(2, CH + 1):
                tt(tmp2, pw[:, ::-1, k - 1, :], lam_ii[:, :, :], MUL)
                link(tt(pw[:, :, k, :], pw[:, :, k - 1, :], lam_rr[:, :, :], MUL))
                link(tt(pw[:, :, k, :], pw[:, :, k, :], tmp2, ADD))
            for d in range(2):
                cols = slice(NPAIR * d, NPAIR * d + NPAIR)
                dve.tensor_copy(pow_c[:, :, :, cols], pw[:, :, :, cols] if d == 0 else pw[:, :, ::-1, cols])
                if d == 0:
                    src, swp = pw[:, :, CH - 1::-1, cols], pw[:, ::-1, CH - 1::-1, cols]
                else:
                    src, swp = pw[:, :, 0:CH, cols], pw[:, ::-1, 0:CH, cols]
                for ri in range(2):
                    tt(pow_b[:, ri, :, cols], src[:, ri], L[4][:, cols].unsqueeze(1).to_broadcast([P, CH, NPAIR]), MUL)
                    ins = tt(pwt[:, ri, :, :], swp[:, ri],
                             L[6 + ri][:, cols].unsqueeze(1).to_broadcast([P, CH, NPAIR]), MUL)
                link(ins)
                link(tt(pow_b[:, :, :, cols], pow_b[:, :, :, cols], pwt[:, :, :, :], ADD))
            for ri in range(2):
                dve.tensor_copy(lam_rr[:, ri, :], pw[:, 0, CH, :])
                ts(lam_ii[:, ri, :], pw[:, 1, CH, :], (-1.0, 1.0)[ri], None, MUL)

            dve.wait_ge(s_filt, 96)
            for layer in range(2):
                dve.wait_ge(s_h1p, layer + 1)
                link(ts(fh[1][:, :], ps[5][0:HID, :], fpar[:, 2 * layer:2 * layer + 1],
                        fpar[:, 2 * layer + 1:2 * layer + 2], ADD, MUL))
                k = T[4][0:HID, :]
                reduce_angle(fh[0][:, :], k, fh[1][:, :], 0.0).then_inc(s_h1a, 1)
            link(ts(T[5][:, :], decay[:, 0:512], -1.0, None, MUL))
            for c in range(4):
                if c:
                    link(ts(T[5][:, :], decay[:, 512 * c:512 * c + 512], -1.0, None, MUL))
                link(tt(decay[:, 512 * c:512 * c + 512], decay[:, 512 * c:512 * c + 512], T[5][:, :], ALU.max))
            dve.sem_inc(s_absd, 1)
            dve.wait_ge(s_pos, 16)
            for k in range(KT):
                if k % 4 == 0:
                    dve.wait_ge(s_x, 64) if k == 0 else None
                xk = x_raw[:, k, :].rearrange("p (r c) -> p r c", c=GRID)
                if k < 8:
                    pos = postab[:, k, 0:8].unsqueeze(2).to_broadcast([P, 8, GRID])
                else:
                    pos = postab[:, k - 8, 8:8 + GRID].unsqueeze(1).to_broadcast([P, 8, GRID])
                tt(xk, xk, pos, ADD).then_inc(s_xp, 1)
            for t in range(4):
                dve.wait_ge(f3_ps, t + 1)
                dve.wait_ge(s_win, 4 * t + 4)
                for c in range(4):
                    ins = tt(T[4 + c][:, :], ps[c][:, :], T[4 + c][:, :], MUL)
                if t == 0:
                    link(ins)
                    for c in range(2, 4):
                        ins = dve.memset(T[4 + c][0:1, :], 0.0)
                ins.then_inc(f3_free, 1)
                dve.wait_ge(f3_free, t + 2)
                for half in range(2):
                    tt(taps_s[:, t, 512 * half:512 * half + 512], T[4 + half][:, :], T[6 + half][:, :], ADD)
                    ins = tt(taps_d[:, t, 512 * half:512 * half + 512], T[4 + half][:, :], T[6 + half][:, :], SUB)
                ins.then_inc(s_tap, 1)
            for st in range(8):
                dve.wait_ge(kf_ps, st + 1)
                if st >= 2:
                    dve.wait_ge(kf_out[st % 2], 32 * (st // 2))
                dve.tensor_copy(T[13 + 2 * (st % 2)][:, :], ps[2 * (st % 2) + 1][:, :]).then_inc(kf_free_d, 1)
            rstd(0, ps[4][:, :], T[0][:, :], T[1][:, :], T[2][:, :], T[3][:, :], SEQ)
            rstd(1, ps[5][:, 0:CTX], T[4][:, 0:CTX], T[5][:, 0:CTX], T[6][:, 0:CTX], T[7][:, 0:CTX], CTX)
            dve.wait_ge(ada0_ps, 1)
            pa = ps[6][:, 0:2 * N_ADA0].rearrange("p (m s) -> p m s", s=2)
            tt(mod_x[:, 0:N_ADA0], pa[:, :, 0], vecs[:, V_BADA:V_BADA + N_ADA0], ADD)
            link(tt(mod_c[:, :], pa[:, :, 1], vecs[:, V_BADA:V_BADA + N_ADA0], ADD))
            for mod, mul in ((mod_x, mul_x), (mod_c, mul_c)):
                ins = stt(mul[:, :], mod[:, KT:2 * KT], 1.0, vecs[:, V_NM:V_NM + KT], ADD, MUL)
            link(ins)

            def modulated(src, rs, tmp, mul, mod, shift0, done, dst_hi, dst_lo, w):
                with dve.Fori(0, KT // 2) as i:
                    for b in range(2):
                        k = 2 * i + b
                        stt(tmp[b], src[:, k, :], mul[:, bass.ds(k, 1)], rs, MUL, MUL).then_inc(s_hm, 1)
                    for b in range(2):
                        k = 2 * i + b
                        dve.wait_ge(s_hm, done + k + 1)
                        ts(tmp[b], tmp[b], mod[:, bass.ds(shift0 + k, 1)], None, ADD).then_inc(s_hv, 1)
                    for b in range(2):
                        k = 2 * i + b
                        dve.wait_ge(s_hh, done + k + 1)
                        tt(dst_lo[:, k, :], tmp[b], dst_hi[:, k, :].bitcast(F32), SUB).then_inc(s_hl, 1)
                    dve.wait_ge(s_hl, done + 2 * i + 2)

            modulated(x_raw, T[3][:, :], [T[8 + b][:, :] for b in range(2)], mul_x, mod_x, 0, 0, h_hi, h_lo, SEQ)
            modulated(c_raw, T[7][:, 0:CTX], [T[8 + b][:, 0:CTX] for b in range(2)], mul_c, mod_c, 0, KT,
                      hc_hi, hc_lo, CTX)
            split_lo(0, 0)
            with dve.Fori(0, 4) as i:
                for b in range(2):
                    split_lo(2 * i + b + 1, 1 - b)
                    dve.wait_ge(u_ps, 2 * i + b + 1)
                    dve.tensor_copy(u_ch[:, 2 * i + b, 0:CTX], ps[2 + b][:, 0:CTX]).then_inc(u_fd, 1)
            with chain.loop(0, 4, 14) as i:
                for sub in range(6):
                    t, c = 6 * i + sub, 2 * i + sub // 3
                    split_lo(8 + t + 1, 1 - sub % 2)
                    dst = (zx1[:, :], uh[:, c, :], x0z[:, c, :])[sub % 3]
                    w = [vecs[:, bass.ds(V_CW + 24 * tap + t, 1)] for tap in range(3)]
                    src = ps[sub % 2]
                    dve.wait_ge(hy_ps, t + 1)
                    link(ts(dst, src[:, :], w[1], vecs[:, bass.ds(V_CB + t, 1)], MUL, ADD))
                    link(stt(dst[:, 1:SEQ], src[:, 0:SEQ - 1], w[0], dst[:, 1:SEQ], MUL, ADD))
                    ins = stt(dst[:, 0:SEQ - 1], src[:, 1:SEQ], w[2], dst[:, 0:SEQ - 1], MUL, ADD)
                    ins.then_inc(hy_free, 1)
                    if sub % 3 == 1:
                        dve.wait_ge(hy_free, 2 + t + 1)
                        link(tt(dst, dst, zx1[:, :], MUL))
            with dve.Fori(0, 15) as i:
                for b in range(2):
                    split_lo(32 + 2 * i + b + 1, 1 - b)
            split_lo(63, 1)
            dve.wait_ge(ada1_ps, 1)
            link(tt(mod_x[:, N_ADA0:N_ADA], ps[7][:, 0:N_ADA - N_ADA0], vecs[:, V_BADA + N_ADA0:V_BADA + N_ADA], ADD))
            link(stt(mul_f[:, :], mod_x[:, 4 * KT:5 * KT], 1.0, vecs[:, V_NF:V_NF + KT], ADD, MUL))
            dve.wait_ge(g_ps, 32)
            for b in range(2):
                dve.wait_ge(g_st[b], 16 * 17)
            dve.wait_ge(u_fa, 10)
            for q in range(4):
                for j in range(1, 4, 2):
                    ins = dve.tensor_copy(U4[32 * j:32 * j + 32, q::4, :], u_ch[32 * q:32 * q + 32, :, j::4])
            ins.then_inc(u4d, 1)
            dve.wait_ge(s_bc, 32)
            dve.wait_ge(u4a, 4)
            dve.wait_ge(u4d, 1)
            dve.memset(bbar[:, :, :, :], 0.0)
            for t in (BL[0], BL[1], CL[0][0], CL[0][1]):
                ins = dve.memset(t[:, :, :, :], 0.0)
            link(ins)
            for d in range(2):
                cols = slice(NPAIR * d, NPAIR * d + NPAIR)
                f = [pow_b[:, ri, CH - 1 if d == 0 else 0, cols].unsqueeze(2).to_broadcast([P, NPAIR, GROUP])
                     for ri in range(2)]
                m = [s5b[:, cols, ri, :] for ri in range(2)]
                tt(bt[0][:, :, :], f[0], m[0], MUL)
                tt(bt[1][:, :, :], f[1], m[1], MUL)
                tt(bt[2][:, :, :], f[0], m[1], MUL)
                link(tt(bt[3][:, :, :], f[1], m[0], MUL))
                for g in range(2):
                    r = slice(64 * g, 64 * g + 64)
                    tt(bbar[r, cols, 0, 16 * g:16 * g + 16], bt[0][r, :, :], bt[1][r, :, :], SUB)
                    ins = tt(bbar[r, cols, 1, 16 * g:16 * g + 16], bt[2][r, :, :], bt[3][r, :, :], ADD)
                link(ins)
            dve.memset(CL[0][0][:, :, :, :], 0.0)
            link(dve.memset(CL[0][1][:, :, :, :], 0.0))
            with chain.loop(0, NPAIR, 2) as q:
                for d in range(2):
                    dq = NPAIR * d + q
                    pb = pow_b[:, :, :, dq].unsqueeze(3).to_broadcast([P, 2, CH, GROUP])
                    bm = s5b[:, dq, :, :].unsqueeze(2).to_broadcast([P, 2, CH, GROUP])
                    tP, tQ = prod[2 * d], prod[2 * d + 1]
                    tt(tP[:, :, 0:CH, :], pb, bm, MUL)
                    tt(tQ[:, 0, 0:CH, :], pb[:, 0], bm[:, 1], MUL)
                    link(tt(tQ[:, 1, 0:CH, :], pb[:, 1], bm[:, 0], MUL))
                    dve.wait_ge(bl_tr, 2 * q + d + 1)
                    for ri, (src, op) in enumerate(((tP, SUB), (tQ, ADD))):
                        for g, dst in enumerate(halves(BL[d], ri, 0, CH)):
                            r = slice(64 * g, 64 * g + 64)
                            ins = tt(dst, src[r, 0, 0:CH, :], src[r, 1, 0:CH, :], op)
                    ins.then_inc(bl_rd, 1)
            dve.wait_ge(xs_ev, NDQ + 2)
            with chain.loop(1, NCH, 3) as s:
                tt(rec[0][:, :, :], X[:, s - 1, :, :], lam_rr[:, :, :], MUL)
                link(tt(rec[1][:, ::-1, :], X[:, s - 1, :, :], lam_ii[:, ::-1, :], MUL))
                link(tt(X[:, s, :, :], X[:, s, :, :], rec[0][:, :, :], ADD))
                link(tt(X[:, s, :, :], X[:, s, :, :], rec[1][:, :, :], ADD))
            dve.memset(CL[1][0][:, :, :, :], 0.0)
            dve.memset(CL[1][1][:, :, :, :], 0.0).then_inc(rec_dn, 1)
            dve.wait_ge(rec_dn, 1)

            def readout_matrix(q, par):
                for d in range(2):
                    dq = NPAIR * d + q
                    pc = pow_c[:, :, :, dq].unsqueeze(3).to_broadcast([P, 2, CH + 1, GROUP])
                    cm = s5c[:, dq, :, :].unsqueeze(2).to_broadcast([P, 2, CH + 1, GROUP])
                    tP, tQ = prod[2 * d], prod[2 * d + 1]
                    tt(tP[:, :, :, :], pc, cm, MUL)
                    tt(tQ[:, 0, :, :], pc[:, 0], cm[:, 1], MUL)
                    link(tt(tQ[:, 1, :, :], pc[:, 1], cm[:, 0], MUL))
                    for g in range(2):
                        r = slice(64 * g, 64 * g + 64)
                        tt(halves(CL[par][d], 0, 0, CH + 1)[g], tP[r, 0, :, :], tP[r, 1, :, :], SUB)
                        ins = stt(halves(CL[par][d], 1, 0, CH + 1)[g], tQ[r, 0, :, :], -1.0, tQ[r, 1, :, :], MUL, SUB)
                    ins.then_inc(cl_rd, 1)

            def readout(q, par, last):
                if not last:
                    dve.wait_ge(y_ps, q + 1)
                    readout_matrix(q + 1, 1 - par)
                dve.wait_ge(l_ps, q + 2)
                for j in range(2, 4):
                    for a in range(2):
                        o7 = 32 * (CH - 1 - 4 * a - j)
                        ins = dve.tensor_copy(TL[32 * j:32 * j + 32, a, :, :].rearrange("p i h -> p (i h)"),
                                              ps[4][32 * j:32 * j + 32, o7:o7 + 256])
                ins.then_inc(tl_d, 1)
                dve.wait_ge(y_ps, q + 2)
                yq = U4[:, q, CTX // 4:].rearrange("p (c a) -> p c a", a=2)
                src = ps[5][:, 0:2 * NC_LAT].rearrange("p (a c) -> p c a", a=2)
                stt(yq, yq, vecs[:, bass.ds(V_D4 + q, 1)], src, MUL, ADD).then_inc(y_ev, 1)

            readout_matrix(0, 0)
            with chain.loop(0, NPAIR // 2 - 1, 4) as i:
                for par in range(2):
                    readout(2 * i + par, par, False)
            readout(NPAIR - 2, 0, False)
            readout(NPAIR - 1, 1, True)
            dve.wait_ge(y_ev, NPAIR + 1)
            for q in range(4):
                for j in range(1, 4, 2):
                    ins = dve.tensor_copy(y_ch[32 * q:32 * q + 32, :, j::4], U4[32 * j:32 * j + 32, q::4, CTX // 4:])
            ins.then_inc(ycd, 1)
            for g in range(2):
                dve.wait_ge(ygh, g + 1)
                tt(yg_lo[:, 4 * g:4 * g + 4, :], y_ch[:, 4 * g:4 * g + 4, :],
                   yg_hi[:, 4 * g:4 * g + 4, :].bitcast(F32), SUB).then_inc(ygl, 1)
            for s in range(4):
                dve.wait_ge(w_hi, U_TAB + s + 1)
                h, l = ((tf_hi, tf_lo), (tg_hi, tg_lo))[s // 2]
                tt(l[:, s % 2, :, :].rearrange("p a b -> p (a b)"), raw[s % 2][:, :],
                   h[:, s % 2, :, :].rearrange("p a b -> p (a b)").bitcast(F32), SUB).then_inc(w_lo, 1)

            def transposed_u(half):
                for t in range(4):
                    dve.wait_ge(ut_h, 4 * half + t + 1)
                    tt(uT_lo[:, t, :], ps[t % 2][:, :], uT_hi[:, t, :].bitcast(F32), SUB).then_inc(ut_l, 1)

            def spectrum(half):
                for f in range(4):
                    n = 4 * half + f
                    dve.wait_ge(pq_ps, n + 1)
                    dve.wait_ge(k_in[f % 2], 16 * (n // 2 + 1))
                    if half and f == 0:
                        dve.wait_ge(ol, 4)
                    A, B = (kfr[f % 2][:, s, :] for s in range(2))
                    pp, pq = (ps[2 + 2 * (f % 2) + s][:, :] for s in range(2))
                    tt(ct[0][:, :], A, pp, MUL)
                    link(tt(ct[1][:, :], B, pq, MUL))
                    link(tt(ct[2][:, :], ct[0][:, :], ct[1][:, :], SUB))
                    dve.sem_inc(yv, 1)
                    tt(ct[0][:, :], A, pq, MUL)
                    ins = tt(ct[1][:, :], B, pp, MUL)
                    ins.then_inc(pq_ev, 1)
                    dve.wait_ge(pq_ev, n + 1)
                    tt(ct[3][:, :], ct[0][:, :], ct[1][:, :], ADD).then_inc(yv, 1)
                    for c in range(2):
                        dve.wait_ge(yh, 8 * half + 2 * f + c + 1)
                        tt(Y_lo[:, c, f, :], ct[2 + c][:, :], Y_hi[:, c, f, :].bitcast(F32), SUB).then_inc(yl, 1)

            def conv_out(half):
                for c in range(4):
                    i = 4 * half + c
                    dve.wait_ge(cv_ps, i + 1)
                    stt(ct[0][:, :], uh[:, i, :], vecs[:, V_HB + i:V_HB + i + 1], ps[6 + i % 2][:, :],
                        MUL, ADD).then_inc(cv_free, 1)
                    dve.wait_ge(cv_free, i + 1)
                    tt(ct[1][:, :], ct[0][:, :], x0z[:, i, :], MUL).then_inc(ov, 1)
                    dve.wait_ge(oh, i + 1)
                    tt(hyo_lo[:, i, :], ct[1][:, :], hyo_hi[:, i, :].bitcast(F32), SUB).then_inc(ol, 1)

            transposed_u(0)
            spectrum(0)
            transposed_u(1)
            conv_out(0)
            spectrum(1)
            conv_out(1)
            split_lo(U_MRG, 0)
            with chain.loop(0, KT // 2, 4) as i:
                for mm in range(2):
                    m, n = 2 * i + mm, U_MRG + 4 * i + 2 * mm
                    split_lo(n + 1, 1, 1024)
                    dve.wait_ge(m_sg, m + 1)
                    link(tt(S1[mm][:, :], ps[3 * mm][:, :], S0[mm][:, :], MUL))
                    dve.wait_ge(gt_in[mm], 16 * (i + 1))
                    tt(S1[mm][:, :], S1[mm][:, :], gT[mm][:, 0, :], MUL)
                    split_lo(n + 2, 0)
                    dve.wait_ge(m_hp, m + 1)
                    tt(S0[mm][:, :], ps[3 * mm + 2][:, :], gT[mm][:, 1, :], MUL).then_inc(m_free, 1)
                    dve.wait_ge(m_free, 2 + m + 1)
                    link(tt(S1[mm][:, :], S1[mm][:, :], S0[mm][:, :], ADD))
                    dve.sem_inc(m_sum, 1)
                    dve.wait_ge(m_hi, m + 1)
                    tt(mg_lo[:, m, :], S1[mm][:, :], mg_hi[:, m, :].bitcast(F32), SUB).then_inc(m_lo, 1)
            for g in range(4):
                dve.wait_ge(xa_in[g], 16)
            link(dve.memset(ct[0][:, :], 0.0))

            def add_square(m):
                link(tt(ct[1][:, :], xacc[:, m, :], xacc[:, m, :], MUL))
                link(tt(ct[0][:, :], ct[0][:, :], ct[1][:, :], ADD))

            with chain.loop(0, KT // 2, 6) as i:
                for b in range(2):
                    m = 2 * i + b
                    split_lo(U_OUT + m + 1, 1 - b)
                    dve.wait_ge(o_ps, m + 1)
                    ins = stt(xacc[:, m, :], ps[6 + b][:, :], mod_x[:, bass.ds(2 * KT + m, 1)], xacc[:, m, :], MUL, ADD)
                    link(ins)
                    dve.sem_inc(o_free, 1)
                    add_square(m)
            dve.sem_inc(s_acc, 1)
            rstd(2, ps[4][:, :], ct[1][:, :], ct[2][:, :], ct[3][:, :], ct[0][:, :], SEQ)
            modulated(xacc, ct[0][:, :], [ct[1 + b][:, :] for b in range(2)], mul_f, mod_x, 3 * KT, 2 * KT,
                      h2_hi, h2_lo, SEQ)
            for q in range(4):
                n0, g0 = U_FFN + U_QUARTER * q, QTILES * q

                def pair(i, cols):
                    n = n0 + 2 * i
                    split_lo(n + 1, 1)
                    split_lo(n + 2, 0, cols)
                    dve.wait_ge(fb_ps, g0 + i + 1)
                    dve.wait_ge(fa_free, 1 + g0 + i + 1)
                    tt(f_t[:, :], f_s[:, :], ps[1][:, :], MUL).then_inc(ft_rd, 1)
                    dve.wait_ge(fh_rd, g0 + i + 1)
                    tt(a_lo[:, i, :], f_t[:, :], a_hi[:, i, :].bitcast(F32), SUB).then_inc(fl_rd, 1)
                    dve.wait_ge(fl_rd, g0 + i + 1)

                with dve.Fori(0, QTILES - 1) as i:
                    pair(i, UNIT)
                pair(QTILES - 1, UNIT2)
                n1 = n0 + 2 * QTILES
                if q == 3:
                    link(dve.memset(ct[0][:, :], 0.0))

                def down(m, b, cols):
                    if cols:
                        split_lo(n1 + m + 1, 1 - b, cols)
                    dve.wait_ge(fd_ps, KT * q + m + 1)
                    ins = stt(xacc[:, m, :], ps[2 + b][:, :], mod_x[:, bass.ds(5 * KT + m, 1)], xacc[:, m, :], MUL, ADD)
                    link(ins)
                    dve.sem_inc(fd_free, 1)
                    if q == 3:
                        add_square(m)

                with chain.loop(0, KT // 2 - 1, 6 if q == 3 else 2) as i:
                    for b in range(2):
                        down(2 * i + b, b, UNIT2)
                down(KT - 2, 0, UNIT2)
                down(KT - 1, 1, UNIT if q < 3 else 0)
            dve.sem_inc(s_acc, 1)
            rstd(3, ps[4][:, :], ct[1][:, :], ct[2][:, :], ct[3][:, :], ct[0][:, :], SEQ)
            for m in range(KT):
                stt(xacc[:, m, :], xacc[:, m, :], vecs[:, V_NO + m:V_NO + m + 1], ct[0][:, :], MUL, MUL).then_inc(o_rd, 1)

        @block.tensor
        def _(pe):
            mm = pe.matmul

            def product(out, wh, wl, xh, xl, nk, first=True, last=True):
                for k in range(nk):
                    mm(out, wh(k), xh(k), start=first and k == 0, stop=False)
                    mm(out, wh(k), xl(k), start=False, stop=False)
                    ins = mm(out, wl(k), xh(k), start=False, stop=last and k == nk - 1)
                return ins

            def w_tile(t, k0=0):
                return lambda k: t[:, (k0 + k) * P:(k0 + k + 1) * P]

            def x_tile(t):
                return lambda k: t[:, k, :]

            pe.wait_ge(s_filt, 96)
            mm(ps[5][0:HID, :], f1w[:, :], feats[:, :], start=True, stop=True).then_inc(s_h1p, 1)
            pe.wait_ge(s_h1, 1)
            mm(ps[5][0:HID, :], f2w[:, :], fh[2][:, :], start=True, stop=True).then_inc(s_h1p, 1)
            pe.wait_ge(s_h1, 2)
            for t in range(4):
                pe.wait_ge(f3_free, t + 1)
                for c in range(4):
                    ins = mm(ps[c][:, :], fh[3][:, P * t:P * t + P], f3w[0:HID, 512 * c:512 * c + 512],
                             start=True, stop=True)
                ins.then_inc(f3_ps, 1)
            pe.wait_ge(s_cmod, 1)
            for k in range(2 * KT):
                pe.wait_ge(s_sq, k + 1)
                dst, w = (ps[4], SEQ) if k < KT else (ps[5], CTX)
                ins = mm(dst[:, 0:w], ones[:, :], sqr[k % 2][:, 0:w], start=k % KT == 0, stop=k % KT == KT - 1)
                ins.then_inc(s_squ, 1)
            pe.wait_ge(s_squ, 2 + 2 * KT)
            pe.sem_inc(s_ss, 2)
            pe.wait_ge(s_silu, 1)
            for st in range(8):
                for j in range(4):
                    n = 4 * st + j
                    pe.wait_ge(ada0_in[j], 16 * (st + 1))
                    for k in range(KT):
                        ins = mm(ps[6][:, 2 * n:2 * n + 2], ada0[j][:, k * P:k * P + P], silu_c[:, k, :],
                                 start=k == 0, stop=k == KT - 1)
                    ins.then_inc(ada0_used, 1)
                f, cs = st // 2, st % 2
                if st == 0:
                    pe.wait_ge(s_tabf, 32)
                    pe.wait_ge(s_tap, 4)
                if st >= 2:
                    pe.wait_ge(kf_free_a, st - 1)
                    pe.wait_ge(kf_free_d, st - 1)
                for half in range(2):
                    for t in range(4):
                        ins = mm(ps[2 * (st % 2) + half][:, :], tab_f[:, cs, t, P * f:P * f + P],
                                 (taps_s, taps_d)[cs][:, t, 512 * half:512 * half + 512], start=t == 0, stop=t == 3)
                ins.then_inc(kf_ps, 1)
            pe.wait_ge(ada0_used, 4 + N_ADA0)
            pe.sem_inc(ada0_ps, 1)

            def ada_unit(n, b, half):
                pe.wait_ge(ada1_in[b], 16 * (half + 1))
                for k in range(KT):
                    ins = mm(ps[7][:, bass.ds(n, 1)], ada1[b][:, k * P:k * P + P], silu_c[:, k, 0:1],
                             start=k == 0, stop=k == KT - 1)
                ins.then_inc(ada1_used, 1)

            pe.wait_ge(s_hl, 2 * KT)
            pe.wait_ge(kf_free_a, 8)
            pe.wait_ge(kf_free_d, 8)
            with pe.Fori(0, 4) as i:
                for b in range(2):
                    n = 2 * i + b
                    pe.wait_ge(w_lo, n + 1)
                    pe.wait_ge(u_fa, n + 1)
                    pe.wait_ge(u_fd, n + 1)
                    for k in range(KT):
                        wh, wl = w_tile(hi[b])(k), w_tile(lo[b])(k)
                        for j, (w, xt, ct_) in enumerate(((wh, h_hi, hc_hi), (wh, h_lo, hc_lo), (wl, h_hi, hc_hi))):
                            s0, s1 = k == 0 and j == 0, k == KT - 1 and j == 2
                            mm(ps[b][:, :], w, xt[:, k, :], start=s0, stop=s1)
                            ins = mm(ps[2 + b][:, 0:CTX], w, ct_[:, k, :], start=s0, stop=s1)
                    ins.then_inc(w_used, 1)
                    pe.wait_ge(w_used, 2 + n + 1)
                    pe.sem_inc(u_ps, 1)
                    ada_unit(n, b, i)
            pe.wait_ge(u_fa, 10)
            with pe.Fori(0, 12) as i:
                for b in range(2):
                    t = 2 * i + b
                    pe.wait_ge(w_lo, 8 + t + 1)
                    pe.wait_ge(hy_free, t + 1)
                    ins = product(ps[b][:, :], w_tile(hi[b]), w_tile(lo[b]), x_tile(h_hi), x_tile(h_lo), KT)
                    ins.then_inc(w_used, 1)
                    ada_unit(8 + t, b, 4 + i)
                    pe.wait_ge(w_used, 2 + 8 + t + 1)
                    pe.sem_inc(hy_ps, 1)
            pe.wait_ge(hy_free, 26)
            with pe.Fori(0, 16) as i:
                for b in range(2):
                    t = 2 * i + b
                    pe.wait_ge(w_lo, 32 + t + 1)
                    pe.wait_ge(g_free, t + 1)
                    ins = product(ps[b][:, :], w_tile(hi[b]), w_tile(lo[b]), x_tile(h_hi), x_tile(h_lo), KT)
                    ins.then_inc(w_used, 1)
                    ada_unit(32 + t, b, 16 + i)
                    pe.wait_ge(w_used, 2 + 32 + t + 1)
                    pe.sem_inc(g_ps, 1)
            pe.wait_ge(ada1_used, 64)
            pe.sem_inc(ada1_ps, 1)
            pe.wait_ge(g_free, 34)
            pe.wait_ge(u4a, 4)
            pe.wait_ge(u4d, 1)
            with pe.Fori(0, NPAIR) as q:
                for d in range(2):
                    pe.wait_ge(bl_rd, 2 * q + d + 1)
                    pe.wait_ge(mt_rd, 2 * q + d + 1)
                    for ri in range(2):
                        for a in range(2):
                            ins = pe.transpose(ps[d][:, (2 * ri + a) * P:(2 * ri + a + 1) * P],
                                               BL[d][:, ri, 4 * a:4 * a + 4, :].rearrange("p j h -> p (j h)"),
                                               ident[:, :])
                    ins.then_inc(bl_tr, 1)
                for d in range(2):
                    pe.wait_ge(mt_rd, 2 * q + d + 3)
                    pe.wait_ge(xs_ev, 2 * q + d + 1)
                    for ri in range(2):
                        for a in range(2):
                            ins = mm(ps[2 + d][:, NCH * ri:NCH * ri + NCH], MT[d][:, 2 * ri + a, :],
                                     U4[:, q, a::2], start=a == 0, stop=a == 1)
                    ins.then_inc(xs_ps, 1)
            pe.wait_ge(rec_dn, 1)

            def readout(q, par):
                pe.wait_ge(cl_rd, 2 * q + 2)
                pe.wait_ge(bb_rd, q + 1)
                pe.wait_ge(tl_a, q + 1)
                pe.wait_ge(tl_d, q + 1)
                C = CL[par]
                jobs = [(1, 0, 256, 1), (0, 224, 256, 0), (0, 256, 480, 1)]
                for n, (d, c0, c1, i0) in enumerate(jobs):
                    for ri in range(2):
                        rhs = C[d][:, ri, i0:i0 + (c1 - c0) // 32, :].rearrange("p m h -> p (m h)")
                        ins = mm(ps[4][:, c0:c1], BB[d][:, ri, :, :].rearrange("p a b -> p (a b)"), rhs,
                                 start=n == 0 and ri == 0, stop=ri == 1 and n == 2, skip_group_check=True)
                ins.then_inc(l_ps, 1)
                pe.wait_ge(tl_a, q + 2)
                pe.wait_ge(tl_d, q + 2)
                pe.wait_ge(y_ev, q + 1)
                for a in range(2):
                    out = ps[5][:, NC_LAT * a:NC_LAT * a + NC_LAT]
                    for ri in range(2):
                        mm(out, C[0][:, ri, 4 * a + 1:4 * a + 5, :].rearrange("p m h -> p (m h)"),
                           X[:, NC_CTX - 1:NCH - 1, ri, q], start=ri == 0, stop=False)
                        mm(out, C[1][:, ri, 4 * a:4 * a + 4, :].rearrange("p m h -> p (m h)"),
                           XR[par][:, ri, :], start=False, stop=False)
                    for ai in range(2):
                        ins = mm(out, TL[:, ai, 4 * a:4 * a + 4, :].rearrange("p m h -> p (m h)"),
                                 U4[:, q, CTX // 4 + ai::2], start=False, stop=ai == 1)
                ins.then_inc(y_ps, 1)

            with pe.Fori(0, NPAIR // 2) as i:
                for par in range(2):
                    readout(2 * i + par, par)
            def transpose_u(half):
                for t in range(4):
                    n = 4 * half + t
                    if n >= 2:
                        pe.wait_ge(ut_l, n - 1)
                    for c in range(4):
                        ins = pe.transpose(ps[t % 2][:, P * c:P * c + P], uh[:, 4 * half + c, P * t:P * t + P], ident[:, :])
                    ins.then_inc(ut_ps, 1)

            def spectrum(half):
                for f in range(4):
                    n = 4 * half + f
                    if n >= 2:
                        pe.wait_ge(pq_ev, n - 1)
                    for s in range(2):
                        ins = product(ps[2 + 2 * (f % 2) + s][:, :], lambda t: tf_hi[:, s, t, P * f:P * f + P],
                                      lambda t: tf_lo[:, s, t, P * f:P * f + P], x_tile(uT_hi), x_tile(uT_lo), 4)
                    ins.then_inc(pq_ps, 1)

            def inverse(half):
                for c in range(4):
                    i = 4 * half + c
                    if i >= 2:
                        pe.wait_ge(cv_free, i - 1)
                    pe.wait_ge(yl, 8 * half + 8)
                    for s in range(2):
                        ins = product(ps[6 + i % 2][:, :], lambda f: Y_hi[:, s, f, P * c:P * c + P],
                                      lambda f: Y_lo[:, s, f, P * c:P * c + P], lambda f: tg_hi[:, s, f, :],
                                      lambda f: tg_lo[:, s, f, :], 4, first=s == 0, last=s == 1)
                    ins.then_inc(cv_ps, 1)

            transpose_u(0)
            pe.wait_ge(w_lo, U_TAB + 2)
            pe.wait_ge(ut_l, 4)
            spectrum(0)
            transpose_u(1)
            pe.wait_ge(w_lo, U_TAB + 4)
            inverse(0)
            pe.wait_ge(ut_l, 8)
            spectrum(1)
            inverse(1)
            pe.wait_ge(cv_ps, 8)
            pe.sem_inc(w_used, 4)
            pe.wait_ge(ygl, 2)
            pe.wait_ge(ol, 8)
            with pe.Fori(0, KT // 2) as i:
                for b in range(2):
                    m, n = 2 * i + b, U_MRG + 4 * i + 2 * b
                    pe.wait_ge(w_lo, n + 1)
                    pe.wait_ge(m_free, m + 1)
                    product(ps[3 * b][:, :], w_tile(hi[0]), w_tile(lo[0]), x_tile(yg_hi), x_tile(yg_lo), ST)
                    ins = product(ps[3 * b + 1][:, :], w_tile(hi[0], ST), w_tile(lo[0], ST), x_tile(yg_hi), x_tile(yg_lo), ST)
                    ins.then_inc(w_used, 1)
                    pe.wait_ge(w_lo, n + 2)
                    pe.wait_ge(w_used, 2 + n + 1)
                    pe.sem_inc(m_gl, 1)
                    ins = product(ps[3 * b + 2][:, :], w_tile(hi[1]), w_tile(lo[1]), x_tile(hyo_hi), x_tile(hyo_lo), ST)
                    ins.then_inc(w_used, 1)
                    pe.wait_ge(w_used, 2 + n + 2)
                    pe.sem_inc(m_hp, 1)
            pe.wait_ge(m_lo, KT)
            with pe.Fori(0, KT // 2) as i:
                for b in range(2):
                    m = 2 * i + b
                    pe.wait_ge(w_lo, U_OUT + m + 1)
                    pe.wait_ge(o_free, m + 1)
                    ins = product(ps[6 + b][:, :], w_tile(hi[b]), w_tile(lo[b]), x_tile(mg_hi), x_tile(mg_lo), KT)
                    ins.then_inc(w_used, 1)
                    pe.wait_ge(w_used, 2 + U_OUT + m + 1)
                    pe.sem_inc(o_ps, 1)
            pe.wait_ge(s_acc, 1)
            mm(ps[4][:, :], ones[:, :], ct[0][:, :], start=True, stop=True).then_inc(s_ss, 1)
            pe.wait_ge(s_hl, 3 * KT)
            for q in range(4):
                n0, g0 = U_FFN + U_QUARTER * q, QTILES * q
                with pe.Fori(0, QTILES) as i:
                    for b, (free, done) in enumerate(((fa_free, fa_ps), (ft_rd, fb_ps))):
                        n = n0 + 2 * i + b
                        pe.wait_ge(w_lo, n + 1)
                        pe.wait_ge(free, g0 + i + 1)
                        ins = product(ps[b][:, :], w_tile(hi[b]), w_tile(lo[b]), x_tile(h2_hi), x_tile(h2_lo), KT)
                        ins.then_inc(w_used, 1)
                        pe.wait_ge(w_used, 2 + n + 1)
                        pe.sem_inc(done, 1)
                n1 = n0 + 2 * QTILES
                pe.wait_ge(fl_rd, g0 + QTILES)
                with pe.Fori(0, KT // 2) as i:
                    for b in range(2):
                        m = 2 * i + b
                        pe.wait_ge(w_lo, n1 + m + 1)
                        pe.wait_ge(fd_free, KT * q + m + 1)
                        ins = product(ps[2 + b][:, :], w_tile(hi[b]), w_tile(lo[b]), x_tile(a_hi), x_tile(a_lo), QTILES)
                        ins.then_inc(w_used, 1)
                        pe.wait_ge(w_used, 2 + n1 + m + 1)
                        pe.sem_inc(fd_ps, 1)
            pe.wait_ge(s_acc, 2)
            mm(ps[4][:, :], ones[:, :], ct[0][:, :], start=True, stop=True).then_inc(s_ss, 1)


def tables():
    f32 = np.float32
    quarter = D // 4
    omega = (f32(10000.0) ** (-np.arange(quarter, dtype=f32) / f32(quarter))).astype(f32)
    rows = (np.arange(SEQ // GRID, dtype=f32)[None, :] * omega[:, None]).astype(f32)
    cols = (np.arange(GRID, dtype=f32)[None, :] * omega[:, None]).astype(f32)
    pos_r = np.concatenate([np.sin(rows), np.cos(rows)]).reshape(8, P, SEQ // GRID)
    pos_c = np.concatenate([np.sin(cols), np.cos(cols)]).reshape(8, P, GRID)
    postab = np.ascontiguousarray(np.concatenate([pos_r, pos_c], axis=2).transpose(1, 0, 2)).astype(f32)
    pos = np.arange(SEQ, dtype=f32)
    t = (pos / f32(SEQ - 1)).astype(f32)
    w = (f32(2.0 * math.pi) * pos / f32(SEQ)).astype(f32)
    bands = np.linspace(1e-4, BANDS - 1, BANDS).astype(f32)
    ang = (w[:, None] * bands).astype(f32)
    feats = np.concatenate([t[:, None], np.cos(ang), -np.sin(ang)], axis=1).astype(f32)
    negt = np.ascontiguousarray((-t).reshape(4, P).T)
    theta = np.pi * (2 * np.arange(SEQ) + 1)[:, None] * np.arange(SEQ)[None, :] / (2 * SEQ)
    cos, sin = np.cos(theta), np.sin(theta)

    def tiled(m):
        return m.reshape(4, P, SEQ).transpose(1, 0, 2).reshape(P, 4 * SEQ)

    tabs = np.stack([tiled(cos.T), tiled(sin.T), tiled(cos / SEQ), tiled(sin / SEQ)]).astype(f32)
    return postab, np.ascontiguousarray(feats.T), negt, tabs, np.eye(P, dtype=f32)


def kernel(**inputs):
    import concourse.bacc as bacc
    from concourse.bass_utils import run_bass_kernel_spmd

    a = {k: np.asarray(v) for k, v in inputs.items()}
    postab, feats, negt, tabs, ident = tables()
    cont = np.ascontiguousarray

    def units(w):
        r, c = w.shape
        return cont(w.reshape(r // P, P, c // P, P).transpose(2, 1, 0, 3).reshape(c // P, P, r))

    def by_channel(v):
        return v.reshape(-1, P).T

    w_in = units(a["w_in"][0])
    hy = [8 * part + 8 + i for i in range(ST) for part in (1, 2, 0)]
    w_in = cont(w_in[list(range(8)) + hy + list(range(32, 64))])
    conv = a["hy_conv_w"][0].reshape(3, 24, P)[:, [h - 8 for h in hy]]
    conv_b = a["hy_conv_b"][0].reshape(24, P)[[h - 8 for h in hy]]
    glu = units(a["w_glu"][0])
    w_glu = cont(np.concatenate([glu[:KT], glu[KT:]], axis=2))
    fi = units(a["w_ffn_in"][0])
    w_fi = cont(np.stack([fi[:DFF // P], fi[DFF // P:]], axis=1).reshape(2 * DFF // P, P, UNIT))
    fo = a["w_ffn_out"][0].reshape(4, QTILES, P, KT, P)
    w_fo = cont(fo.transpose(0, 3, 2, 1, 4).reshape(4 * KT, P, UNIT2))
    d4 = np.tile(a["s5_d"][0].reshape(NPAIR, 32).T, (4, 1))
    vecs = cont(np.concatenate([
        by_channel(a["norm_mix"][0]), by_channel(a["norm_ffn"][0]), by_channel(a["norm_f"]),
        by_channel(a["c"][0]), by_channel(a["c_ctx"]), by_channel(a["b_ada"][0]),
        conv.reshape(72, P).T, conv_b.T, by_channel(a["hy_bias"][0]), d4, negt], axis=1))

    def poles(v):
        return v.reshape(2, NPAIR, 2, STATE).transpose(2, 3, 0, 1).reshape(P, NDQ)

    log_dt = np.broadcast_to(a["s5_log_dt"][0][:, :, None], (2, 2 * NPAIR, STATE))
    s5a = cont(np.stack([poles(a["s5_a_re"][0]), poles(a["s5_a_im"][0]), poles(log_dt)], axis=1))

    def modes(re, im, perm):
        v = np.stack([re, im]).transpose(perm)
        v = v.reshape(2, 2, NPAIR, 2, STATE, GROUP).transpose(3, 4, 1, 2, 0, 5)
        return cont(v.reshape(P, NDQ, 2, GROUP))

    data = {
        "vecs": vecs, "w_ada": units(a["w_ada"][0]), "w_in": w_in, "w_glu": w_glu,
        "w_hy": units(a["w_hy_out"][0]), "w_out": units(a["w_out"][0]), "w_fi": w_fi, "w_fo": w_fo,
        "x": cont(a["x"][0].T.reshape(KT, P, SEQ).transpose(1, 0, 2)),
        "ctx": cont(a["ctx"][0].T.reshape(KT, P, CTX).transpose(1, 0, 2)),
        "s5a": s5a, "s5b": modes(a["s5_b_re"][0], a["s5_b_im"][0], (0, 1, 2, 3, 4)),
        "s5c": modes(a["s5_c_re"][0], a["s5_c_im"][0], (0, 1, 2, 4, 3)),
        "f1w": cont(a["hy_f1_w"][0]), "f2w": cont(a["hy_f2_w"][0]), "f3w": cont(a["hy_f3_w"][0]),
        "fpar": cont(np.stack([a["hy_f1_b"][0], a["hy_f1_freq"][0], a["hy_f2_b"][0], a["hy_f2_freq"][0]], axis=1)),
        "decay": cont(a["hy_decay"][0].reshape(1, 2 * HYW)),
        "feats": feats, "postab": postab, "tabs": tabs, "ident": ident,
    }
    nc = bacc.Bacc("TRN2", target_bir_lowering=False, num_devices=1)
    arrays, args = {}, []
    for name, v in data.items():
        arrays[f"in_{name}"] = v
        args.append(nc.dram_tensor(f"in_{name}", v.shape, F32, kind="ExternalInput").ap())
    args.append(nc.dram_tensor("out", (KT, P, SEQ), F32, kind="ExternalOutput").ap())
    args.append(nc.dram_tensor("xp", (P, KT, SEQ), F32, kind="Internal").ap())
    args.append(nc.dram_tensor("gates", (2 * KT, P, SEQ), F32, kind="Internal").ap())
    args.append(nc.dram_tensor("kf", (4, 2, P, HYW), F32, kind="Internal").ap())
    block_kernel(nc, *args)
    got = run_bass_kernel_spmd(nc, [arrays], core_ids=[0]).results[0]["out"]
    return got.reshape(D, SEQ).T.reshape(1, SEQ, D)
```

```python
import math
from contextlib import contextmanager

import numpy as np

import concourse.bass as bass
from concourse import mybir

P = 128
D = 2048
SEQ = 512
CTX = 256
GRID = 64
S5W = 1024
HYW = 1024
STATE = 64
GROUP = 16
HID = 64
BANDS = 16
POSD = 1 + 2 * BANDS
DFF = 5632
EPS = 1e-6

KT = D // P
ST = S5W // P
NPAIR = S5W // 32
NDQ = 2 * NPAIR
CH = 8
NC_CTX = CTX // CH
NC_LAT = SEQ // CH
NCH = NC_CTX + NC_LAT
UNIT = KT * P
QTILES = DFF // P // 4
UNIT2 = QTILES * P
N_ADA = 96
N_ADA0 = 32

U_IN = 0
U_TAB = 64
U_MRG = 68
U_OUT = 100
U_FFN = 116
U_QUARTER = 2 * QTILES + KT

V_NM, V_NF, V_NO, V_C, V_CC, V_BADA = 0, 16, 32, 48, 64, 80
V_CW, V_CB, V_HB, V_D4, V_NEGT, NVEC = 176, 248, 272, 280, 312, 316

F32 = mybir.dt.float32
F32R = mybir.dt.float32r
ALU = mybir.AluOpType
ACT = mybir.ActivationFunctionType
MUL, ADD, SUB = ALU.mult, ALU.add, ALU.subtract

MAGIC = 12582912.0
TWO_PI_1 = 6.28125
TWO_PI_2 = float(np.float32(np.round((2 * math.pi - TWO_PI_1) * 2.0 ** 20) / 2.0 ** 20))
TWO_PI_3 = float(np.float32(2 * math.pi - TWO_PI_1 - TWO_PI_2))
PI_SAFE = 3.1415925


class Chain:

    def __init__(self, eng, sem):
        self.eng, self.sem, self.base, self.k = eng, sem, 0, 0

    def mark(self, ins):
        ins.then_inc(self.sem, 1)
        self.k += 1

    def wait(self):
        self.eng.wait_ge(self.sem, self.base + self.k)

    def link(self, ins):
        self.mark(ins)
        self.wait()

    @contextmanager
    def loop(self, lo, hi, marks):
        start = self.base + self.k
        with self.eng.Fori(lo, hi) as i:
            self.base, self.k = start + (i - lo) * marks, 0
            yield i
            assert self.k == marks, (self.k, marks)
        self.base, self.k = start + (hi - lo) * marks, 0


def block_kernel(nc, vecs_d, w_ada_d, w_ar_d, w_in_d, w_glu_d, w_hy_d, w_out_d, w_fi_d, w_fo_d, x_d, ctx_d,
                 s5a_d, s5b_d, s5c_d, f1w_d, f2w_d, f3w_d, fpar_d, decay_d, feats_d, postab_d,
                 tabs_d, ident_d, out_d, xp_d, gates_d, kf_d):
    kb = 1024
    base = (nc.sbuf_base + 63) // 64 * 64

    def at(name, off_kb, shape, dt=F32):
        return nc.alloc_sbuf_tensor_at(name, shape, dt, offset=base + int(off_kb * kb))

    raw = [at("w_raw0", 0, [P, UNIT]), at("w_raw1", 8, [P, UNIT])]
    hi = [at("w_hi0", 16, [P, UNIT], F32R), at("w_hi1", 32, [P, UNIT], F32R)]
    lo = [at("w_lo0", 24, [P, UNIT], F32R), at("w_lo1", 40, [P, UNIT], F32R)]
    small = 48
    vecs = at("vecs", small, [P, NVEC])
    o = small + 320 * 4 / kb
    silu_c = at("silu_c", o, [P, KT, 2]); o += 32 * 4 / kb
    mod_x = at("mod_x", o, [P, N_ADA]); o += N_ADA * 4 / kb
    mod_c = at("mod_c", o, [P, N_ADA0]); o += N_ADA0 * 4 / kb
    mul_x = at("mul_x", o, [P, KT]); o += KT * 4 / kb
    mul_c = at("mul_c", o, [P, KT]); o += KT * 4 / kb
    mul_f = at("mul_f", o, [P, KT]); o += 2 * KT * 4 / kb
    ident = at("ident", o, [P, P]); o += P * 4 / kb
    ones = at("ones", o, [P, P]); o += P * 4 / kb
    pow_at = o
    pow_c = at("pow_c", o, [P, 2, CH + 1, NDQ]); o += 2 * (CH + 1) * NDQ * 4 / kb
    pow_b = at("pow_b", o, [P, 2, CH, NDQ]); o += 2 * CH * NDQ * 4 / kb
    lam8 = at("lam8", o, [P, 2, 2, NDQ]); o += 4 * NDQ * 4 / kb
    assert o <= 62, o
    tab_f = at("tab_f", 62, [P, 2, 4, 512])
    taps_s = at("taps_sum", 78, [P, 4, HYW])
    taps_d = at("taps_dif", 94, [P, 4, HYW])
    decay = at("decay", 110, [P, 2 * HYW])
    f3w = at("f3w", 118, [P, 2 * HYW])
    x_raw = at("x_raw", 126, [P, KT, SEQ])
    c_raw = at("c_raw", 158, [P, KT, CTX])
    ada0 = [at(f"ada0_{j}", 174 + 8 * j, [P, UNIT]) for j in range(4)]
    postab = at("postab", 0, [P, 8, 8 + GRID])
    sqr = [at(f"sqr{j}", 8 + 2 * j, [P, 512]) for j in range(2)]
    T = [at(f"tmp{j}", 16 + 2 * j, [P, 512]) for j in range(16)]
    h_hi = at("h_hi", 62, [P, KT, SEQ], F32R)
    h_lo = at("h_lo", 94, [P, KT, SEQ], F32R)
    hc_hi = at("hc_hi", 126, [P, KT, CTX], F32R)
    hc_lo = at("hc_lo", 142, [P, KT, CTX], F32R)
    gst = [at(f"gate_st{j}", 158 + 2 * j, [P, SEQ]) for j in range(2)]
    zx1 = at("zx1", 162, [P, SEQ])
    ada1 = [at(f"ada1_{j}", 166 + 4 * j, [P, 1024]) for j in range(2)]
    acc1 = at("acc1", 174, [P, 1024])
    u_ch = at("u_ch", 182, [P, ST, CTX + SEQ])
    uh = at("uh", 126, [P, ST, SEQ])
    x0z = at("x0z", 142, [P, ST, SEQ])
    X = at("states", 62, [P, NCH, 2, NDQ])
    s5b = at("s5b", 110, [P, NDQ, 2, GROUP])
    s5c = at("s5c", 118, [P, NDQ, 2, GROUP])
    U4 = at("u4", 158, [P, NPAIR, (CTX + SEQ) // 4])
    bbar = at("bbar", 182, [P, NDQ, 2, 32])
    BL = [at(f"b_lam{d}", 16 + 2 * d, [P, 2, CH, 32]) for d in range(2)]
    MT = [at(f"m_in{d}", 20 + 2 * d, [P, 4, P]) for d in range(2)]
    prod = [at(f"prod{j}", 24 + 1.25 * j, [P, 2, CH + 1, GROUP]) for j in range(4)]
    CL = [[at(f"c_lam{par}{d}", (30, 16)[par] + 2.5 * d, [P, 2, CH + 1, 32]) for d in range(2)] for par in range(2)]
    BB = [[at(f"b_rep{par}{d}", 35 + 2 * par + d, [P, 2, 4, 32]) for d in range(2)] for par in range(2)]
    TL = [at(f"toeplitz{par}", 39 + 2 * par, [P, 2, CH, 32]) for par in range(2)]
    rec = at("rec", 44, [P, 2, 2, NDQ])
    XR = [at(f"states_back{j}", 43 + 0.5 * j, [P, 2, NC_LAT]) for j in range(2)]
    bt = [at(f"bt{j}", 24 + 2 * j, [P, NPAIR, GROUP]) for j in range(4)]
    y_ch = at("y_ch", 94, [P, ST, SEQ])
    yg_hi = at("yg_hi", 62, [P, ST, SEQ], F32R)
    yg_lo = at("yg_lo", 78, [P, ST, SEQ], F32R)
    uT_hi = at("uT_hi", 94, [P, 4, 512], F32R)
    uT_lo = at("uT_lo", 102, [P, 4, 512], F32R)
    tf_hi = at("tf_hi", 158, [P, 2, 4, 512], F32R)
    tf_lo = at("tf_lo", 174, [P, 2, 4, 512], F32R)
    tg_hi = at("tg_hi", 110, [P, 2, 4, 512], F32R)
    tg_lo = at("tg_lo", 190, [P, 2, 4, 512], F32R)
    Y_hi = at("Y_hi", 16, [P, 2, 4, 512], F32R)
    Y_lo = at("Y_lo", 32, [P, 2, 4, 512], F32R)
    kfr = [at(f"kf_in{j}", 8 + 4 * j, [P, 2, 512]) for j in range(2)]
    ct = [at(f"ct{j}", pow_at + 2 * j, [P, 512]) for j in range(4)]
    hyo_hi = at("hyo_hi", 126, [P, ST, SEQ], F32R)
    hyo_lo = at("hyo_lo", 142, [P, ST, SEQ], F32R)
    mg_hi = at("mg_hi", 94, [P, KT, SEQ], F32R)
    mg_lo = at("mg_lo", 158, [P, KT, SEQ], F32R)
    gT = [at(f"gates{j}", 190 + 4 * j, [P, 2, SEQ]) for j in range(2)]
    S0 = [at(f"mrg_a{j}", 198 + 2 * j, [P, SEQ]) for j in range(2)]
    S1 = [at(f"mrg_b{j}", 202 + 2 * j, [P, SEQ]) for j in range(2)]
    xacc = at("xacc", 126, [P, KT, SEQ])
    h2_hi = at("h2_hi", 62, [P, KT, SEQ], F32R)
    h2_lo = at("h2_lo", 94, [P, KT, SEQ], F32R)
    a_hi = at("act_hi", 158, [P, QTILES, SEQ], F32R)
    a_lo = at("act_lo", 180, [P, QTILES, SEQ], F32R)
    f_s = at("ffn_silu", 202, [P, SEQ])
    f_t = at("ffn_prod", 204, [P, SEQ])

    ps = [nc.alloc_psum_tensor(f"ps{j}", [P, 512], F32) for j in range(8)]

    fh = [at(f"fh{j}", 16 + 2 * j, [HID, SEQ]) for j in range(4)]
    lt = at("lam_tmp", 32.75, [P, 13, NDQ])
    lam_rr, lam_ii = (at(n, 46.5 + 0.5 * j, [P, 2, NDQ]) for j, n in enumerate(("lam_rr", "lam_ii")))
    s5a = at("s5a", 32, [P, 3, NDQ])
    feats = at("feats", 36, [POSD, SEQ])
    f1w = at("f1w", 38, [POSD, HID])
    f2w = at("f2w", 38.5, [HID, HID])
    fpar = at("fpar", 39, [HID, 4])
    pwt = at("pow_b_tmp", 39.5, [P, 2, CH, NPAIR])
    pw = at("pow_tmp", 42, [P, 2, CH + 1, NDQ])

    def sem(name):
        return nc.alloc_semaphore(name)

    s_vec, s_par, s_filt, s_tabf, s_x, s_ctx = (sem(n) for n in
        ("vec_loaded", "s5a_loaded", "filter_loaded", "tabf_loaded", "x_loaded", "ctx_loaded"))
    s_pos = sem("postab_loaded")
    ada0_in = [sem(f"ada0_loaded{j}") for j in range(4)]
    ada0_used, ada1_used = sem("ada0_used"), sem("ada1_used")
    ada1_in = [sem(f"ada1_loaded{j}") for j in range(2)]
    w_in = [sem(f"w_loaded{j}") for j in range(2)]
    w_hi, w_lo, w_used = sem("w_hi_ready"), sem("w_lo_ready"), sem("w_used")
    dch, ach, pch = sem("dve_chain"), sem("act_chain"), sem("pool_chain")
    s_silu = sem("silu_c_ready")
    s_mod = sem("mod_ready")
    ada0_ps, acc1_red = sem("ada0_psum"), sem("ada1_acc_reduced")
    s_h1p, s_h1a, s_h1 = sem("filter_psum"), sem("filter_arg"), sem("filter_sin")
    f3_ps, f3_free, s_win, s_tap = sem("f3_psum"), sem("f3_free"), sem("window_ready"), sem("taps_ready")
    s_absd = sem("decay_abs")
    kf_ps, kf_free_a, kf_free_d = (sem(n) for n in ("kf_psum", "kf_evac_act", "kf_evac_dve"))
    kf_out = [sem(f"kf_stored{j}") for j in range(2)]
    lam_z, lam_s = sem("lam_arg"), sem("lam_sin")
    s_xp, s_xpo, s_sq, s_squ = sem("xp_ready"), sem("xp_stored"), sem("square_ready"), sem("square_used")
    s_var, s_sqrt = sem("var_ready"), sem("sqrt_ready")
    s_ss = sem("sumsq_psum")
    s_cmod, s_hv, s_hh, s_hl = sem("const_ready"), sem("h_ready"), sem("h_hi_ready"), sem("h_lo_ready")
    u_fa, u_fd = sem("u_evac_act"), sem("u_evac_dve")
    hy_free = sem("hy_free")
    g_free = sem("gate_free")
    g_st = [sem(f"gate_stored{j}") for j in range(2)]
    s_bc = sem("s5bc_loaded")
    u4a, u4d = sem("u4_act"), sem("u4_dve")
    bl_rd = [sem(f"blam_ready{d}") for d in range(2)]
    cl_rd = [sem(f"clam_ready{d}") for d in range(2)]
    bl_tr, mt_rd, xs_ps, xs_ev = (sem(n) for n in ("blam_transposed", "m_in_ready", "x_psum", "x_stored"))
    rec_dn = sem("scan_done")
    s_bneg, s_zero = sem("s5b_conjugated"), sem("s5_tables_cleared")
    bb_rd, l_ps, tl_a, tl_d, y_ps, y_ev = (sem(n) for n in
        ("brep_ready", "taps_psum", "toepl_act", "toepl_dve", "y_psum", "y_stored"))
    ych, ycd, gel, ygh, ygl = (sem(n) for n in ("ych_act", "ych_dve", "gelu_ready", "yg_hi_ready", "yg_lo_ready"))
    tab_h, tab_l = sem("tab_hi_ready"), sem("tab_lo_ready")
    ut_ps, ut_h, ut_l = sem("uT_psum"), sem("uT_hi_ready"), sem("uT_lo_ready")
    pq_ps, pq_ev, k_in = sem("spec_psum"), sem("spec_free"), [sem(f"kf_in{j}") for j in range(2)]
    yv, yh, yl = sem("Y_ready"), sem("Y_hi_ready"), sem("Y_lo_ready")
    cv_ps, cv_free, ov, oh, ol = (sem(n) for n in ("conv_psum", "conv_free", "hyo_ready", "hyo_hi_ready", "hyo_lo_ready"))
    gt_in = [sem(f"gates_loaded{j}") for j in range(2)]
    m_sg, m_free, m_sum, m_hi, m_lo = (sem(n) for n in
        ("glu_sigmoid", "merge_free", "merged_ready", "merged_hi_ready", "merged_lo_ready"))
    xa_in = [sem(f"xacc_loaded{j}") for j in range(4)]
    o_free = sem("out_free")
    s_acc = sem("acc_ready")
    s_hm = sem("h_scaled")
    fa_free, ft_rd, fh_rd, fl_rd = (sem(n) for n in
        ("ffn_a_free", "ffn_prod_ready", "ffn_hi_ready", "ffn_lo_ready"))
    fd_free = sem("ffn_out_free")
    o_rd, s_out = sem("out_ready"), sem("out_stored")

    def halves(tensor, ri, idx0, idx1):
        return [tensor[64 * g:64 * g + 64, ri, idx0:idx1, 16 * g:16 * g + 16] for g in range(2)]

    gates_v = gates_d.rearrange("(g m) p t -> g m p t", g=2)

    with nc.Block() as block:
        @block.sync
        def _(sp):
            sp.dma_start(vecs[:, :], vecs_d).then_inc(s_vec, 16)
            sp.dma_start(ident[:, :], ident_d).then_inc(s_vec, 16)
            sp.dma_start(s5a[:, :, :], s5a_d).then_inc(s_par, 16)
            sp.dma_start(feats[:, :], feats_d).then_inc(s_filt, 16)
            sp.dma_start(f1w[:, :], f1w_d).then_inc(s_filt, 16)
            sp.dma_start(f2w[:, :], f2w_d).then_inc(s_filt, 16)
            sp.dma_start(fpar[:, :], fpar_d).then_inc(s_filt, 16)
            sp.dma_start(f3w[0:HID, :], f3w_d).then_inc(s_filt, 16)
            sp.dma_start(decay[:, :], decay_d.to_broadcast([P, 2 * HYW])).then_inc(s_filt, 16)
            for s in range(2):
                sp.dma_start(tab_f[:, s, :, :], tabs_d[s].rearrange("p (t k) -> p t k", t=4)).then_inc(s_tabf, 16)
            with sp.Fori(0, N_ADA0 // 4) as i:
                for j in range(4):
                    sp.wait_ge(ada0_used, 4 * i + j + 1)
                    sp.dma_start(ada0[j][:, :], w_ada_d[4 * i + j]).then_inc(ada0_in[j], 16)
            sp.wait_ge(s_xp, KT)
            sp.dma_start(raw[0][:, :], w_in_d[0]).then_inc(w_in[0], 16)
            sp.wait_ge(s_squ, 2 * KT + 2)
            sp.dma_start(raw[1][:, :], w_in_d[1]).then_inc(w_in[1], 16)
            with sp.Fori(1, 32) as i:
                for b in range(2):
                    sp.wait_ge(w_lo, 2 * i + b - 1)
                    sp.dma_start(raw[b][:, :], w_in_d[2 * i + b]).then_inc(w_in[b], 16)
            for s in range(4):
                sp.wait_ge(w_lo, U_TAB + s - 1)
                sp.dma_start(raw[s % 2][:, :], tabs_d[s]).then_inc(w_in[s % 2], 16)
            sp.wait_ge(w_lo, U_MRG)
            sp.dma_start(raw[0][:, :], w_glu_d[0]).then_inc(w_in[0], 16)
            for half in range(2):
                for f in range(4):
                    j = f % 2
                    if 4 * half + f >= 2:
                        sp.wait_ge(pq_ev, 4 * half + f - 1)
                    sp.dma_start(kfr[j][:, :, :],
                                 kf_d[f, :, :, 512 * half:512 * half + 512].rearrange("s p c -> p s c")
                                 ).then_inc(k_in[j], 16)
            sp.wait_ge(pq_ev, 8)
            sp.dma_start(raw[1][:, 0:1024], w_hy_d[0]).then_inc(w_in[1], 16)
            with sp.Fori(1, 16) as m:
                sp.wait_ge(w_lo, U_MRG + 2 * m - 1)
                sp.dma_start(raw[0][:, :], w_glu_d[m]).then_inc(w_in[0], 16)
                sp.wait_ge(w_lo, U_MRG + 2 * m)
                sp.dma_start(raw[1][:, 0:1024], w_hy_d[m]).then_inc(w_in[1], 16)
            with sp.Fori(0, 8) as i:
                for b in range(2):
                    sp.wait_ge(w_lo, U_OUT + 2 * i + b - 1)
                    sp.dma_start(raw[b][:, :], w_out_d[2 * i + b]).then_inc(w_in[b], 16)
            for q in range(4):
                n0 = U_FFN + U_QUARTER * q
                with sp.Fori(0, QTILES) as i:
                    for b in range(2):
                        sp.wait_ge(w_lo, n0 + 2 * i + b - 1)
                        sp.dma_start(raw[b][:, :], w_fi_d[2 * QTILES * q + 2 * i + b]).then_inc(w_in[b], 16)
                with sp.Fori(0, KT // 2) as i:
                    for b in range(2):
                        sp.wait_ge(w_lo, n0 + 2 * QTILES + 2 * i + b - 1)
                        sp.dma_start(raw[b][:, 0:UNIT2], w_fo_d[KT * q + 2 * i + b]).then_inc(w_in[b], 16)
            for g in range(4):
                sp.wait_ge(o_rd, 4 * (g + 1))
                sp.dma_start(out_d[4 * g:4 * g + 4].rearrange("k p t -> p k t"),
                             xacc[:, 4 * g:4 * g + 4, :]).then_inc(s_out, 16)
            sp.wait_ge(s_out, 64)

        @block.gpsimd
        def _(pool):
            pool.sem_inc(ada0_used, 4)
            for s, n in ((w_used, 2), (u_fa, 2), (u_fd, 2), (hy_free, 2), (g_free, 2), (m_free, 2), (o_free, 2),
                         (fa_free, 1), (fd_free, 2), (s_squ, 2), (f3_free, 1),
                         (ada1_used, 1), (bl_tr, 2), (mt_rd, 2), (xs_ps, 2), (xs_ev, 2), (l_ps, 2), (y_ps, 2), (tl_a, 2),
                         (tl_d, 2), (y_ev, 2), (ft_rd, 1), (g_st[0], 16), (g_st[1], 16)):
                pool.sem_inc(s, n)
            chain = Chain(pool, pch)
            link = chain.link
            tt, ts = pool.tensor_tensor, pool.tensor_scalar
            pool.memset(ones[:, :], 1.0).then_inc(s_cmod, 1)
            for g in range(4):
                pool.dma_start(x_raw[:, 4 * g:4 * g + 4, :], x_d[:, 4 * g:4 * g + 4, :]).then_inc(s_x, 16)
            pool.dma_start(postab[:, :, :], postab_d).then_inc(s_pos, 16)
            pool.dma_start(c_raw[:, :, :], ctx_d).then_inc(s_ctx, 16)
            for g in range(4):
                pool.wait_ge(s_xp, 4 * g + 4)
                pool.dma_start(xp_d[:, 4 * g:4 * g + 4, :], x_raw[:, 4 * g:4 * g + 4, :]).then_inc(s_xpo, 16)
            for st in range(8):
                f, cs = st // 2, st % 2
                pool.wait_ge(kf_free_a, st + 1)
                pool.wait_ge(kf_free_d, st + 1)
                for half in range(2):
                    pool.dma_start(kf_d[f, cs, :, 512 * half:512 * half + 512],
                                   T[12 + 2 * (st % 2) + half][:, :]).then_inc(kf_out[st % 2], 16)
            pool.wait_ge(s_hl, 2 * KT)
            for e in range(2):
                pool.dma_start(ada1[e][:, :], w_ar_d[e]).then_inc(ada1_in[e], 16)
            with pool.Fori(1, 64) as g:
                for e in range(2):
                    pool.wait_ge(ada1_used, 2 * g + e)
                    pool.dma_start(ada1[e][:, :], w_ar_d[2 * g + e]).then_inc(ada1_in[e], 16)
            pool.wait_ge(w_used, 2 + U_TAB)
            pool.dma_start(s5b[:, :, :, :], s5b_d).then_inc(s_bc, 16)
            pool.dma_start(s5c[:, :, :, :], s5c_d).then_inc(s_bc, 16)
            pool.wait_ge(s_bc, 32)
            link(ts(s5b[:, :, 1, :], s5b[:, :, 1, :], -1.0, None, MUL))
            pool.sem_inc(s_bneg, 1)
            pool.wait_ge(s_zero, 1)

            def table(q, dst, pows, modes, n, tP, tQ, free, ready):
                tt(tP[:, :, 0:n, :], pows, modes, MUL)
                tt(tQ[:, 0, 0:n, :], pows[:, 0], modes[:, 1], MUL)
                link(tt(tQ[:, 1, 0:n, :], pows[:, 1], modes[:, 0], MUL))
                pool.wait_ge(*free)
                for ri, (src, op) in enumerate(((tP, SUB), (tQ, ADD))):
                    for g, out in enumerate(halves(dst, ri, 0, n)):
                        r = slice(64 * g, 64 * g + 64)
                        ins = tt(out, src[r, 0, 0:n, :], src[r, 1, 0:n, :], op)
                ins.then_inc(ready, 1)
                pool.wait_ge(ready, q + 1)

            with chain.loop(0, NPAIR, 1) as q:
                dq = NPAIR + q
                table(q, BL[1], pow_b[:, :, :, dq].unsqueeze(3).to_broadcast([P, 2, CH, GROUP]),
                      s5b[:, dq, :, :].unsqueeze(2).to_broadcast([P, 2, CH, GROUP]), CH, prod[2], prod[3],
                      (bl_tr, 2 * q + 2), bl_rd[1])
            pool.wait_ge(rec_dn, 1)
            with chain.loop(0, NPAIR // 2, 2) as i:
                for par in range(2):
                    q = 2 * i + par
                    dq = NPAIR + q
                    table(q, CL[par][1], pow_c[:, :, :, dq].unsqueeze(3).to_broadcast([P, 2, CH + 1, GROUP]),
                          s5c[:, dq, :, :].unsqueeze(2).to_broadcast([P, 2, CH + 1, GROUP]), CH + 1, prod[2],
                          prod[3], (y_ps, q + 1), cl_rd[1])
            pool.wait_ge(cv_ps, 8)
            for m in range(2):
                pool.dma_start(gT[m][:, :, :], gates_v[:, m].rearrange("g p t -> p g t")).then_inc(gt_in[m], 16)
            with pool.Fori(1, KT // 2) as i:
                for b in range(2):
                    m = 2 * i + b
                    pool.wait_ge(m_sum, m - 1)
                    pool.dma_start(gT[b][:, :, :],
                                   gates_v[:, bass.ds(m, 1)].rearrange("g o p t -> p (g o) t")
                                   ).then_inc(gt_in[b], 16)
            pool.wait_ge(w_used, 2 + U_OUT)
            for g in range(4):
                pool.dma_start(xacc[:, 4 * g:4 * g + 4, :], xp_d[:, 4 * g:4 * g + 4, :]).then_inc(xa_in[g], 16)

        @block.scalar
        def _(act):
            chain = Chain(act, ach)

            def split_hi(n, half, b, cols=UNIT):
                act.wait_ge(w_in[b], 16 * (half + 1))
                act.wait_ge(w_used, n + 1)
                act.activation(hi[b][:, 0:cols], raw[b][:, 0:cols], ACT.Copy).then_inc(w_hi, 1)

            act.wait_ge(s_vec, 32)
            act.activation(silu_c[:, :, 0], vecs[:, V_C:V_C + KT], ACT.Silu)
            act.activation(silu_c[:, :, 1], vecs[:, V_CC:V_CC + KT], ACT.Silu).then_inc(s_silu, 1)
            act.wait_ge(s_par, 16)
            act.activation(lt[:, 0, :], s5a[:, 2, :], ACT.Exp).then_inc(lam_s, 1)
            act.wait_ge(lam_z, 1)
            act.activation(lt[:, 3, :], lt[:, 1, :], ACT.Exp).then_inc(lam_s, 1)
            act.wait_ge(lam_z, 2)
            act.activation(lt[:, 7, :], lt[:, 5, :], ACT.Sin)
            act.activation(lt[:, 8, :], lt[:, 6, :], ACT.Sin).then_inc(lam_s, 1)
            act.wait_ge(s_h1a, 1)
            act.activation(fh[2][:, :], fh[0][:, :], ACT.Sin).then_inc(s_h1, 1)
            act.wait_ge(s_h1a, 2)
            act.activation(fh[3][:, :], fh[0][:, :], ACT.Sin).then_inc(s_h1, 1)
            act.wait_ge(s_absd, 1)
            for t in range(4):
                if t:
                    act.wait_ge(s_tap, t)
                for c in range(4):
                    act.activation(T[4 + c][:, :], decay[:, 512 * c:512 * c + 512], ACT.Exp,
                                   scale=vecs[:, V_NEGT + t:V_NEGT + t + 1]).then_inc(s_win, 1)
            for k in range(2 * KT):
                act.wait_ge(s_squ, k + 1)
                if k < KT:
                    act.wait_ge(s_xp, k + 1)
                    act.activation(sqr[k % 2][:, :], x_raw[:, k, :], ACT.Square).then_inc(s_sq, 1)
                else:
                    if k == KT:
                        act.wait_ge(s_ctx, 16)
                    act.activation(sqr[k % 2][:, 0:CTX], c_raw[:, k - KT, :], ACT.Square).then_inc(s_sq, 1)
            for st in range(8):
                act.wait_ge(kf_ps, st + 1)
                if st >= 2:
                    act.wait_ge(kf_out[st % 2], 32 * (st // 2))
                act.activation(T[12 + 2 * (st % 2)][:, :], ps[2 * (st % 2)][:, :], ACT.Copy).then_inc(kf_free_a, 1)
            for v, (a, b, w) in enumerate(((T[1], T[2], SEQ), (T[5], T[6], CTX))):
                act.wait_ge(s_var, v + 1)
                act.activation(b[:, 0:w], a[:, 0:w], ACT.Sqrt).then_inc(s_sqrt, 1)
            with act.Fori(0, KT // 2) as i:
                for b in range(2):
                    act.wait_ge(s_hv, 2 * i + b + 1)
                    act.activation(h_hi[:, 2 * i + b, :], T[8 + b][:, :], ACT.Copy).then_inc(s_hh, 1)
            act.wait_ge(s_xpo, 64)
            act.wait_ge(s_hl, KT)
            with act.Fori(0, KT // 2) as i:
                for b in range(2):
                    act.wait_ge(s_hv, KT + 2 * i + b + 1)
                    act.activation(hc_hi[:, 2 * i + b, :], T[8 + b][:, 0:CTX], ACT.Copy).then_inc(s_hh, 1)
            act.wait_ge(s_hl, 2 * KT)
            for j in range(2):
                act.wait_ge(kf_out[j], 128)
            split_hi(0, 0, 0)
            with act.Fori(0, 4) as i:
                for b in range(2):
                    split_hi(2 * i + b + 1, i + b, 1 - b)
                    act.wait_ge(w_used, 2 + 2 * i + b + 1)
                    act.activation(u_ch[:, 2 * i + b, CTX:CTX + SEQ], ps[b][:, :], ACT.Copy).then_inc(u_fa, 1)
            with act.Fori(0, 12) as i:
                for b in range(2):
                    split_hi(8 + 2 * i + b + 1, 4 + i + b, 1 - b)
            def gate_tile(i, b):
                act.wait_ge(w_used, 2 + 32 + 2 * i + b + 1)
                act.wait_ge(g_st[b], 16 * i + 16)
                act.activation(gst[b][:, :], ps[b][:, :], ACT.Sigmoid).then_inc(g_free, 1)
                act.wait_ge(g_free, 2 + 2 * i + b + 1)
                act.dma_start(gates_d[2 * i + b], gst[b][:, :]).then_inc(g_st[b], 16)

            with act.Fori(0, 15) as i:
                for b in range(2):
                    split_hi(32 + 2 * i + b + 1, 16 + i + b, 1 - b)
                    gate_tile(i, b)
            split_hi(63, 31, 1)
            gate_tile(15, 0)
            gate_tile(15, 1)
            for b in range(2):
                act.wait_ge(g_st[b], 16 * 17)
            act.wait_ge(acc1_red, 8)
            act.wait_ge(u_fd, 10)
            for q in range(4):
                for j in range(0, 4, 2):
                    ins = act.activation(U4[32 * j:32 * j + 32, q::4, :],
                                         u_ch[32 * q:32 * q + 32, :, j::4], ACT.Copy)
                ins.then_inc(u4a, 1)
            with act.Fori(0, NPAIR) as q:
                for d in range(2):
                    act.wait_ge(bl_tr, 2 * q + d + 3)
                    act.wait_ge(xs_ps, 2 * q + d + 1)
                    act.activation(MT[d][:, :, :].rearrange("p a b -> p (a b)"), ps[d][:, :],
                                   ACT.Copy).then_inc(mt_rd, 1)
                for d in range(2):
                    act.wait_ge(xs_ps, 2 * q + d + 3)
                    src = ps[2 + d][:, 0:2 * NCH].rearrange("p (r c) -> p c r", r=2)
                    dq = NPAIR * d + q
                    if d == 0:
                        act.activation(X[:, :, :, dq], src, ACT.Copy).then_inc(xs_ev, 1)
                    else:
                        act.activation(X[:, 0:NC_CTX, :, dq], src[:, NC_CTX - 1::-1, :], ACT.Copy)
                        act.activation(X[:, NC_CTX:NCH, :, dq], src[:, NCH - 1:NC_CTX - 1:-1, :],
                                       ACT.Copy).then_inc(xs_ev, 1)
            act.wait_ge(rec_dn, 1)

            def replicas(q, par):
                act.wait_ge(l_ps, q + 1)
                act.wait_ge(y_ps, q + 1)
                act.activation(XR[par][:, :, ::-1], X[:, NC_CTX - 1:NCH - 1, :, NPAIR + q].rearrange("p c r -> p r c"),
                               ACT.Copy)
                for d in range(2):
                    ins = act.activation(BB[par][d][:, :, :, :],
                                         bbar[:, NPAIR * d + q, :, :].unsqueeze(2).to_broadcast([P, 2, 4, 32]),
                                         ACT.Copy)
                ins.then_inc(bb_rd, 1)

            def toeplitz(q, par):
                act.wait_ge(l_ps, q + 3)
                for j in range(3):
                    for a in range(2):
                        o7 = 32 * (CH - 1 - 4 * a - j)
                        ins = act.activation(TL[par][32 * j:32 * j + 32, a, :, :].rearrange("p i h -> p (i h)"),
                                             ps[4 + 2 * par][32 * j:32 * j + 32, o7:o7 + 256], ACT.Copy)
                ins.then_inc(tl_a, 1)

            replicas(0, 0)
            with act.Fori(0, NPAIR // 2 - 1) as i:
                for par in range(2):
                    replicas(2 * i + par + 1, 1 - par)
                    toeplitz(2 * i + par, par)
            replicas(NPAIR - 1, 1)
            toeplitz(NPAIR - 2, 0)
            toeplitz(NPAIR - 1, 1)
            act.wait_ge(y_ev, NPAIR + 2)
            for q in range(4):
                for j in range(0, 4, 2):
                    ins = act.activation(y_ch[32 * q:32 * q + 32, :, j::4],
                                         U4[32 * j:32 * j + 32, q::4, CTX // 4:], ACT.Copy)
            ins.then_inc(ych, 1)
            act.wait_ge(ych, 1)
            act.wait_ge(ycd, 1)
            for g in range(2):
                act.activation(y_ch[:, 4 * g:4 * g + 4, :], y_ch[:, 4 * g:4 * g + 4, :],
                               ACT.Gelu_apprx_tanh).then_inc(gel, 1)
                act.wait_ge(gel, g + 1)
                act.activation(yg_hi[:, 4 * g:4 * g + 4, :], y_ch[:, 4 * g:4 * g + 4, :], ACT.Copy).then_inc(ygh, 1)
            for s in range(4):
                act.wait_ge(w_in[s % 2], 16 * (33 + s // 2))
                dst = (tf_hi, tg_hi)[s // 2][:, s % 2, :, :].rearrange("p a b -> p (a b)")
                act.activation(dst, raw[s % 2][:, :], ACT.Copy).then_inc(w_hi, 1)

            def transposed_u(half):
                for t in range(4):
                    act.wait_ge(ut_ps, 4 * half + t + 1)
                    act.activation(uT_hi[:, t, :], ps[t % 2][:, :], ACT.Copy).then_inc(ut_h, 1)

            def spectrum(half):
                for f in range(4):
                    for c in range(2):
                        act.wait_ge(yv, 8 * half + 2 * f + c + 1)
                        if half and f == 0 and c == 0:
                            act.wait_ge(cv_ps, 4)
                        act.activation(Y_hi[:, c, f, :], ct[2 + c][:, :], ACT.Copy).then_inc(yh, 1)

            def conv_out(half):
                for c in range(4):
                    i = 4 * half + c
                    act.wait_ge(ov, i + 1)
                    act.activation(hyo_hi[:, i, :], ct[1][:, :], ACT.Copy).then_inc(oh, 1)

            act.wait_ge(ygl, 2)
            transposed_u(0)
            spectrum(0)
            act.wait_ge(pq_ps, 4)
            transposed_u(1)
            conv_out(0)
            spectrum(1)
            conv_out(1)
            def merge(n, m, half, mm, last=False):
                split_hi(n + 1, half, 1, 1024)
                act.wait_ge(w_used, n + 3)
                act.activation(S0[mm][:, :], ps[3 * mm + 1][:, :], ACT.Sigmoid).then_inc(m_sg, 1)
                split_hi(n + 2, half + 1, 0)
                act.wait_ge(m_sum, m + 1)
                act.activation(mg_hi[:, m, :], S1[mm][:, :], ACT.Copy).then_inc(m_hi, 1)

            split_hi(U_MRG, U_MRG // 2, 0)
            with act.Fori(0, KT // 2) as i:
                for mm in range(2):
                    merge(U_MRG + 4 * i + 2 * mm, 2 * i + mm, U_MRG // 2 + 2 * i + mm, mm)
            with act.Fori(0, KT // 2) as i:
                for b in range(2):
                    split_hi(U_OUT + 2 * i + b + 1, U_OUT // 2 + i + b, 1 - b)

            def sqrt_and_h(v):
                act.wait_ge(s_var, v + 1)
                act.activation(ct[3][:, :], ct[2][:, :], ACT.Sqrt).then_inc(s_sqrt, 1)

            sqrt_and_h(2)
            with act.Fori(0, KT // 2) as i:
                for b in range(2):
                    act.wait_ge(s_hv, 2 * KT + 2 * i + b + 1)
                    act.activation(h2_hi[:, 2 * i + b, :], ct[1 + b][:, :], ACT.Copy).then_inc(s_hh, 1)
            for q in range(4):
                n0, g0 = U_FFN + U_QUARTER * q, QTILES * q

                def pair(i, cols):
                    n, half = n0 + 2 * i, n0 // 2 + i
                    split_hi(n + 1, half, 1)
                    act.wait_ge(w_used, n + 3)
                    act.activation(f_s[:, :], ps[0][:, :], ACT.Silu).then_inc(fa_free, 1)
                    split_hi(n + 2, half + 1, 0, cols)
                    act.wait_ge(ft_rd, g0 + i + 2)
                    act.activation(a_hi[:, i, :], f_t[:, :], ACT.Copy).then_inc(fh_rd, 1)

                with act.Fori(0, QTILES - 1) as i:
                    pair(i, UNIT)
                pair(QTILES - 1, UNIT2)
                n1 = n0 + 2 * QTILES
                with act.Fori(0, KT // 2 - 1) as i:
                    for b in range(2):
                        split_hi(n1 + 2 * i + b + 1, n1 // 2 + i + b, 1 - b, UNIT2)
                split_hi(n1 + KT - 1, n1 // 2 + KT // 2 - 1, 1, UNIT2)
                if q < 3:
                    split_hi(n1 + KT, n1 // 2 + KT // 2, 0)
            sqrt_and_h(3)

        @block.vector
        def _(dve):
            chain = Chain(dve, dch)
            link, mark = chain.link, chain.mark
            tt, ts, stt = dve.tensor_tensor, dve.tensor_scalar, dve.scalar_tensor_tensor

            def split_lo(n, b, cols=UNIT):
                dve.wait_ge(w_hi, n + 1)
                tt(lo[b][:, 0:cols], raw[b][:, 0:cols], hi[b][:, 0:cols].bitcast(F32), SUB).then_inc(w_lo, 1)

            def reduce_angle(dst, k, src, shift):
                link(ts(k, src, 1.0 / (2 * math.pi), shift / (2 * math.pi), MUL, ADD))
                link(ts(k, k, MAGIC, MAGIC, ADD, SUB))
                link(stt(dst, k, -TWO_PI_1, src, MUL, ADD))
                link(stt(dst, k, -TWO_PI_2, dst, MUL, ADD))
                link(stt(dst, k, -TWO_PI_3, dst, MUL, ADD))
                link(ts(dst, dst, shift, PI_SAFE, ADD, ALU.min))
                return ts(dst, dst, -PI_SAFE, None, ALU.max)

            def rstd(v, sums, a, b, c, out, w):
                dve.wait_ge(s_ss, v + 1)
                link(ts(a, sums, 1.0 / D, EPS, MUL, ADD))
                dve.reciprocal(b, a).then_inc(s_var, 1)
                dve.wait_ge(s_sqrt, v + 1)
                link(tt(b, c, c, MUL))
                link(tt(b, b, a, MUL))
                link(ts(b, b, -0.5, 1.5, MUL, ADD))
                link(tt(out, b, c, MUL))

            a_re, a_im = s5a[:, 0, :], s5a[:, 1, :]
            L = [lt[:, j, :] for j in range(13)]
            dve.wait_ge(lam_s, 1)
            tt(L[1], a_re, L[0], MUL).then_inc(lam_z, 1)
            link(tt(L[2], a_im, L[0], MUL))
            link(reduce_angle(L[5], L[4], L[2], 0.0))
            reduce_angle(L[6], L[4], L[2], math.pi / 2).then_inc(lam_z, 1)
            dve.wait_ge(lam_s, 3)
            tt(lam_rr[:, 0, :], L[3], L[8], MUL)
            link(tt(lam_ii[:, 1, :], L[3], L[7], MUL))
            dve.tensor_copy(lam_rr[:, 1, :], lam_rr[:, 0, :])
            ts(lam_ii[:, 0, :], lam_ii[:, 1, :], -1.0, None, MUL)
            ts(L[9], lam_rr[:, 0, :], -1.0, None, ADD)
            tt(L[10], a_re, a_re, MUL)
            link(tt(L[11], a_im, a_im, MUL))
            link(tt(L[10], L[10], L[11], ADD))
            dve.reciprocal(L[10], L[10])
            tt(L[0], L[9], a_re, MUL)
            tt(L[1], lam_ii[:, 1, :], a_im, MUL)
            tt(L[2], lam_ii[:, 1, :], a_re, MUL)
            link(tt(L[3], L[9], a_im, MUL))
            tt(L[0], L[0], L[1], ADD)
            link(tt(L[2], L[2], L[3], SUB))
            tt(L[4], L[0], L[10], MUL)
            tt(L[5], L[0], L[10], MUL)
            link(tt(L[7], L[2], L[10], MUL))
            link(ts(L[6], L[7], -1.0, None, MUL))
            dve.memset(pw[:, 0, 0, :], 1.0)
            dve.memset(pw[:, 1, 0, :], 0.0)
            dve.tensor_copy(pw[:, 0, 1, :], lam_rr[:, 0, :])
            link(dve.tensor_copy(pw[:, 1, 1, :], lam_ii[:, 1, :]))
            tmp2 = lt[:, 9:11, :]
            for k in range(2, CH + 1):
                tt(tmp2, pw[:, ::-1, k - 1, :], lam_ii[:, :, :], MUL)
                link(tt(pw[:, :, k, :], pw[:, :, k - 1, :], lam_rr[:, :, :], MUL))
                link(tt(pw[:, :, k, :], pw[:, :, k, :], tmp2, ADD))
            for d in range(2):
                cols = slice(NPAIR * d, NPAIR * d + NPAIR)
                dve.tensor_copy(pow_c[:, :, :, cols], pw[:, :, :, cols] if d == 0 else pw[:, :, ::-1, cols])
                if d == 0:
                    src, swp = pw[:, :, CH - 1::-1, cols], pw[:, ::-1, CH - 1::-1, cols]
                else:
                    src, swp = pw[:, :, 0:CH, cols], pw[:, ::-1, 0:CH, cols]
                for ri in range(2):
                    tt(pow_b[:, ri, :, cols], src[:, ri], L[4][:, cols].unsqueeze(1).to_broadcast([P, CH, NPAIR]), MUL)
                    ins = tt(pwt[:, ri, :, :], swp[:, ri],
                             L[6 + ri][:, cols].unsqueeze(1).to_broadcast([P, CH, NPAIR]), MUL)
                link(ins)
                link(tt(pow_b[:, :, :, cols], pow_b[:, :, :, cols], pwt[:, :, :, :], ADD))
                link(ts(pow_b[:, 1, :, cols], pow_b[:, 1, :, cols], -1.0, None, MUL))
            for ri in range(2):
                dve.tensor_copy(lam8[:, 0, ri, :], pw[:, 0, CH, :])
                ts(lam8[:, 1, ri, :], pw[:, 1, CH, :], (-1.0, 1.0)[ri], None, MUL)

            dve.wait_ge(s_filt, 96)
            for layer in range(2):
                dve.wait_ge(s_h1p, layer + 1)
                link(ts(fh[1][:, :], ps[5][0:HID, :], fpar[:, 2 * layer:2 * layer + 1],
                        fpar[:, 2 * layer + 1:2 * layer + 2], ADD, MUL))
                k = T[4][0:HID, :]
                reduce_angle(fh[0][:, :], k, fh[1][:, :], 0.0).then_inc(s_h1a, 1)
            link(ts(T[5][:, :], decay[:, 0:512], -1.0, None, MUL))
            for c in range(4):
                if c:
                    link(ts(T[5][:, :], decay[:, 512 * c:512 * c + 512], -1.0, None, MUL))
                link(tt(decay[:, 512 * c:512 * c + 512], decay[:, 512 * c:512 * c + 512], T[5][:, :], ALU.max))
            dve.sem_inc(s_absd, 1)
            dve.wait_ge(s_pos, 16)
            for k in range(KT):
                if k % 4 == 0:
                    dve.wait_ge(s_x, 64) if k == 0 else None
                xk = x_raw[:, k, :].rearrange("p (r c) -> p r c", c=GRID)
                if k < 8:
                    pos = postab[:, k, 0:8].unsqueeze(2).to_broadcast([P, 8, GRID])
                else:
                    pos = postab[:, k - 8, 8:8 + GRID].unsqueeze(1).to_broadcast([P, 8, GRID])
                tt(xk, xk, pos, ADD).then_inc(s_xp, 1)
            for t in range(4):
                dve.wait_ge(f3_ps, t + 1)
                dve.wait_ge(s_win, 4 * t + 4)
                for c in range(4):
                    ins = tt(T[4 + c][:, :], ps[c][:, :], T[4 + c][:, :], MUL)
                if t == 0:
                    link(ins)
                    for c in range(2, 4):
                        ins = dve.memset(T[4 + c][0:1, :], 0.0)
                ins.then_inc(f3_free, 1)
                dve.wait_ge(f3_free, t + 2)
                for half in range(2):
                    tt(taps_s[:, t, 512 * half:512 * half + 512], T[4 + half][:, :], T[6 + half][:, :], ADD)
                    ins = tt(taps_d[:, t, 512 * half:512 * half + 512], T[4 + half][:, :], T[6 + half][:, :], SUB)
                ins.then_inc(s_tap, 1)
            for st in range(8):
                dve.wait_ge(kf_ps, st + 1)
                if st >= 2:
                    dve.wait_ge(kf_out[st % 2], 32 * (st // 2))
                dve.tensor_copy(T[13 + 2 * (st % 2)][:, :], ps[2 * (st % 2) + 1][:, :]).then_inc(kf_free_d, 1)
            rstd(0, ps[4][:, :], T[0][:, :], T[1][:, :], T[2][:, :], T[3][:, :], SEQ)
            rstd(1, ps[5][:, 0:CTX], T[4][:, 0:CTX], T[5][:, 0:CTX], T[6][:, 0:CTX], T[7][:, 0:CTX], CTX)
            dve.wait_ge(ada0_ps, 1)
            pa = ps[6][:, 0:2 * N_ADA0].rearrange("p (m s) -> p m s", s=2)
            tt(mod_x[:, 0:N_ADA0], pa[:, :, 0], vecs[:, V_BADA:V_BADA + N_ADA0], ADD)
            link(tt(mod_c[:, :], pa[:, :, 1], vecs[:, V_BADA:V_BADA + N_ADA0], ADD))
            for mod, mul in ((mod_x, mul_x), (mod_c, mul_c)):
                ins = stt(mul[:, :], mod[:, KT:2 * KT], 1.0, vecs[:, V_NM:V_NM + KT], ADD, MUL)
            link(ins)

            def modulated(src, rs, tmp, mul, mod, shift0, done, dst_hi, dst_lo, w):
                with dve.Fori(0, KT // 2) as i:
                    for b in range(2):
                        k = 2 * i + b
                        stt(tmp[b], src[:, k, :], mul[:, bass.ds(k, 1)], rs, MUL, MUL).then_inc(s_hm, 1)
                    for b in range(2):
                        k = 2 * i + b
                        dve.wait_ge(s_hm, done + k + 1)
                        ts(tmp[b], tmp[b], mod[:, bass.ds(shift0 + k, 1)], None, ADD).then_inc(s_hv, 1)
                    for b in range(2):
                        k = 2 * i + b
                        dve.wait_ge(s_hh, done + k + 1)
                        tt(dst_lo[:, k, :], tmp[b], dst_hi[:, k, :].bitcast(F32), SUB).then_inc(s_hl, 1)
                    dve.wait_ge(s_hl, done + 2 * i + 2)

            modulated(x_raw, T[3][:, :], [T[8 + b][:, :] for b in range(2)], mul_x, mod_x, 0, 0, h_hi, h_lo, SEQ)
            modulated(c_raw, T[7][:, 0:CTX], [T[8 + b][:, 0:CTX] for b in range(2)], mul_c, mod_c, 0, KT,
                      hc_hi, hc_lo, CTX)
            def ada_rows(g, k0):
                for e in range(2):
                    dve.wait_ge(ada1_used, 16 * g + k0 + e + 1)
                    dve.wait_ge(ada1_in[e], 16 * (8 * g + 1) + 8 * k0)
                    stt(acc1[:, :], ada1[e][:, :], silu_c[:, bass.ds(k0 + e, 1), 0], acc1[:, :], MUL, ADD
                        ).then_inc(ada1_used, 1)

            split_lo(0, 0)
            link(dve.memset(acc1[:, :], 0.0))
            with dve.Fori(0, 4) as i:
                for b in range(2):
                    split_lo(2 * i + b + 1, 1 - b)
                    ada_rows(0, 4 * i + 2 * b)
                    dve.wait_ge(w_used, 2 + 2 * i + b + 1)
                    dve.tensor_copy(u_ch[:, 2 * i + b, 0:CTX], ps[2 + b][:, 0:CTX]).then_inc(u_fd, 1)
            for part in range(3):
                dve.wait_ge(acc1_red, part + 1)
                link(dve.memset(acc1[:, :], 0.0))
                with chain.loop(0, 4, (4, 6, 4)[part]) as i:
                    for b in range(2):
                        c = 2 * i + b
                        t = 8 * part + c
                        split_lo(8 + t + 1, 1 - b)
                        ada_rows(part + 1, 4 * i + 2 * b)
                        dst = (uh[:, c, :], zx1[:, :], x0z[:, c, :])[part]
                        w = [vecs[:, bass.ds(V_CW + 24 * tap + t, 1)] for tap in range(3)]
                        src = ps[b]
                        dve.wait_ge(w_used, 2 + 8 + t + 1)
                        link(ts(dst, src[:, :], w[1], vecs[:, bass.ds(V_CB + t, 1)], MUL, ADD))
                        link(stt(dst[:, 1:SEQ], src[:, 0:SEQ - 1], w[0], dst[:, 1:SEQ], MUL, ADD))
                        ins = stt(dst[:, 0:SEQ - 1], src[:, 1:SEQ], w[2], dst[:, 0:SEQ - 1], MUL, ADD)
                        ins.then_inc(hy_free, 1)
                        if part == 1:
                            dve.wait_ge(hy_free, 2 + t + 1)
                            link(tt(uh[:, c, :], uh[:, c, :], zx1[:, :], MUL))

            def gate_units(g, last):
                dve.wait_ge(acc1_red, g + 4)
                link(dve.memset(acc1[:, :], 0.0))
                for j in range(8):
                    if not (last and j == 7):
                        split_lo(32 + 8 * g + j + 1, 1 - j % 2)
                    ada_rows(4 + g, 2 * j)

            with chain.loop(0, 3, 1) as g:
                gate_units(g, False)
            gate_units(3, True)
            dve.wait_ge(acc1_red, 8)
            link(tt(mod_x[:, N_ADA0:N_ADA], ps[7][:, 0:N_ADA - N_ADA0], vecs[:, V_BADA + N_ADA0:V_BADA + N_ADA], ADD))
            link(stt(mul_f[:, :], mod_x[:, 4 * KT:5 * KT], 1.0, vecs[:, V_NF:V_NF + KT], ADD, MUL))
            for b in range(2):
                dve.wait_ge(g_st[b], 16 * 17)
            dve.wait_ge(u_fa, 10)
            for q in range(4):
                for j in range(1, 4, 2):
                    ins = dve.tensor_copy(U4[32 * j:32 * j + 32, q::4, :], u_ch[32 * q:32 * q + 32, :, j::4])
            ins.then_inc(u4d, 1)
            dve.wait_ge(s_bneg, 1)
            dve.wait_ge(u4a, 4)
            dve.wait_ge(u4d, 1)
            dve.memset(bbar[:, :, :, :], 0.0)
            for t in (BL[0], BL[1]):
                ins = dve.memset(t[:, :, :, :], 0.0)
            link(ins)
            for d in range(2):
                cols = slice(NPAIR * d, NPAIR * d + NPAIR)
                f = [pow_b[:, ri, CH - 1 if d == 0 else 0, cols].unsqueeze(2).to_broadcast([P, NPAIR, GROUP])
                     for ri in range(2)]
                m = [s5b[:, cols, ri, :] for ri in range(2)]
                tt(bt[0][:, :, :], f[0], m[0], MUL)
                tt(bt[1][:, :, :], f[1], m[1], MUL)
                tt(bt[2][:, :, :], f[0], m[1], MUL)
                link(tt(bt[3][:, :, :], f[1], m[0], MUL))
                for g in range(2):
                    r = slice(64 * g, 64 * g + 64)
                    tt(bbar[r, cols, 0, 16 * g:16 * g + 16], bt[0][r, :, :], bt[1][r, :, :], SUB)
                    ins = tt(bbar[r, cols, 1, 16 * g:16 * g + 16], bt[2][r, :, :], bt[3][r, :, :], ADD)
                link(ins)
            dve.memset(CL[0][0][:, :, :, :], 0.0)
            dve.memset(CL[0][1][:, :, :, :], 0.0).then_inc(s_zero, 1)
            dve.wait_ge(s_zero, 1)

            def table(q, dst, pows, modes, n, tP, tQ, free, ready):
                tt(tP[:, :, 0:n, :], pows, modes, MUL)
                tt(tQ[:, 0, 0:n, :], pows[:, 0], modes[:, 1], MUL)
                link(tt(tQ[:, 1, 0:n, :], pows[:, 1], modes[:, 0], MUL))
                dve.wait_ge(*free)
                for ri, (src, op) in enumerate(((tP, SUB), (tQ, ADD))):
                    for g, out in enumerate(halves(dst, ri, 0, n)):
                        r = slice(64 * g, 64 * g + 64)
                        ins = tt(out, src[r, 0, 0:n, :], src[r, 1, 0:n, :], op)
                ins.then_inc(ready, 1)
                dve.wait_ge(ready, q + 1)

            with chain.loop(0, NPAIR, 1) as q:
                table(q, BL[0], pow_b[:, :, :, q].unsqueeze(3).to_broadcast([P, 2, CH, GROUP]),
                      s5b[:, q, :, :].unsqueeze(2).to_broadcast([P, 2, CH, GROUP]), CH, prod[0], prod[1],
                      (bl_tr, 2 * q + 1), bl_rd[0])
            dve.wait_ge(xs_ev, NDQ + 2)
            SCAN = 5
            with chain.loop(0, (NCH - 1) // SCAN, 3 * SCAN) as r:
                for step in range(SCAN):
                    s = SCAN * r + step + 1
                    link(tt(rec[:, :, :, :], X[:, s - 1, :, :].unsqueeze(1).to_broadcast([P, 2, 2, NDQ]),
                            lam8[:, :, :, :], MUL))
                    link(tt(X[:, s, :, :], X[:, s, :, :], rec[:, 0, :, :], ADD))
                    link(tt(X[:, s, :, :], X[:, s, :, :], rec[:, 1, ::-1, :], ADD))
            for d in range(2):
                ins = dve.memset(CL[1][d][:, :, :, :], 0.0)
            ins.then_inc(rec_dn, 1)
            dve.wait_ge(rec_dn, 1)

            def readout_matrix(q, par):
                table(q, CL[par][0], pow_c[:, :, :, q].unsqueeze(3).to_broadcast([P, 2, CH + 1, GROUP]),
                      s5c[:, q, :, :].unsqueeze(2).to_broadcast([P, 2, CH + 1, GROUP]), CH + 1, prod[0], prod[1],
                      (y_ps, q + 1), cl_rd[0])

            def toeplitz(q, par):
                dve.wait_ge(l_ps, q + 3)
                for a in range(2):
                    o7 = 32 * (CH - 1 - 4 * a - 3)
                    ins = dve.tensor_copy(TL[par][96:128, a, :, :].rearrange("p i h -> p (i h)"),
                                          ps[4 + 2 * par][96:128, o7:o7 + 256])
                ins.then_inc(tl_d, 1)

            def outputs(q, par):
                dve.wait_ge(y_ps, q + 3)
                yq = U4[:, q, CTX // 4:].rearrange("p (c a) -> p c a", a=2)
                src = ps[5 + 2 * par][:, 0:2 * NC_LAT].rearrange("p (a c) -> p c a", a=2)
                stt(yq, yq, vecs[:, bass.ds(V_D4 + q, 1)], src, MUL, ADD).then_inc(y_ev, 1)

            readout_matrix(0, 0)
            readout_matrix(1, 1)
            toeplitz(0, 0)
            with chain.loop(0, NPAIR // 2 - 1, 2) as i:
                for par in range(2):
                    q = 2 * i + par
                    toeplitz(q + 1, 1 - par)
                    outputs(q, par)
                    readout_matrix(q + 2, par)
            toeplitz(NPAIR - 1, 1)
            outputs(NPAIR - 2, 0)
            outputs(NPAIR - 1, 1)
            dve.wait_ge(y_ev, NPAIR + 2)
            for q in range(4):
                for j in range(1, 4, 2):
                    ins = dve.tensor_copy(y_ch[32 * q:32 * q + 32, :, j::4], U4[32 * j:32 * j + 32, q::4, CTX // 4:])
            ins.then_inc(ycd, 1)
            for g in range(2):
                dve.wait_ge(ygh, g + 1)
                tt(yg_lo[:, 4 * g:4 * g + 4, :], y_ch[:, 4 * g:4 * g + 4, :],
                   yg_hi[:, 4 * g:4 * g + 4, :].bitcast(F32), SUB).then_inc(ygl, 1)
            for s in range(4):
                dve.wait_ge(w_hi, U_TAB + s + 1)
                h, l = ((tf_hi, tf_lo), (tg_hi, tg_lo))[s // 2]
                tt(l[:, s % 2, :, :].rearrange("p a b -> p (a b)"), raw[s % 2][:, :],
                   h[:, s % 2, :, :].rearrange("p a b -> p (a b)").bitcast(F32), SUB).then_inc(w_lo, 1)

            def transposed_u(half):
                for t in range(4):
                    dve.wait_ge(ut_h, 4 * half + t + 1)
                    tt(uT_lo[:, t, :], ps[t % 2][:, :], uT_hi[:, t, :].bitcast(F32), SUB).then_inc(ut_l, 1)

            def spectrum(half):
                for f in range(4):
                    n = 4 * half + f
                    dve.wait_ge(pq_ps, n + 1)
                    dve.wait_ge(k_in[f % 2], 16 * (n // 2 + 1))
                    if half and f == 0:
                        dve.wait_ge(ol, 4)
                    A, B = (kfr[f % 2][:, s, :] for s in range(2))
                    pp, pq = (ps[2 + 2 * (f % 2) + s][:, :] for s in range(2))
                    tt(ct[0][:, :], A, pp, MUL)
                    link(tt(ct[1][:, :], B, pq, MUL))
                    link(tt(ct[2][:, :], ct[0][:, :], ct[1][:, :], SUB))
                    dve.sem_inc(yv, 1)
                    tt(ct[0][:, :], A, pq, MUL)
                    ins = tt(ct[1][:, :], B, pp, MUL)
                    ins.then_inc(pq_ev, 1)
                    dve.wait_ge(pq_ev, n + 1)
                    tt(ct[3][:, :], ct[0][:, :], ct[1][:, :], ADD).then_inc(yv, 1)
                    for c in range(2):
                        dve.wait_ge(yh, 8 * half + 2 * f + c + 1)
                        tt(Y_lo[:, c, f, :], ct[2 + c][:, :], Y_hi[:, c, f, :].bitcast(F32), SUB).then_inc(yl, 1)

            def conv_out(half):
                for c in range(4):
                    i = 4 * half + c
                    dve.wait_ge(cv_ps, i + 1)
                    stt(ct[0][:, :], uh[:, i, :], vecs[:, V_HB + i:V_HB + i + 1], ps[6 + i % 2][:, :],
                        MUL, ADD).then_inc(cv_free, 1)
                    dve.wait_ge(cv_free, i + 1)
                    tt(ct[1][:, :], ct[0][:, :], x0z[:, i, :], MUL).then_inc(ov, 1)
                    dve.wait_ge(oh, i + 1)
                    tt(hyo_lo[:, i, :], ct[1][:, :], hyo_hi[:, i, :].bitcast(F32), SUB).then_inc(ol, 1)

            transposed_u(0)
            spectrum(0)
            transposed_u(1)
            conv_out(0)
            spectrum(1)
            conv_out(1)
            split_lo(U_MRG, 0)
            with chain.loop(0, KT // 2, 4) as i:
                for mm in range(2):
                    m, n = 2 * i + mm, U_MRG + 4 * i + 2 * mm
                    split_lo(n + 1, 1, 1024)
                    dve.wait_ge(m_sg, m + 1)
                    link(tt(S1[mm][:, :], ps[3 * mm][:, :], S0[mm][:, :], MUL))
                    dve.wait_ge(gt_in[mm], 16 * (i + 1))
                    tt(S1[mm][:, :], S1[mm][:, :], gT[mm][:, 0, :], MUL)
                    split_lo(n + 2, 0)
                    dve.wait_ge(w_used, 2 + n + 2)
                    tt(S0[mm][:, :], ps[3 * mm + 2][:, :], gT[mm][:, 1, :], MUL).then_inc(m_free, 1)
                    dve.wait_ge(m_free, 2 + m + 1)
                    link(tt(S1[mm][:, :], S1[mm][:, :], S0[mm][:, :], ADD))
                    dve.sem_inc(m_sum, 1)
                    dve.wait_ge(m_hi, m + 1)
                    tt(mg_lo[:, m, :], S1[mm][:, :], mg_hi[:, m, :].bitcast(F32), SUB).then_inc(m_lo, 1)
            for g in range(4):
                dve.wait_ge(xa_in[g], 16)
            link(dve.memset(ct[0][:, :], 0.0))

            def add_square(m):
                link(tt(ct[1][:, :], xacc[:, m, :], xacc[:, m, :], MUL))
                link(tt(ct[0][:, :], ct[0][:, :], ct[1][:, :], ADD))

            with chain.loop(0, KT // 2, 6) as i:
                for b in range(2):
                    m = 2 * i + b
                    split_lo(U_OUT + m + 1, 1 - b)
                    dve.wait_ge(w_used, 2 + U_OUT + m + 1)
                    ins = stt(xacc[:, m, :], ps[6 + b][:, :], mod_x[:, bass.ds(2 * KT + m, 1)], xacc[:, m, :], MUL, ADD)
                    link(ins)
                    dve.sem_inc(o_free, 1)
                    add_square(m)
            dve.sem_inc(s_acc, 1)
            rstd(2, ps[4][:, :], ct[1][:, :], ct[2][:, :], ct[3][:, :], ct[0][:, :], SEQ)
            modulated(xacc, ct[0][:, :], [ct[1 + b][:, :] for b in range(2)], mul_f, mod_x, 3 * KT, 2 * KT,
                      h2_hi, h2_lo, SEQ)
            for q in range(4):
                n0, g0 = U_FFN + U_QUARTER * q, QTILES * q

                def pair(i, cols):
                    n = n0 + 2 * i
                    split_lo(n + 1, 1)
                    split_lo(n + 2, 0, cols)
                    dve.wait_ge(w_used, 2 + n + 2)
                    dve.wait_ge(fa_free, 1 + g0 + i + 1)
                    tt(f_t[:, :], f_s[:, :], ps[1][:, :], MUL).then_inc(ft_rd, 1)
                    dve.wait_ge(fh_rd, g0 + i + 1)
                    tt(a_lo[:, i, :], f_t[:, :], a_hi[:, i, :].bitcast(F32), SUB).then_inc(fl_rd, 1)
                    dve.wait_ge(fl_rd, g0 + i + 1)

                with dve.Fori(0, QTILES - 1) as i:
                    pair(i, UNIT)
                pair(QTILES - 1, UNIT2)
                n1 = n0 + 2 * QTILES
                if q == 3:
                    link(dve.memset(ct[0][:, :], 0.0))

                def down(m, b, cols):
                    if cols:
                        split_lo(n1 + m + 1, 1 - b, cols)
                    dve.wait_ge(w_used, 2 + n1 + m + 1)
                    ins = stt(xacc[:, m, :], ps[2 + b][:, :], mod_x[:, bass.ds(5 * KT + m, 1)], xacc[:, m, :], MUL, ADD)
                    link(ins)
                    dve.sem_inc(fd_free, 1)
                    if q == 3:
                        add_square(m)

                with chain.loop(0, KT // 2 - 1, 6 if q == 3 else 2) as i:
                    for b in range(2):
                        down(2 * i + b, b, UNIT2)
                down(KT - 2, 0, UNIT2)
                down(KT - 1, 1, UNIT if q < 3 else 0)
            dve.sem_inc(s_acc, 1)
            rstd(3, ps[4][:, :], ct[1][:, :], ct[2][:, :], ct[3][:, :], ct[0][:, :], SEQ)
            for m in range(KT):
                stt(xacc[:, m, :], xacc[:, m, :], vecs[:, V_NO + m:V_NO + m + 1], ct[0][:, :], MUL, MUL).then_inc(o_rd, 1)

        @block.tensor
        def _(pe):
            mm = pe.matmul

            def product(out, wh, wl, xh, xl, nk, first=True, last=True):
                for k in range(nk):
                    mm(out, wh(k), xh(k), start=first and k == 0, stop=False)
                    mm(out, wh(k), xl(k), start=False, stop=False)
                    ins = mm(out, wl(k), xh(k), start=False, stop=last and k == nk - 1)
                return ins

            def w_tile(t, k0=0):
                return lambda k: t[:, (k0 + k) * P:(k0 + k + 1) * P]

            def x_tile(t):
                return lambda k: t[:, k, :]

            pe.wait_ge(s_filt, 96)
            mm(ps[5][0:HID, :], f1w[:, :], feats[:, :], start=True, stop=True).then_inc(s_h1p, 1)
            pe.wait_ge(s_h1, 1)
            mm(ps[5][0:HID, :], f2w[:, :], fh[2][:, :], start=True, stop=True).then_inc(s_h1p, 1)
            pe.wait_ge(s_h1, 2)
            for t in range(4):
                pe.wait_ge(f3_free, t + 1)
                for c in range(4):
                    ins = mm(ps[c][:, :], fh[3][:, P * t:P * t + P], f3w[0:HID, 512 * c:512 * c + 512],
                             start=True, stop=True)
                ins.then_inc(f3_ps, 1)
            pe.wait_ge(s_cmod, 1)
            for k in range(2 * KT):
                pe.wait_ge(s_sq, k + 1)
                dst, w = (ps[4], SEQ) if k < KT else (ps[5], CTX)
                ins = mm(dst[:, 0:w], ones[:, :], sqr[k % 2][:, 0:w], start=k % KT == 0, stop=k % KT == KT - 1)
                ins.then_inc(s_squ, 1)
            pe.wait_ge(s_squ, 2 + 2 * KT)
            pe.sem_inc(s_ss, 2)
            pe.wait_ge(s_silu, 1)
            for st in range(8):
                for j in range(4):
                    n = 4 * st + j
                    pe.wait_ge(ada0_in[j], 16 * (st + 1))
                    for k in range(KT):
                        ins = mm(ps[6][:, 2 * n:2 * n + 2], ada0[j][:, k * P:k * P + P], silu_c[:, k, :],
                                 start=k == 0, stop=k == KT - 1)
                    ins.then_inc(ada0_used, 1)
                f, cs = st // 2, st % 2
                if st == 0:
                    pe.wait_ge(s_tabf, 32)
                    pe.wait_ge(s_tap, 4)
                if st >= 2:
                    pe.wait_ge(kf_free_a, st - 1)
                    pe.wait_ge(kf_free_d, st - 1)
                for half in range(2):
                    for t in range(4):
                        ins = mm(ps[2 * (st % 2) + half][:, :], tab_f[:, cs, t, P * f:P * f + P],
                                 (taps_s, taps_d)[cs][:, t, 512 * half:512 * half + 512], start=t == 0, stop=t == 3)
                ins.then_inc(kf_ps, 1)
            pe.wait_ge(ada0_used, 4 + N_ADA0)
            pe.sem_inc(ada0_ps, 1)

            def ada_columns(g):
                pe.wait_ge(ada1_used, 16 * (g + 1) + 1)
                for j in range(8):
                    ins = mm(ps[7][:, bass.ds(8 * g + j, 1)], acc1[:, P * j:P * j + P], ones[:, 0:1],
                             start=True, stop=True)
                ins.then_inc(acc1_red, 1)

            pe.wait_ge(kf_free_a, 8)
            pe.wait_ge(kf_free_d, 8)

            def u_unit(n, b, first):
                pe.wait_ge(w_lo, n + 1)
                pe.wait_ge(u_fa, n + 1)
                pe.wait_ge(u_fd, n + 1)
                for k in range(KT):
                    wh, wl = w_tile(hi[b])(k), w_tile(lo[b])(k)
                    for j, (w, xt, ct_) in enumerate(((wh, h_hi, hc_hi), (wh, h_lo, hc_lo), (wl, h_hi, hc_hi))):
                        s0, s1 = k == 0 and j == 0, k == KT - 1 and j == 2
                        mm(ps[b][:, :], w, xt[:, k, :], start=s0, stop=s1)
                        ins = mm(ps[2 + b][:, 0:CTX], w, ct_[:, k, :], start=s0, stop=s1)
                ins.then_inc(w_used, 1)

            pe.wait_ge(s_hl, 2 * KT)
            with pe.Fori(0, 4) as i:
                for b in range(2):
                    u_unit(2 * i + b, b, False)
            pe.wait_ge(u_fa, 10)

            def unit(n, b, free):
                pe.wait_ge(w_lo, n + 1)
                pe.wait_ge(*free)
                ins = product(ps[b][:, :], w_tile(hi[b]), w_tile(lo[b]), x_tile(h_hi), x_tile(h_lo), KT)
                ins.then_inc(w_used, 1)

            for part in range(3):
                ada_columns(part)
                with pe.Fori(0, 4) as i:
                    for b in range(2):
                        t = 8 * part + 2 * i + b
                        unit(8 + t, b, (hy_free, t + 1))
            pe.wait_ge(hy_free, 26)
            with pe.Fori(0, 4) as g:
                ada_columns(3 + g)
                for j in range(8):
                    unit(32 + 8 * g + j, j % 2, (g_free, 8 * g + j + 1))
            ada_columns(7)
            pe.wait_ge(g_free, 34)
            pe.wait_ge(u4a, 4)
            pe.wait_ge(u4d, 1)
            with pe.Fori(0, NPAIR) as q:
                for d in range(2):
                    pe.wait_ge(bl_rd[d], q + 1)
                    pe.wait_ge(mt_rd, 2 * q + d + 1)
                    for ri in range(2):
                        for a in range(2):
                            ins = pe.transpose(ps[d][:, (2 * ri + a) * P:(2 * ri + a + 1) * P],
                                               BL[d][:, ri, 4 * a:4 * a + 4, :].rearrange("p j h -> p (j h)"),
                                               ident[:, :])
                    ins.then_inc(bl_tr, 1)
                for d in range(2):
                    pe.wait_ge(mt_rd, 2 * q + d + 3)
                    pe.wait_ge(xs_ev, 2 * q + d + 1)
                    for ri in range(2):
                        for a in range(2):
                            ins = mm(ps[2 + d][:, NCH * ri:NCH * ri + NCH], MT[d][:, 2 * ri + a, :],
                                     U4[:, q, a::2], start=a == 0, stop=a == 1)
                    ins.then_inc(xs_ps, 1)
            pe.wait_ge(rec_dn, 1)

            def taps(q, par):
                for d in range(2):
                    pe.wait_ge(cl_rd[d], q + 1)
                pe.wait_ge(bb_rd, q + 1)
                pe.wait_ge(tl_a, q + 1)
                pe.wait_ge(tl_d, q + 1)
                jobs = [(1, 0, 256, 1), (0, 224, 256, 0), (0, 256, 480, 1)]
                for n, (d, c0, c1, i0) in enumerate(jobs):
                    for ri in range(2):
                        rhs = CL[par][d][:, ri, i0:i0 + (c1 - c0) // 32, :].rearrange("p m h -> p (m h)")
                        ins = mm(ps[4 + 2 * par][:, c0:c1], BB[par][d][:, ri, :, :].rearrange("p a b -> p (a b)"),
                                 rhs, start=n == 0 and ri == 0, stop=ri == 1 and n == 2, skip_group_check=True)
                ins.then_inc(l_ps, 1)

            def chunk_outputs(q, par):
                pe.wait_ge(tl_a, q + 3)
                pe.wait_ge(tl_d, q + 3)
                pe.wait_ge(y_ev, q + 1)
                C = CL[par]
                for a in range(2):
                    out = ps[5 + 2 * par][:, NC_LAT * a:NC_LAT * a + NC_LAT]
                    for ri in range(2):
                        mm(out, C[0][:, ri, 4 * a + 1:4 * a + 5, :].rearrange("p m h -> p (m h)"),
                           X[:, NC_CTX - 1:NCH - 1, ri, q], start=ri == 0, stop=False)
                        mm(out, C[1][:, ri, 4 * a:4 * a + 4, :].rearrange("p m h -> p (m h)"),
                           XR[par][:, ri, :], start=False, stop=False)
                    for ai in range(2):
                        ins = mm(out, TL[par][:, ai, 4 * a:4 * a + 4, :].rearrange("p m h -> p (m h)"),
                                 U4[:, q, CTX // 4 + ai::2], start=False, stop=ai == 1)
                ins.then_inc(y_ps, 1)

            taps(0, 0)
            with pe.Fori(0, NPAIR // 2 - 1) as i:
                for par in range(2):
                    q = 2 * i + par
                    taps(q + 1, 1 - par)
                    chunk_outputs(q, par)
            taps(NPAIR - 1, 1)
            chunk_outputs(NPAIR - 2, 0)
            chunk_outputs(NPAIR - 1, 1)
            def transpose_u(half):
                for t in range(4):
                    n = 4 * half + t
                    if n >= 2:
                        pe.wait_ge(ut_l, n - 1)
                    for c in range(4):
                        ins = pe.transpose(ps[t % 2][:, P * c:P * c + P], uh[:, 4 * half + c, P * t:P * t + P], ident[:, :])
                    ins.then_inc(ut_ps, 1)

            def spectrum(half):
                for f in range(4):
                    n = 4 * half + f
                    if n >= 2:
                        pe.wait_ge(pq_ev, n - 1)
                    for s in range(2):
                        ins = product(ps[2 + 2 * (f % 2) + s][:, :], lambda t: tf_hi[:, s, t, P * f:P * f + P],
                                      lambda t: tf_lo[:, s, t, P * f:P * f + P], x_tile(uT_hi), x_tile(uT_lo), 4)
                    ins.then_inc(pq_ps, 1)

            def inverse(half):
                for c in range(4):
                    i = 4 * half + c
                    if i >= 2:
                        pe.wait_ge(cv_free, i - 1)
                    pe.wait_ge(yl, 8 * half + 8)
                    for s in range(2):
                        ins = product(ps[6 + i % 2][:, :], lambda f: Y_hi[:, s, f, P * c:P * c + P],
                                      lambda f: Y_lo[:, s, f, P * c:P * c + P], lambda f: tg_hi[:, s, f, :],
                                      lambda f: tg_lo[:, s, f, :], 4, first=s == 0, last=s == 1)
                    ins.then_inc(cv_ps, 1)

            transpose_u(0)
            pe.wait_ge(w_lo, U_TAB + 2)
            pe.wait_ge(ut_l, 4)
            spectrum(0)
            transpose_u(1)
            pe.wait_ge(w_lo, U_TAB + 4)
            inverse(0)
            pe.wait_ge(ut_l, 8)
            spectrum(1)
            inverse(1)
            pe.wait_ge(cv_ps, 8)
            pe.sem_inc(w_used, 4)
            pe.wait_ge(ygl, 2)
            pe.wait_ge(ol, 8)
            with pe.Fori(0, KT // 2) as i:
                for b in range(2):
                    m, n = 2 * i + b, U_MRG + 4 * i + 2 * b
                    pe.wait_ge(w_lo, n + 1)
                    pe.wait_ge(m_free, m + 1)
                    product(ps[3 * b][:, :], w_tile(hi[0]), w_tile(lo[0]), x_tile(yg_hi), x_tile(yg_lo), ST)
                    ins = product(ps[3 * b + 1][:, :], w_tile(hi[0], ST), w_tile(lo[0], ST), x_tile(yg_hi), x_tile(yg_lo), ST)
                    ins.then_inc(w_used, 1)
                    pe.wait_ge(w_lo, n + 2)
                    ins = product(ps[3 * b + 2][:, :], w_tile(hi[1]), w_tile(lo[1]), x_tile(hyo_hi), x_tile(hyo_lo), ST)
                    ins.then_inc(w_used, 1)
            pe.wait_ge(m_lo, KT)
            with pe.Fori(0, KT // 2) as i:
                for b in range(2):
                    m = 2 * i + b
                    pe.wait_ge(w_lo, U_OUT + m + 1)
                    pe.wait_ge(o_free, m + 1)
                    ins = product(ps[6 + b][:, :], w_tile(hi[b]), w_tile(lo[b]), x_tile(mg_hi), x_tile(mg_lo), KT)
                    ins.then_inc(w_used, 1)
            pe.wait_ge(s_acc, 1)
            mm(ps[4][:, :], ones[:, :], ct[0][:, :], start=True, stop=True).then_inc(s_ss, 1)
            pe.wait_ge(s_hl, 3 * KT)
            for q in range(4):
                n0, g0 = U_FFN + U_QUARTER * q, QTILES * q
                with pe.Fori(0, QTILES) as i:
                    for b, free in enumerate((fa_free, ft_rd)):
                        n = n0 + 2 * i + b
                        pe.wait_ge(w_lo, n + 1)
                        pe.wait_ge(free, g0 + i + 1)
                        ins = product(ps[b][:, :], w_tile(hi[b]), w_tile(lo[b]), x_tile(h2_hi), x_tile(h2_lo), KT)
                        ins.then_inc(w_used, 1)
                n1 = n0 + 2 * QTILES
                pe.wait_ge(fl_rd, g0 + QTILES)
                with pe.Fori(0, KT // 2) as i:
                    for b in range(2):
                        m = 2 * i + b
                        pe.wait_ge(w_lo, n1 + m + 1)
                        pe.wait_ge(fd_free, KT * q + m + 1)
                        ins = product(ps[2 + b][:, :], w_tile(hi[b]), w_tile(lo[b]), x_tile(a_hi), x_tile(a_lo), QTILES)
                        ins.then_inc(w_used, 1)
            pe.wait_ge(s_acc, 2)
            mm(ps[4][:, :], ones[:, :], ct[0][:, :], start=True, stop=True).then_inc(s_ss, 1)


def tables():
    f32 = np.float32
    quarter = D // 4
    omega = (f32(10000.0) ** (-np.arange(quarter, dtype=f32) / f32(quarter))).astype(f32)
    rows = (np.arange(SEQ // GRID, dtype=f32)[None, :] * omega[:, None]).astype(f32)
    cols = (np.arange(GRID, dtype=f32)[None, :] * omega[:, None]).astype(f32)
    pos_r = np.concatenate([np.sin(rows), np.cos(rows)]).reshape(8, P, SEQ // GRID)
    pos_c = np.concatenate([np.sin(cols), np.cos(cols)]).reshape(8, P, GRID)
    postab = np.ascontiguousarray(np.concatenate([pos_r, pos_c], axis=2).transpose(1, 0, 2)).astype(f32)
    pos = np.arange(SEQ, dtype=f32)
    t = (pos / f32(SEQ - 1)).astype(f32)
    w = (f32(2.0 * math.pi) * pos / f32(SEQ)).astype(f32)
    bands = np.linspace(1e-4, BANDS - 1, BANDS).astype(f32)
    ang = (w[:, None] * bands).astype(f32)
    feats = np.concatenate([t[:, None], np.cos(ang), -np.sin(ang)], axis=1).astype(f32)
    negt = np.ascontiguousarray((-t).reshape(4, P).T)
    theta = np.pi * (2 * np.arange(SEQ) + 1)[:, None] * np.arange(SEQ)[None, :] / (2 * SEQ)
    cos, sin = np.cos(theta), np.sin(theta)

    def tiled(m):
        return m.reshape(4, P, SEQ).transpose(1, 0, 2).reshape(P, 4 * SEQ)

    tabs = np.stack([tiled(cos.T), tiled(sin.T), tiled(cos / SEQ), tiled(sin / SEQ)]).astype(f32)
    return postab, np.ascontiguousarray(feats.T), negt, tabs, np.eye(P, dtype=f32)


def kernel(**inputs):
    import concourse.bacc as bacc
    from concourse.bass_utils import run_bass_kernel_spmd

    a = {k: np.asarray(v) for k, v in inputs.items()}
    postab, feats, negt, tabs, ident = tables()
    cont = np.ascontiguousarray

    def units(w):
        r, c = w.shape
        return cont(w.reshape(r // P, P, c // P, P).transpose(2, 1, 0, 3).reshape(c // P, P, r))

    def by_channel(v):
        return v.reshape(-1, P).T

    w_in = units(a["w_in"][0])
    hy = [8 * part + 8 + i for part in (1, 2, 0) for i in range(ST)]
    w_in = cont(w_in[list(range(8)) + hy + list(range(32, 64))])
    conv = a["hy_conv_w"][0].reshape(3, 24, P)[:, [h - 8 for h in hy]]
    conv_b = a["hy_conv_b"][0].reshape(24, P)[[h - 8 for h in hy]]
    glu = units(a["w_glu"][0])
    w_glu = cont(np.concatenate([glu[:KT], glu[KT:]], axis=2))
    fi = units(a["w_ffn_in"][0])
    w_fi = cont(np.stack([fi[:DFF // P], fi[DFF // P:]], axis=1).reshape(2 * DFF // P, P, UNIT))
    fo = a["w_ffn_out"][0].reshape(4, QTILES, P, KT, P)
    w_fo = cont(fo.transpose(0, 3, 2, 1, 4).reshape(4 * KT, P, UNIT2))
    d4 = np.tile(a["s5_d"][0].reshape(NPAIR, 32).T, (4, 1))
    vecs = cont(np.concatenate([
        by_channel(a["norm_mix"][0]), by_channel(a["norm_ffn"][0]), by_channel(a["norm_f"]),
        by_channel(a["c"][0]), by_channel(a["c_ctx"]), by_channel(a["b_ada"][0]),
        conv.reshape(72, P).T, conv_b.T, by_channel(a["hy_bias"][0]), d4, negt], axis=1))

    def poles(v):
        return v.reshape(2, NPAIR, 2, STATE).transpose(2, 3, 0, 1).reshape(P, NDQ)

    log_dt = np.broadcast_to(a["s5_log_dt"][0][:, :, None], (2, 2 * NPAIR, STATE))
    s5a = cont(np.stack([poles(a["s5_a_re"][0]), poles(a["s5_a_im"][0]), poles(log_dt)], axis=1))

    def modes(re, im, perm):
        v = np.stack([re, im]).transpose(perm)
        v = v.reshape(2, 2, NPAIR, 2, STATE, GROUP).transpose(3, 4, 1, 2, 0, 5)
        return cont(v.reshape(P, NDQ, 2, GROUP))

    w_ar = cont(a["w_ada"][0][:, N_ADA0 * P:].reshape(KT, P, 8, 1024).transpose(2, 0, 1, 3).reshape(8 * KT, P, 1024))
    data = {
        "vecs": vecs, "w_ada": units(a["w_ada"][0][:, :N_ADA0 * P]), "w_ar": w_ar, "w_in": w_in, "w_glu": w_glu,
        "w_hy": units(a["w_hy_out"][0]), "w_out": units(a["w_out"][0]), "w_fi": w_fi, "w_fo": w_fo,
        "x": cont(a["x"][0].T.reshape(KT, P, SEQ).transpose(1, 0, 2)),
        "ctx": cont(a["ctx"][0].T.reshape(KT, P, CTX).transpose(1, 0, 2)),
        "s5a": s5a, "s5b": modes(a["s5_b_re"][0], a["s5_b_im"][0], (0, 1, 2, 3, 4)),
        "s5c": modes(a["s5_c_re"][0], a["s5_c_im"][0], (0, 1, 2, 4, 3)),
        "f1w": cont(a["hy_f1_w"][0]), "f2w": cont(a["hy_f2_w"][0]), "f3w": cont(a["hy_f3_w"][0]),
        "fpar": cont(np.stack([a["hy_f1_b"][0], a["hy_f1_freq"][0], a["hy_f2_b"][0], a["hy_f2_freq"][0]], axis=1)),
        "decay": cont(a["hy_decay"][0].reshape(1, 2 * HYW)),
        "feats": feats, "postab": postab, "tabs": tabs, "ident": ident,
    }
    nc = bacc.Bacc("TRN2", target_bir_lowering=False, num_devices=1)
    arrays, args = {}, []
    for name, v in data.items():
        arrays[f"in_{name}"] = v
        args.append(nc.dram_tensor(f"in_{name}", v.shape, F32, kind="ExternalInput").ap())
    args.append(nc.dram_tensor("out", (KT, P, SEQ), F32, kind="ExternalOutput").ap())
    args.append(nc.dram_tensor("xp", (P, KT, SEQ), F32, kind="Internal").ap())
    args.append(nc.dram_tensor("gates", (2 * KT, P, SEQ), F32, kind="Internal").ap())
    args.append(nc.dram_tensor("kf", (4, 2, P, HYW), F32, kind="Internal").ap())
    block_kernel(nc, *args)
    got = run_bass_kernel_spmd(nc, [arrays], core_ids=[0]).results[0]["out"]
    return got.reshape(D, SEQ).T.reshape(1, SEQ, D)
```

```python
import math
from contextlib import contextmanager

import numpy as np

import concourse.bass as bass
from concourse import mybir

P = 128
D = 2048
SEQ = 512
CTX = 256
GRID = 64
S5W = 1024
HYW = 1024
STATE = 64
GROUP = 16
HID = 64
BANDS = 16
POSD = 1 + 2 * BANDS
DFF = 5632
EPS = 1e-6

KT = D // P
ST = S5W // P
NPAIR = S5W // 32
NDQ = 2 * NPAIR
CH = 8
NC_CTX = CTX // CH
NC_LAT = SEQ // CH
NCH = NC_CTX + NC_LAT
SCAN = 5
UNIT = KT * P
QTILES = DFF // P // 4
UNIT2 = QTILES * P
N_ADA = 96
N_ADA0 = 32

U_IN = 0
U_TAB = 64
U_MRG = 68
U_OUT = 100
U_FFN = 116
U_QUARTER = 2 * QTILES + KT

V_NM, V_NF, V_NO, V_C, V_CC, V_BADA = 0, 16, 32, 48, 64, 80
V_CW, V_CB, V_HB, V_D4, V_NEGT, NVEC = 176, 248, 272, 280, 312, 316

F32 = mybir.dt.float32
F32R = mybir.dt.float32r
ALU = mybir.AluOpType
ACT = mybir.ActivationFunctionType
MUL, ADD, SUB = ALU.mult, ALU.add, ALU.subtract

MAGIC = 12582912.0
TWO_PI_1 = 6.28125
TWO_PI_2 = float(np.float32(np.round((2 * math.pi - TWO_PI_1) * 2.0 ** 20) / 2.0 ** 20))
TWO_PI_3 = float(np.float32(2 * math.pi - TWO_PI_1 - TWO_PI_2))
PI_SAFE = 3.1415925


class Chain:

    def __init__(self, eng, sem):
        self.eng, self.sem, self.base, self.k = eng, sem, 0, 0

    def mark(self, ins):
        ins.then_inc(self.sem, 1)
        self.k += 1

    def wait(self):
        self.eng.wait_ge(self.sem, self.base + self.k)

    def link(self, ins):
        self.mark(ins)
        self.wait()

    @contextmanager
    def loop(self, lo, hi, marks):
        start = self.base + self.k
        with self.eng.Fori(lo, hi) as i:
            self.base, self.k = start + (i - lo) * marks, 0
            yield i
            assert self.k == marks, (self.k, marks)
        self.base, self.k = start + (hi - lo) * marks, 0


def block_kernel(nc, vecs_d, w_as_d, w_am_d, w_ar_d, w_in_d, w_glu_d, w_hy_d, w_out_d, w_fi_d, w_fo_d, x_d, ctx_d,
                 s5a_d, s5b_d, s5c_d, f1w_d, f2w_d, f3w_d, fpar_d, decay_d, feats_d, postab_d,
                 tabs_d, ident_d, out_d, xp_d, gates_d, kf_d):
    kb = 1024
    base = (nc.sbuf_base + 63) // 64 * 64

    def at(name, off_kb, shape, dt=F32):
        return nc.alloc_sbuf_tensor_at(name, shape, dt, offset=base + int(off_kb * kb))

    raw = [at("w_raw0", 0, [P, UNIT]), at("w_raw1", 8, [P, UNIT])]
    hi = [at("w_hi0", 16, [P, UNIT], F32R), at("w_hi1", 32, [P, UNIT], F32R)]
    lo = [at("w_lo0", 24, [P, UNIT], F32R), at("w_lo1", 40, [P, UNIT], F32R)]
    small = 48
    vecs = at("vecs", small, [P, NVEC])
    o = small + 320 * 4 / kb
    silu_c = at("silu_c", o, [P, KT, 2]); o += 32 * 4 / kb
    mod_x = at("mod_x", o, [P, N_ADA]); o += N_ADA * 4 / kb
    mod_c = at("mod_c", o, [P, N_ADA0]); o += N_ADA0 * 4 / kb
    mul_x = at("mul_x", o, [P, KT]); o += KT * 4 / kb
    mul_c = at("mul_c", o, [P, KT]); o += KT * 4 / kb
    mul_f = at("mul_f", o, [P, KT]); o += 2 * KT * 4 / kb
    ident = at("ident", o, [P, P]); o += P * 4 / kb
    ones = at("ones", o, [P, P]); o += P * 4 / kb
    pow_at = o
    pow_c = at("pow_c", o, [P, 2, CH + 1, NDQ]); o += 2 * (CH + 1) * NDQ * 4 / kb
    pow_b = at("pow_b", o, [P, 2, CH, NDQ]); o += 2 * CH * NDQ * 4 / kb
    lam8 = at("lam8", o, [P, 2, 2, NDQ]); o += 4 * NDQ * 4 / kb
    assert o <= 62, o
    tab_f = at("tab_f", 62, [P, 2, 4, 512])
    taps_s = at("taps_sum", 78, [P, 4, HYW])
    x_raw = at("x_raw", 94, [P, KT, SEQ])
    taps_d = at("taps_dif", 126, [P, 4, HYW])
    decay = at("decay", 142, [P, 2 * HYW])
    f3w = at("f3w", 150, [P, 2 * HYW])
    c_raw = at("c_raw", 158, [P, KT, CTX])
    ada_s = [at(f"ada_shift{j}", 174 + 4 * j, [P, 1024]) for j in range(4)]
    ada_m = [at(f"ada_scale{j}", 190 + 8 * j, [P, UNIT]) for j in range(2)]
    acc_s = [at(f"acc_shift{a}", 24 * a, [P, 2, 1024]) for a in range(2)]
    sqr = [at(f"sqr{j}", 8 + 2 * j, [P, 512]) for j in range(2)]
    postab = at("postab", 12, [P, 8, 8 + GRID])
    rs_c = at("rstd_ctx", 12, [P, CTX])
    T = [at(f"tmp{j}", 16 + 2 * j, [P, 512]) for j in range(16)]
    row_m = at("row_scale", 32, [P, D])
    h_hi = at("h_hi", 62, [P, KT, SEQ], F32R)
    h_lo = at("h_lo", 94, [P, KT, SEQ], F32R)
    hc_hi = at("hc_hi", 126, [P, KT, CTX], F32R)
    hc_lo = at("hc_lo", 142, [P, KT, CTX], F32R)
    gst = [at(f"gate_st{j}", 158 + 2 * j, [P, SEQ]) for j in range(2)]
    zx1 = at("zx1", 162, [P, SEQ])
    ada1 = [at(f"ada1_{j}", 166 + 4 * j, [P, 1024]) for j in range(2)]
    acc1 = at("acc1", 174, [P, 1024])
    u_ch = at("u_ch", 182, [P, ST, CTX + SEQ])
    uh = at("uh", 126, [P, ST, SEQ])
    x0z = at("x0z", 142, [P, ST, SEQ])
    X = at("states", 62, [P, NCH, 2, NDQ])
    s5b = at("s5b", 110, [P, NDQ, 2, GROUP])
    s5c = at("s5c", 118, [P, NDQ, 2, GROUP])
    U4 = at("u4", 158, [P, NPAIR, (CTX + SEQ) // 4])
    bbar = at("bbar", 182, [P, NDQ, 2, 32])
    BL = [at(f"b_lam{d}", 16 + 2 * d, [P, 2, CH, 32]) for d in range(2)]
    MT = [at(f"m_in{d}", 20 + 2 * d, [P, 4, P]) for d in range(2)]
    prod = [at(f"prod{j}", 24 + 1.25 * j, [P, 2, CH + 1, GROUP]) for j in range(4)]
    CL = [[at(f"c_lam{j}{d}", (30, 16, 198, 110)[j] + 2.5 * d, [P, 2, CH + 1, 32]) for d in range(2)] for j in range(4)]
    BB = [[at(f"b_rep{j}{d}", (35, 37, 115, 46)[j] + d, [P, 2, 4, 32]) for d in range(2)] for j in range(4)]
    TL = [at(f"toeplitz{par}", 39 + 2 * par, [P, 2, CH, 32]) for par in range(2)]
    rec = at("rec", 44, [P, 2, 2, NDQ])
    XR = [at(f"states_back{j}", (43, 43.5, 45, 45.5)[j], [P, 2, NC_LAT]) for j in range(4)]
    bt = [at(f"bt{j}", 24 + 2 * j, [P, NPAIR, GROUP]) for j in range(4)]
    y_ch = at("y_ch", 94, [P, ST, SEQ])
    yg_hi = at("yg_hi", 62, [P, ST, SEQ], F32R)
    yg_lo = at("yg_lo", 78, [P, ST, SEQ], F32R)
    uT_hi = at("uT_hi", 94, [P, 4, 512], F32R)
    uT_lo = at("uT_lo", 102, [P, 4, 512], F32R)
    tf_hi = at("tf_hi", 158, [P, 2, 4, 512], F32R)
    tf_lo = at("tf_lo", 174, [P, 2, 4, 512], F32R)
    tg_hi = at("tg_hi", 110, [P, 2, 4, 512], F32R)
    tg_lo = at("tg_lo", 190, [P, 2, 4, 512], F32R)
    Y_hi = at("Y_hi", 16, [P, 2, 4, 512], F32R)
    Y_lo = at("Y_lo", 32, [P, 2, 4, 512], F32R)
    kfr = [at(f"kf_in{j}", 8 + 4 * j, [P, 2, 512]) for j in range(2)]
    ct = [at(f"ct{j}", pow_at + 2 * j, [P, 512]) for j in range(4)]
    hyo_hi = at("hyo_hi", 126, [P, ST, SEQ], F32R)
    hyo_lo = at("hyo_lo", 142, [P, ST, SEQ], F32R)
    mg_hi = at("mg_hi", 94, [P, KT, SEQ], F32R)
    mg_lo = at("mg_lo", 158, [P, KT, SEQ], F32R)
    gT = [at(f"gates{j}", 190 + 4 * j, [P, 2, SEQ]) for j in range(2)]
    S0 = [at(f"mrg_a{j}", 198 + 2 * j, [P, SEQ]) for j in range(2)]
    S1 = [at(f"mrg_b{j}", 202 + 2 * j, [P, SEQ]) for j in range(2)]
    xacc = at("xacc", 126, [P, KT, SEQ])
    h2_hi = at("h2_hi", 62, [P, KT, SEQ], F32R)
    h2_lo = at("h2_lo", 94, [P, KT, SEQ], F32R)
    a_hi = at("act_hi", 158, [P, QTILES, SEQ], F32R)
    a_lo = at("act_lo", 180, [P, QTILES, SEQ], F32R)
    f_s = at("ffn_silu", 202, [P, SEQ])
    f_t = at("ffn_prod", 204, [P, SEQ])

    ps = [nc.alloc_psum_tensor(f"ps{j}", [P, 512], F32) for j in range(8)]

    fh = [at(f"fh{j}", 16 + 2 * j, [HID, SEQ]) for j in range(4)]
    lt = at("lam_tmp", 32.75, [P, 13, NDQ])
    lam_rr, lam_ii = (at(n, 46.5 + 0.5 * j, [P, 2, NDQ]) for j, n in enumerate(("lam_rr", "lam_ii")))
    s5a = at("s5a", 32, [P, 3, NDQ])
    feats = at("feats", 36, [POSD, SEQ])
    f1w = at("f1w", 38, [POSD, HID])
    f2w = at("f2w", 38.5, [HID, HID])
    fpar = at("fpar", 39, [HID, 4])
    pwt = at("pow_b_tmp", 39.5, [P, 2, CH, NPAIR])
    pw = at("pow_tmp", 42, [P, 2, CH + 1, NDQ])

    def sem(name):
        return nc.alloc_semaphore(name)

    s_vec, s_par, s_filt, s_tabf, s_x, s_ctx = (sem(n) for n in
        ("vec_loaded", "s5a_loaded", "filter_loaded", "tabf_loaded", "x_loaded", "ctx_loaded"))
    s_pos = sem("postab_loaded")
    as_in = [sem(f"ada_shift_loaded{j}") for j in range(4)]
    am_in = [sem(f"ada_scale_loaded{j}") for j in range(2)]
    as_used, am_used, ada1_used = sem("ada_shift_used"), sem("ada_scale_used"), sem("ada1_used")
    as_red, am_row, am_ps = sem("shift_reduced"), sem("scale_rows_ready"), sem("scale_psum")
    s_xn = sem("x_normed")
    s_rs, c_mod, cv_, ch_, cl_ = (sem(n) for n in
        ("ctx_rstd_ready", "mod_coef_ready", "hc_ready", "hc_hi_ready", "hc_lo_ready"))
    ada1_in = [sem(f"ada1_loaded{j}") for j in range(2)]
    w_in = [sem(f"w_loaded{j}") for j in range(2)]
    w_hi, w_lo, w_used = sem("w_hi_ready"), sem("w_lo_ready"), sem("w_used")
    dch, ach, pch = sem("dve_chain"), sem("act_chain"), sem("pool_chain")
    s_silu = sem("silu_c_ready")
    acc1_red = sem("ada1_acc_reduced")
    s_h1p, s_h1a, s_h1 = sem("filter_psum"), sem("filter_arg"), sem("filter_sin")
    f3_ps, f3_free, s_win, s_tap = sem("f3_psum"), sem("f3_free"), sem("window_ready"), sem("taps_ready")
    s_absd = sem("decay_abs")
    kf_ps, kf_free = sem("kf_psum"), sem("kf_evac")
    kf_out = [sem(f"kf_stored{j}") for j in range(2)]
    lam_z, lam_s = sem("lam_arg"), sem("lam_sin")
    s_xp, s_xpo, s_sq, s_squ = sem("xp_ready"), sem("xp_stored"), sem("square_ready"), sem("square_used")
    s_var, s_sqrt = sem("var_ready"), sem("sqrt_ready")
    s_ss = sem("sumsq_psum")
    s_cmod, s_hv, s_hh, s_hl = sem("const_ready"), sem("h_ready"), sem("h_hi_ready"), sem("h_lo_ready")
    u_fa, u_fd = sem("u_evac_act"), sem("u_evac_dve")
    hy_free = sem("hy_free")
    g_free = sem("gate_free")
    g_st = [sem(f"gate_stored{j}") for j in range(2)]
    s_bc = sem("s5bc_loaded")
    u4a, u4d = sem("u4_act"), sem("u4_dve")
    bl_rd = [sem(f"blam_ready{d}") for d in range(2)]
    cl_rd = [sem(f"clam_ready{d}") for d in range(2)]
    bl_tr, mt_rd, xs_ps, xs_ev = (sem(n) for n in ("blam_transposed", "m_in_ready", "x_psum", "x_stored"))
    rec_dn = sem("scan_done")
    s_bneg, s_zero = sem("s5b_conjugated"), sem("s5_tables_cleared")
    bb_rd, l_ps, tl_a, tl_d, y_ps, y_ev = (sem(n) for n in
        ("brep_ready", "taps_psum", "toepl_act", "toepl_dve", "y_psum", "y_stored"))
    ych, ycd, gel, ygh, ygl = (sem(n) for n in ("ych_act", "ych_dve", "gelu_ready", "yg_hi_ready", "yg_lo_ready"))
    ut_ps, ut_h, ut_l = sem("uT_psum"), sem("uT_hi_ready"), sem("uT_lo_ready")
    pq_ps, pq_ev, k_in = sem("spec_psum"), sem("spec_free"), [sem(f"kf_in{j}") for j in range(2)]
    yv, yh, yl = sem("Y_ready"), sem("Y_hi_ready"), sem("Y_lo_ready")
    cv_ps, cv_free, ov, oh, ol = (sem(n) for n in ("conv_psum", "conv_free", "hyo_ready", "hyo_hi_ready", "hyo_lo_ready"))
    gt_in = [sem(f"gates_loaded{j}") for j in range(2)]
    m_sg, m_free, m_sum, m_hi, m_lo = (sem(n) for n in
        ("glu_sigmoid", "merge_free", "merged_ready", "merged_hi_ready", "merged_lo_ready"))
    xa_in = [sem(f"xacc_loaded{j}") for j in range(4)]
    o_free = sem("out_free")
    s_acc = sem("acc_ready")
    s_hm = sem("h_scaled")
    fa_free, ft_rd, fh_rd, fl_rd = (sem(n) for n in
        ("ffn_a_free", "ffn_prod_ready", "ffn_hi_ready", "ffn_lo_ready"))
    fd_free = sem("ffn_out_free")
    o_rd, s_out = sem("out_ready"), sem("out_stored")

    def halves(tensor, ri, idx0, idx1):
        return [tensor[64 * g:64 * g + 64, ri, idx0:idx1, 16 * g:16 * g + 16] for g in range(2)]

    gates_v = gates_d.rearrange("(g m) p t -> g m p t", g=2)

    with nc.Block() as block:
        @block.sync
        def _(sp):
            sp.dma_start(vecs[:, :], vecs_d).then_inc(s_vec, 16)
            sp.dma_start(ident[:, :], ident_d).then_inc(s_vec, 16)
            sp.dma_start(s5a[:, :, :], s5a_d).then_inc(s_par, 16)
            sp.dma_start(feats[:, :], feats_d).then_inc(s_filt, 16)
            sp.dma_start(f1w[:, :], f1w_d).then_inc(s_filt, 16)
            sp.dma_start(f2w[:, :], f2w_d).then_inc(s_filt, 16)
            sp.dma_start(fpar[:, :], fpar_d).then_inc(s_filt, 16)
            sp.dma_start(f3w[0:HID, :], f3w_d).then_inc(s_filt, 16)
            sp.dma_start(decay[:, :], decay_d.to_broadcast([P, 2 * HYW])).then_inc(s_filt, 16)
            for s in range(2):
                sp.dma_start(tab_f[:, s, :, :], tabs_d[s].rearrange("p (t k) -> p t k", t=4)).then_inc(s_tabf, 16)
            with sp.Fori(0, 8) as i:
                for b in range(2):
                    sp.wait_ge(am_used, 2 * i + b + 1)
                    sp.dma_start(ada_m[b][:, :], w_am_d[2 * i + b]).then_inc(am_in[b], 16)
            with sp.Fori(0, 8) as i:
                for j in range(4):
                    sp.wait_ge(as_used, 4 * i + j + 1)
                    sp.dma_start(ada_s[j][:, :], w_as_d[4 * i + j]).then_inc(as_in[j], 16)
            sp.wait_ge(as_red, 1)
            sp.dma_start(raw[0][:, :], w_in_d[0]).then_inc(w_in[0], 16)
            sp.wait_ge(cv_, 1)
            sp.dma_start(raw[1][:, :], w_in_d[1]).then_inc(w_in[1], 16)
            with sp.Fori(1, 32) as i:
                for b in range(2):
                    sp.wait_ge(w_lo, 2 * i + b - 1)
                    sp.dma_start(raw[b][:, :], w_in_d[2 * i + b]).then_inc(w_in[b], 16)
            for s in range(4):
                sp.wait_ge(w_lo, U_TAB + s - 1)
                sp.dma_start(raw[s % 2][:, :], tabs_d[s]).then_inc(w_in[s % 2], 16)
            sp.wait_ge(w_lo, U_MRG)
            sp.dma_start(raw[0][:, :], w_glu_d[0]).then_inc(w_in[0], 16)
            for half in range(2):
                for f in range(4):
                    j = f % 2
                    if 4 * half + f >= 2:
                        sp.wait_ge(pq_ev, 4 * half + f - 1)
                    sp.dma_start(kfr[j][:, :, :],
                                 kf_d[f, :, :, 512 * half:512 * half + 512].rearrange("s p c -> p s c")
                                 ).then_inc(k_in[j], 16)
            sp.wait_ge(pq_ev, 8)
            sp.dma_start(raw[1][:, 0:1024], w_hy_d[0]).then_inc(w_in[1], 16)
            with sp.Fori(1, 16) as m:
                sp.wait_ge(w_lo, U_MRG + 2 * m - 1)
                sp.dma_start(raw[0][:, :], w_glu_d[m]).then_inc(w_in[0], 16)
                sp.wait_ge(w_lo, U_MRG + 2 * m)
                sp.dma_start(raw[1][:, 0:1024], w_hy_d[m]).then_inc(w_in[1], 16)
            with sp.Fori(0, 8) as i:
                for b in range(2):
                    sp.wait_ge(w_lo, U_OUT + 2 * i + b - 1)
                    sp.dma_start(raw[b][:, :], w_out_d[2 * i + b]).then_inc(w_in[b], 16)
            for q in range(4):
                n0 = U_FFN + U_QUARTER * q
                with sp.Fori(0, QTILES) as i:
                    for b in range(2):
                        sp.wait_ge(w_lo, n0 + 2 * i + b - 1)
                        sp.dma_start(raw[b][:, :], w_fi_d[2 * QTILES * q + 2 * i + b]).then_inc(w_in[b], 16)
                with sp.Fori(0, KT // 2) as i:
                    for b in range(2):
                        sp.wait_ge(w_lo, n0 + 2 * QTILES + 2 * i + b - 1)
                        sp.dma_start(raw[b][:, 0:UNIT2], w_fo_d[KT * q + 2 * i + b]).then_inc(w_in[b], 16)
            for g in range(4):
                sp.wait_ge(o_rd, 4 * (g + 1))
                sp.dma_start(out_d[4 * g:4 * g + 4].rearrange("k p t -> p k t"),
                             xacc[:, 4 * g:4 * g + 4, :]).then_inc(s_out, 16)
            sp.wait_ge(s_out, 64)

        @block.gpsimd
        def _(pool):
            for s, n in ((as_used, 4), (am_used, 2), (w_used, 2), (u_fa, 2), (u_fd, 2), (hy_free, 2), (g_free, 2), (m_free, 2), (o_free, 2),
                         (fa_free, 1), (fd_free, 2), (s_squ, 2), (f3_free, 1),
                         (ada1_used, 1), (bl_tr, 2), (mt_rd, 2), (xs_ps, 2), (xs_ev, 2), (l_ps, 4), (y_ps, 4), (tl_a, 2),
                         (tl_d, 2), (y_ev, 2), (ft_rd, 1), (g_st[0], 16), (g_st[1], 16)):
                pool.sem_inc(s, n)
            chain = Chain(pool, pch)
            link = chain.link
            tt, ts = pool.tensor_tensor, pool.tensor_scalar
            pool.memset(ones[:, :], 1.0).then_inc(s_cmod, 1)
            for g in range(4):
                pool.dma_start(x_raw[:, 4 * g:4 * g + 4, :], x_d[:, 4 * g:4 * g + 4, :]).then_inc(s_x, 16)
            pool.dma_start(postab[:, :, :], postab_d).then_inc(s_pos, 16)
            pool.dma_start(c_raw[:, :, :], ctx_d).then_inc(s_ctx, 16)
            for g in range(4):
                pool.wait_ge(s_xp, 4 * g + 4)
                pool.dma_start(xp_d[:, 4 * g:4 * g + 4, :], x_raw[:, 4 * g:4 * g + 4, :]).then_inc(s_xpo, 16)
            pool.wait_ge(s_rs, 1)
            for k in range(KT):
                ins = tt(c_raw[:, k, :], c_raw[:, k, :], rs_c[:, :], MUL)
            link(ins)
            pool.wait_ge(s_xpo, 64)
            for st in range(8):
                f, cs = st // 2, st % 2
                pool.wait_ge(kf_free, st + 1)
                for half in range(2):
                    pool.dma_start(kf_d[f, cs, :, 512 * half:512 * half + 512],
                                   T[12 + 2 * (st % 2) + half][:, :]).then_inc(kf_out[st % 2], 16)
                for k in range(4 * st, 4 * st + 4):
                    if k < KT:
                        ins = tt(x_raw[:, k, :], x_raw[:, k, :], T[3][:, :], MUL)
                    if k == KT - 1:
                        ins.then_inc(s_xn, 1)
            pool.wait_ge(c_mod, 1)
            for i in range(KT // 2):
                for b in range(2):
                    k = 2 * i + b
                    ts(T[10 + b][:, 0:CTX], c_raw[:, k, :], mul_c[:, k:k + 1], mod_c[:, k:k + 1],
                       MUL, ADD).then_inc(cv_, 1)
                for b in range(2):
                    k = 2 * i + b
                    pool.wait_ge(ch_, k + 1)
                    tt(hc_lo[:, k, :], T[10 + b][:, 0:CTX], hc_hi[:, k, :].bitcast(F32), SUB).then_inc(cl_, 1)
                pool.wait_ge(cl_, 2 * i + 2)
            for e in range(2):
                pool.dma_start(ada1[e][:, :], w_ar_d[e]).then_inc(ada1_in[e], 16)
            with pool.Fori(1, 64) as g:
                for e in range(2):
                    pool.wait_ge(ada1_used, 2 * g + e)
                    pool.dma_start(ada1[e][:, :], w_ar_d[2 * g + e]).then_inc(ada1_in[e], 16)
            pool.wait_ge(w_used, 2 + U_TAB)
            pool.dma_start(s5b[:, :, :, :], s5b_d).then_inc(s_bc, 16)
            pool.dma_start(s5c[:, :, :, :], s5c_d).then_inc(s_bc, 16)
            pool.wait_ge(s_bc, 32)
            link(ts(s5b[:, :, 1, :], s5b[:, :, 1, :], -1.0, None, MUL))
            pool.sem_inc(s_bneg, 1)
            pool.wait_ge(s_zero, 1)

            def table(q, dst, pows, modes, n, tP, tQ, free, ready):
                tt(tP[:, :, 0:n, :], pows, modes, MUL)
                tt(tQ[:, 0, 0:n, :], pows[:, 0], modes[:, 1], MUL)
                link(tt(tQ[:, 1, 0:n, :], pows[:, 1], modes[:, 0], MUL))
                pool.wait_ge(*free)
                for ri, (src, op) in enumerate(((tP, SUB), (tQ, ADD))):
                    for g, out in enumerate(halves(dst, ri, 0, n)):
                        r = slice(64 * g, 64 * g + 64)
                        ins = tt(out, src[r, 0, 0:n, :], src[r, 1, 0:n, :], op)
                ins.then_inc(ready, 1)
                pool.wait_ge(ready, q + 1)

            with chain.loop(0, NPAIR, 1) as q:
                dq = NPAIR + q
                table(q, BL[1], pow_b[:, :, :, dq].unsqueeze(3).to_broadcast([P, 2, CH, GROUP]),
                      s5b[:, dq, :, :].unsqueeze(2).to_broadcast([P, 2, CH, GROUP]), CH, prod[2], prod[3],
                      (bl_tr, 2 * q + 2), bl_rd[1])
            pool.wait_ge(rec_dn, 1)
            with chain.loop(0, NPAIR // 4, 4) as i:
                for j in range(4):
                    q = 4 * i + j
                    dq = NPAIR + q
                    table(q, CL[j][1], pow_c[:, :, :, dq].unsqueeze(3).to_broadcast([P, 2, CH + 1, GROUP]),
                          s5c[:, dq, :, :].unsqueeze(2).to_broadcast([P, 2, CH + 1, GROUP]), CH + 1, prod[2],
                          prod[3], (y_ps, q + 1), cl_rd[1])
            pool.wait_ge(cv_ps, 8)
            for m in range(2):
                pool.dma_start(gT[m][:, :, :], gates_v[:, m].rearrange("g p t -> p g t")).then_inc(gt_in[m], 16)
            with pool.Fori(1, KT // 2) as i:
                for b in range(2):
                    m = 2 * i + b
                    pool.wait_ge(m_sum, m - 1)
                    pool.dma_start(gT[b][:, :, :],
                                   gates_v[:, bass.ds(m, 1)].rearrange("g o p t -> p (g o) t")
                                   ).then_inc(gt_in[b], 16)
            pool.wait_ge(w_used, 2 + U_OUT)
            for g in range(4):
                pool.dma_start(xacc[:, 4 * g:4 * g + 4, :], xp_d[:, 4 * g:4 * g + 4, :]).then_inc(xa_in[g], 16)

        @block.scalar
        def _(act):
            chain = Chain(act, ach)

            def split_hi(n, half, b, cols=UNIT):
                act.wait_ge(w_in[b], 16 * (half + 1))
                act.wait_ge(w_used, n + 1)
                act.activation(hi[b][:, 0:cols], raw[b][:, 0:cols], ACT.Copy).then_inc(w_hi, 1)

            act.wait_ge(s_vec, 32)
            act.activation(silu_c[:, :, 0], vecs[:, V_C:V_C + KT], ACT.Silu)
            act.activation(silu_c[:, :, 1], vecs[:, V_CC:V_CC + KT], ACT.Silu).then_inc(s_silu, 1)
            act.wait_ge(s_par, 16)
            act.activation(lt[:, 0, :], s5a[:, 2, :], ACT.Exp).then_inc(lam_s, 1)
            act.wait_ge(lam_z, 1)
            act.activation(lt[:, 3, :], lt[:, 1, :], ACT.Exp).then_inc(lam_s, 1)
            act.wait_ge(lam_z, 2)
            act.activation(lt[:, 7, :], lt[:, 5, :], ACT.Sin)
            act.activation(lt[:, 8, :], lt[:, 6, :], ACT.Sin).then_inc(lam_s, 1)
            act.wait_ge(s_h1a, 1)
            act.activation(fh[2][:, :], fh[0][:, :], ACT.Sin).then_inc(s_h1, 1)
            act.wait_ge(s_h1a, 2)
            act.activation(fh[3][:, :], fh[0][:, :], ACT.Sin).then_inc(s_h1, 1)
            act.wait_ge(s_absd, 1)
            for t in range(4):
                if t:
                    act.wait_ge(s_tap, t)
                for c in range(4):
                    act.activation(T[4 + c][:, :], decay[:, 512 * c:512 * c + 512], ACT.Exp,
                                   scale=vecs[:, V_NEGT + t:V_NEGT + t + 1]).then_inc(s_win, 1)
            for k in range(2 * KT):
                act.wait_ge(s_squ, k + 1)
                if k < KT:
                    act.wait_ge(s_xp, k + 1)
                    act.activation(sqr[k % 2][:, :], x_raw[:, k, :], ACT.Square).then_inc(s_sq, 1)
                else:
                    if k == KT:
                        act.wait_ge(s_ctx, 16)
                    act.activation(sqr[k % 2][:, 0:CTX], c_raw[:, k - KT, :], ACT.Square).then_inc(s_sq, 1)
            for v, w in enumerate((SEQ, CTX)):
                act.wait_ge(s_var, v + 1)
                act.activation(T[2][:, 0:w], T[1][:, 0:w], ACT.Sqrt).then_inc(s_sqrt, 1)
            act.wait_ge(s_tap, 4)
            act.wait_ge(am_used, 2 + KT)
            for j in range(4):
                ins = act.activation(row_m[0:2, 512 * j:512 * j + 512], ps[4 + j][0:2, :], ACT.Copy)
            ins.then_inc(am_row, 1)
            for st in range(8):
                act.wait_ge(kf_ps, st + 1)
                if st >= 2:
                    act.wait_ge(kf_out[st % 2], 32 * (st // 2))
                for half in range(2):
                    ins = act.activation(T[12 + 2 * (st % 2) + half][:, :], ps[2 * (st % 2) + half][:, :], ACT.Copy)
                ins.then_inc(kf_free, 1)
            act.wait_ge(c_mod, 1)
            act.wait_ge(s_xn, 1)
            split_hi(0, 0, 0)
            with act.Fori(0, KT // 2) as i:
                for b in range(2):
                    act.wait_ge(s_hv, 2 * i + b + 1)
                    act.activation(h_hi[:, 2 * i + b, :], T[8 + b][:, :], ACT.Copy).then_inc(s_hh, 1)
                    act.wait_ge(cv_, 2 * i + b + 1)
                    act.activation(hc_hi[:, 2 * i + b, :], T[10 + b][:, 0:CTX], ACT.Copy).then_inc(ch_, 1)
            act.wait_ge(s_hl, KT)
            act.wait_ge(cl_, KT)
            for j in range(2):
                act.wait_ge(kf_out[j], 128)
            with act.Fori(0, 4) as i:
                for b in range(2):
                    split_hi(2 * i + b + 1, i + b, 1 - b)
                    act.wait_ge(w_used, 2 + 2 * i + b + 1)
                    act.activation(u_ch[:, 2 * i + b, CTX:CTX + SEQ], ps[b][:, :], ACT.Copy).then_inc(u_fa, 1)
            with act.Fori(0, 12) as i:
                for b in range(2):
                    split_hi(8 + 2 * i + b + 1, 4 + i + b, 1 - b)
            def gate_tile(i, b):
                act.wait_ge(w_used, 2 + 32 + 2 * i + b + 1)
                act.wait_ge(g_st[b], 16 * i + 16)
                act.activation(gst[b][:, :], ps[b][:, :], ACT.Sigmoid).then_inc(g_free, 1)
                act.wait_ge(g_free, 2 + 2 * i + b + 1)
                act.dma_start(gates_d[2 * i + b], gst[b][:, :]).then_inc(g_st[b], 16)

            with act.Fori(0, 15) as i:
                for b in range(2):
                    split_hi(32 + 2 * i + b + 1, 16 + i + b, 1 - b)
                    gate_tile(i, b)
            split_hi(63, 31, 1)
            gate_tile(15, 0)
            gate_tile(15, 1)
            for b in range(2):
                act.wait_ge(g_st[b], 16 * 17)
            act.wait_ge(acc1_red, 8)
            act.wait_ge(u_fd, 10)
            for q in range(4):
                for j in range(0, 4, 2):
                    ins = act.activation(U4[32 * j:32 * j + 32, q::4, :],
                                         u_ch[32 * q:32 * q + 32, :, j::4], ACT.Copy)
                ins.then_inc(u4a, 1)
            with act.Fori(0, NPAIR) as q:
                for d in range(2):
                    act.wait_ge(bl_tr, 2 * q + d + 3)
                    act.wait_ge(xs_ps, 2 * q + d + 1)
                    act.activation(MT[d][:, :, :].rearrange("p a b -> p (a b)"), ps[d][:, :],
                                   ACT.Copy).then_inc(mt_rd, 1)
                for d in range(2):
                    act.wait_ge(xs_ps, 2 * q + d + 3)
                    src = ps[2 + d][:, 0:2 * NCH].rearrange("p (r c) -> p c r", r=2)
                    dq = NPAIR * d + q
                    if d == 0:
                        act.activation(X[:, :, :, dq], src, ACT.Copy).then_inc(xs_ev, 1)
                    else:
                        act.activation(X[:, 0:NC_CTX, :, dq], src[:, NC_CTX - 1::-1, :], ACT.Copy)
                        act.activation(X[:, NC_CTX:NCH, :, dq], src[:, NCH - 1:NC_CTX - 1:-1, :],
                                       ACT.Copy).then_inc(xs_ev, 1)
            act.wait_ge(rec_dn, 1)

            def replicas(q, j):
                act.wait_ge(l_ps, q + 1)
                act.wait_ge(y_ps, q + 1)
                act.activation(XR[j][:, :, ::-1], X[:, NC_CTX - 1:NCH - 1, :, NPAIR + q].rearrange("p c r -> p r c"),
                               ACT.Copy)
                for d in range(2):
                    ins = act.activation(BB[j][d][:, :, :, :],
                                         bbar[:, NPAIR * d + q, :, :].unsqueeze(2).to_broadcast([P, 2, 4, 32]),
                                         ACT.Copy)
                ins.then_inc(bb_rd, 1)

            def toeplitz(q, par):
                act.wait_ge(l_ps, q + 5)
                for j in range(3):
                    for a in range(2):
                        o7 = 32 * (CH - 1 - 4 * a - j)
                        ins = act.activation(TL[par][32 * j:32 * j + 32, a, :, :].rearrange("p i h -> p (i h)"),
                                             ps[4 + 2 * par][32 * j:32 * j + 32, o7:o7 + 256], ACT.Copy)
                ins.then_inc(tl_a, 1)

            for q in range(3):
                replicas(q, q)
            with act.Fori(0, NPAIR // 4 - 1) as i:
                for j in range(4):
                    q = 4 * i + j
                    toeplitz(q, j % 2)
                    replicas(q + 3, (j + 3) % 4)
            for j in range(4):
                q = NPAIR - 4 + j
                toeplitz(q, j % 2)
                if j == 0:
                    replicas(q + 3, 3)
            act.wait_ge(y_ev, NPAIR + 2)
            for q in range(4):
                for j in range(0, 4, 2):
                    ins = act.activation(y_ch[32 * q:32 * q + 32, :, j::4],
                                         U4[32 * j:32 * j + 32, q::4, CTX // 4:], ACT.Copy)
            ins.then_inc(ych, 1)
            act.wait_ge(ych, 1)
            act.wait_ge(ycd, 1)
            for g in range(2):
                act.activation(y_ch[:, 4 * g:4 * g + 4, :], y_ch[:, 4 * g:4 * g + 4, :],
                               ACT.Gelu_apprx_tanh).then_inc(gel, 1)
                act.wait_ge(gel, g + 1)
                act.activation(yg_hi[:, 4 * g:4 * g + 4, :], y_ch[:, 4 * g:4 * g + 4, :], ACT.Copy).then_inc(ygh, 1)
            for s in range(4):
                act.wait_ge(w_in[s % 2], 16 * (33 + s // 2))
                dst = (tf_hi, tg_hi)[s // 2][:, s % 2, :, :].rearrange("p a b -> p (a b)")
                act.activation(dst, raw[s % 2][:, :], ACT.Copy).then_inc(w_hi, 1)

            def transposed_u(half):
                for t in range(4):
                    act.wait_ge(ut_ps, 4 * half + t + 1)
                    act.activation(uT_hi[:, t, :], ps[t % 2][:, :], ACT.Copy).then_inc(ut_h, 1)

            def spectrum(half):
                for f in range(4):
                    for c in range(2):
                        act.wait_ge(yv, 8 * half + 2 * f + c + 1)
                        if half and f == 0 and c == 0:
                            act.wait_ge(cv_ps, 4)
                        act.activation(Y_hi[:, c, f, :], ct[2 + c][:, :], ACT.Copy).then_inc(yh, 1)

            def conv_out(half):
                for c in range(4):
                    i = 4 * half + c
                    act.wait_ge(ov, i + 1)
                    act.activation(hyo_hi[:, i, :], ct[1][:, :], ACT.Copy).then_inc(oh, 1)

            act.wait_ge(ygl, 2)
            transposed_u(0)
            spectrum(0)
            act.wait_ge(pq_ps, 4)
            transposed_u(1)
            conv_out(0)
            spectrum(1)
            conv_out(1)
            def merge(n, m, half, mm):
                split_hi(n + 1, half, 1, 1024)
                act.wait_ge(w_used, n + 3)
                act.activation(S0[mm][:, :], ps[3 * mm + 1][:, :], ACT.Sigmoid).then_inc(m_sg, 1)
                split_hi(n + 2, half + 1, 0)
                act.wait_ge(m_sum, m + 1)
                act.activation(mg_hi[:, m, :], S1[mm][:, :], ACT.Copy).then_inc(m_hi, 1)

            split_hi(U_MRG, U_MRG // 2, 0)
            with act.Fori(0, KT // 2) as i:
                for mm in range(2):
                    merge(U_MRG + 4 * i + 2 * mm, 2 * i + mm, U_MRG // 2 + 2 * i + mm, mm)
            with act.Fori(0, KT // 2) as i:
                for b in range(2):
                    split_hi(U_OUT + 2 * i + b + 1, U_OUT // 2 + i + b, 1 - b)

            def sqrt_and_h(v):
                act.wait_ge(s_var, v + 1)
                act.activation(ct[3][:, :], ct[2][:, :], ACT.Sqrt).then_inc(s_sqrt, 1)

            sqrt_and_h(2)
            with act.Fori(0, KT // 2) as i:
                for b in range(2):
                    act.wait_ge(s_hv, KT + 2 * i + b + 1)
                    act.activation(h2_hi[:, 2 * i + b, :], ct[1 + b][:, :], ACT.Copy).then_inc(s_hh, 1)
            for q in range(4):
                n0, g0 = U_FFN + U_QUARTER * q, QTILES * q

                def pair(i, cols):
                    n, half = n0 + 2 * i, n0 // 2 + i
                    split_hi(n + 1, half, 1)
                    act.wait_ge(w_used, n + 3)
                    act.activation(f_s[:, :], ps[0][:, :], ACT.Silu).then_inc(fa_free, 1)
                    split_hi(n + 2, half + 1, 0, cols)
                    act.wait_ge(ft_rd, g0 + i + 2)
                    act.activation(a_hi[:, i, :], f_t[:, :], ACT.Copy).then_inc(fh_rd, 1)

                with act.Fori(0, QTILES - 1) as i:
                    pair(i, UNIT)
                pair(QTILES - 1, UNIT2)
                n1 = n0 + 2 * QTILES
                with act.Fori(0, KT // 2 - 1) as i:
                    for b in range(2):
                        split_hi(n1 + 2 * i + b + 1, n1 // 2 + i + b, 1 - b, UNIT2)
                split_hi(n1 + KT - 1, n1 // 2 + KT // 2 - 1, 1, UNIT2)
                if q < 3:
                    split_hi(n1 + KT, n1 // 2 + KT // 2, 0)
            sqrt_and_h(3)

        @block.vector
        def _(dve):
            chain = Chain(dve, dch)
            link, mark = chain.link, chain.mark
            tt, ts, stt = dve.tensor_tensor, dve.tensor_scalar, dve.scalar_tensor_tensor

            def split_lo(n, b, cols=UNIT):
                dve.wait_ge(w_hi, n + 1)
                tt(lo[b][:, 0:cols], raw[b][:, 0:cols], hi[b][:, 0:cols].bitcast(F32), SUB).then_inc(w_lo, 1)

            def reduce_angle(dst, k, src, shift):
                link(ts(k, src, 1.0 / (2 * math.pi), shift / (2 * math.pi), MUL, ADD))
                link(ts(k, k, MAGIC, MAGIC, ADD, SUB))
                link(stt(dst, k, -TWO_PI_1, src, MUL, ADD))
                link(stt(dst, k, -TWO_PI_2, dst, MUL, ADD))
                link(stt(dst, k, -TWO_PI_3, dst, MUL, ADD))
                link(ts(dst, dst, shift, PI_SAFE, ADD, ALU.min))
                return ts(dst, dst, -PI_SAFE, None, ALU.max)

            def rstd(v, sums, a, b, c, out, w):
                dve.wait_ge(s_ss, v + 1)
                link(ts(a, sums, 1.0 / D, EPS, MUL, ADD))
                dve.reciprocal(b, a).then_inc(s_var, 1)
                dve.wait_ge(s_sqrt, v + 1)
                link(tt(b, c, c, MUL))
                link(tt(b, b, a, MUL))
                link(ts(b, b, -0.5, 1.5, MUL, ADD))
                link(tt(out, b, c, MUL))

            a_re, a_im = s5a[:, 0, :], s5a[:, 1, :]
            L = [lt[:, j, :] for j in range(13)]
            dve.wait_ge(lam_s, 1)
            tt(L[1], a_re, L[0], MUL).then_inc(lam_z, 1)
            link(tt(L[2], a_im, L[0], MUL))
            link(reduce_angle(L[5], L[4], L[2], 0.0))
            reduce_angle(L[6], L[4], L[2], math.pi / 2).then_inc(lam_z, 1)
            dve.wait_ge(lam_s, 3)
            tt(lam_rr[:, 0, :], L[3], L[8], MUL)
            link(tt(lam_ii[:, 1, :], L[3], L[7], MUL))
            dve.tensor_copy(lam_rr[:, 1, :], lam_rr[:, 0, :])
            ts(lam_ii[:, 0, :], lam_ii[:, 1, :], -1.0, None, MUL)
            ts(L[9], lam_rr[:, 0, :], -1.0, None, ADD)
            tt(L[10], a_re, a_re, MUL)
            link(tt(L[11], a_im, a_im, MUL))
            link(tt(L[10], L[10], L[11], ADD))
            dve.reciprocal(L[10], L[10])
            tt(L[0], L[9], a_re, MUL)
            tt(L[1], lam_ii[:, 1, :], a_im, MUL)
            tt(L[2], lam_ii[:, 1, :], a_re, MUL)
            link(tt(L[3], L[9], a_im, MUL))
            tt(L[0], L[0], L[1], ADD)
            link(tt(L[2], L[2], L[3], SUB))
            tt(L[4], L[0], L[10], MUL)
            tt(L[5], L[0], L[10], MUL)
            link(tt(L[7], L[2], L[10], MUL))
            link(ts(L[6], L[7], -1.0, None, MUL))
            dve.memset(pw[:, 0, 0, :], 1.0)
            dve.memset(pw[:, 1, 0, :], 0.0)
            dve.tensor_copy(pw[:, 0, 1, :], lam_rr[:, 0, :])
            link(dve.tensor_copy(pw[:, 1, 1, :], lam_ii[:, 1, :]))
            tmp2 = lt[:, 9:11, :]
            for k in range(2, CH + 1):
                tt(tmp2, pw[:, ::-1, k - 1, :], lam_ii[:, :, :], MUL)
                link(tt(pw[:, :, k, :], pw[:, :, k - 1, :], lam_rr[:, :, :], MUL))
                link(tt(pw[:, :, k, :], pw[:, :, k, :], tmp2, ADD))
            for d in range(2):
                cols = slice(NPAIR * d, NPAIR * d + NPAIR)
                dve.tensor_copy(pow_c[:, :, :, cols], pw[:, :, :, cols] if d == 0 else pw[:, :, ::-1, cols])
                if d == 0:
                    src, swp = pw[:, :, CH - 1::-1, cols], pw[:, ::-1, CH - 1::-1, cols]
                else:
                    src, swp = pw[:, :, 0:CH, cols], pw[:, ::-1, 0:CH, cols]
                for ri in range(2):
                    tt(pow_b[:, ri, :, cols], src[:, ri], L[4][:, cols].unsqueeze(1).to_broadcast([P, CH, NPAIR]), MUL)
                    ins = tt(pwt[:, ri, :, :], swp[:, ri],
                             L[6 + ri][:, cols].unsqueeze(1).to_broadcast([P, CH, NPAIR]), MUL)
                link(ins)
                link(tt(pow_b[:, :, :, cols], pow_b[:, :, :, cols], pwt[:, :, :, :], ADD))
                link(ts(pow_b[:, 1, :, cols], pow_b[:, 1, :, cols], -1.0, None, MUL))
            for ri in range(2):
                dve.tensor_copy(lam8[:, 0, ri, :], pw[:, 0, CH, :])
                ts(lam8[:, 1, ri, :], pw[:, 1, CH, :], (-1.0, 1.0)[ri], None, MUL)

            dve.wait_ge(s_filt, 96)
            for layer in range(2):
                dve.wait_ge(s_h1p, layer + 1)
                link(ts(fh[1][:, :], ps[0][0:HID, :], fpar[:, 2 * layer:2 * layer + 1],
                        fpar[:, 2 * layer + 1:2 * layer + 2], ADD, MUL))
                k = T[4][0:HID, :]
                reduce_angle(fh[0][:, :], k, fh[1][:, :], 0.0).then_inc(s_h1a, 1)
            link(ts(T[5][:, :], decay[:, 0:512], -1.0, None, MUL))
            for c in range(4):
                if c:
                    link(ts(T[5][:, :], decay[:, 512 * c:512 * c + 512], -1.0, None, MUL))
                link(tt(decay[:, 512 * c:512 * c + 512], decay[:, 512 * c:512 * c + 512], T[5][:, :], ALU.max))
            dve.sem_inc(s_absd, 1)
            dve.wait_ge(s_pos, 16)
            dve.wait_ge(s_x, 64)
            for k in range(KT):
                xk = x_raw[:, k, :].rearrange("p (r c) -> p r c", c=GRID)
                if k < 8:
                    pos = postab[:, k, 0:8].unsqueeze(2).to_broadcast([P, 8, GRID])
                else:
                    pos = postab[:, k - 8, 8:8 + GRID].unsqueeze(1).to_broadcast([P, 8, GRID])
                tt(xk, xk, pos, ADD).then_inc(s_xp, 1)
            for t in range(4):
                dve.wait_ge(f3_ps, t + 1)
                dve.wait_ge(s_win, 4 * t + 4)
                for c in range(4):
                    ins = tt(T[4 + c][:, :], ps[c][:, :], T[4 + c][:, :], MUL)
                if t == 0:
                    link(ins)
                    for c in range(2, 4):
                        ins = dve.memset(T[4 + c][0:1, :], 0.0)
                ins.then_inc(f3_free, 1)
                dve.wait_ge(f3_free, t + 2)
                for half in range(2):
                    tt(taps_s[:, t, 512 * half:512 * half + 512], T[4 + half][:, :], T[6 + half][:, :], ADD)
                    ins = tt(taps_d[:, t, 512 * half:512 * half + 512], T[4 + half][:, :], T[6 + half][:, :], SUB)
                ins.then_inc(s_tap, 1)
            def shift_rows(half, i):
                for j in range(4):
                    n = KT * half + 4 * i + j
                    dve.wait_ge(as_in[j], 16 * (4 * half + i + 1))
                    dve.wait_ge(as_used, 4 + n)
                    for v in range(2):
                        ins = stt(acc_s[half][:, v, :], ada_s[j][:, :], silu_c[:, bass.ds(4 * i + j, 1), v],
                                  acc_s[half][:, v, :], MUL, ADD)
                    ins.then_inc(as_used, 1)

            dve.wait_ge(s_tap, 4)
            for a in acc_s:
                ins = dve.memset(a[:, :, :], 0.0)
            link(ins)
            dve.wait_ge(s_silu, 1)
            shift_rows(0, 0)
            shift_rows(0, 1)
            rstd(0, ps[2][:, :], T[0][:, :], T[1][:, :], T[2][:, :], T[3][:, :], SEQ)
            rstd(1, ps[3][:, 0:CTX], T[0][:, 0:CTX], T[1][:, 0:CTX], T[2][:, 0:CTX], rs_c[:, :], CTX)
            dve.sem_inc(s_rs, 1)
            with dve.Fori(2, 4) as i:
                shift_rows(0, i)
            with dve.Fori(0, 4) as i:
                shift_rows(1, i)
            dve.wait_ge(am_ps, 1)
            dve.wait_ge(as_red, 2)
            for v, (mod, mul) in enumerate(((mod_x, mul_x), (mod_c, mul_c))):
                for bank in range(2):
                    cols = slice(KT * bank, KT * bank + KT)
                    src = ps[5 - bank][:, 0:2 * KT].rearrange("p (m s) -> p m s", s=2)[:, :, v]
                    ins = tt(mod[:, cols], src, vecs[:, V_BADA + KT * bank:V_BADA + KT * bank + KT], ADD)
                link(ins)
                ins = stt(mul[:, :], mod[:, KT:2 * KT], 1.0, vecs[:, V_NM:V_NM + KT], ADD, MUL)
            ins.then_inc(c_mod, 1)
            dve.wait_ge(c_mod, 1)
            dve.wait_ge(s_xn, 1)

            def first_h(lo_i, hi_i):
                with dve.Fori(lo_i, hi_i) as i:
                    for b in range(2):
                        k = 2 * i + b
                        ts(T[8 + b][:, :], x_raw[:, k, :], mul_x[:, bass.ds(k, 1)], mod_x[:, bass.ds(k, 1)],
                           MUL, ADD).then_inc(s_hv, 1)
                    for b in range(2):
                        k = 2 * i + b
                        dve.wait_ge(s_hh, k + 1)
                        tt(h_lo[:, k, :], T[8 + b][:, :], h_hi[:, k, :].bitcast(F32), SUB).then_inc(s_hl, 1)
                    dve.wait_ge(s_hl, 2 * i + 2)

            first_h(0, 2)
            split_lo(0, 0)
            first_h(2, KT // 2)

            def modulated(src, rs, tmp, mul, mod, shift0, done, dst_hi, dst_lo):
                with dve.Fori(0, KT // 2) as i:
                    for b in range(2):
                        k = 2 * i + b
                        stt(tmp[b], src[:, k, :], mul[:, bass.ds(k, 1)], rs, MUL, MUL).then_inc(s_hm, 1)
                    for b in range(2):
                        k = 2 * i + b
                        dve.wait_ge(s_hm, k + 1)
                        ts(tmp[b], tmp[b], mod[:, bass.ds(shift0 + k, 1)], None, ADD).then_inc(s_hv, 1)
                    for b in range(2):
                        k = 2 * i + b
                        dve.wait_ge(s_hh, done + k + 1)
                        tt(dst_lo[:, k, :], tmp[b], dst_hi[:, k, :].bitcast(F32), SUB).then_inc(s_hl, 1)
                    dve.wait_ge(s_hl, done + 2 * i + 2)

            def ada_rows(g, k0):
                for e in range(2):
                    dve.wait_ge(ada1_used, 16 * g + k0 + e + 1)
                    dve.wait_ge(ada1_in[e], 16 * (8 * g + 1) + 8 * k0)
                    stt(acc1[:, :], ada1[e][:, :], silu_c[:, bass.ds(k0 + e, 1), 0], acc1[:, :], MUL, ADD
                        ).then_inc(ada1_used, 1)

            link(dve.memset(acc1[:, :], 0.0))
            with dve.Fori(0, 4) as i:
                for b in range(2):
                    split_lo(2 * i + b + 1, 1 - b)
                    ada_rows(0, 4 * i + 2 * b)
                    dve.wait_ge(w_used, 2 + 2 * i + b + 1)
                    dve.tensor_copy(u_ch[:, 2 * i + b, 0:CTX], ps[2 + b][:, 0:CTX]).then_inc(u_fd, 1)
            for part in range(3):
                dve.wait_ge(acc1_red, part + 1)
                link(dve.memset(acc1[:, :], 0.0))
                with chain.loop(0, 4, (4, 6, 4)[part]) as i:
                    for b in range(2):
                        c = 2 * i + b
                        t = 8 * part + c
                        split_lo(8 + t + 1, 1 - b)
                        ada_rows(part + 1, 4 * i + 2 * b)
                        dst = (uh[:, c, :], zx1[:, :], x0z[:, c, :])[part]
                        w = [vecs[:, bass.ds(V_CW + 24 * tap + t, 1)] for tap in range(3)]
                        src = ps[b]
                        dve.wait_ge(w_used, 2 + 8 + t + 1)
                        link(ts(dst, src[:, :], w[1], vecs[:, bass.ds(V_CB + t, 1)], MUL, ADD))
                        link(stt(dst[:, 1:SEQ], src[:, 0:SEQ - 1], w[0], dst[:, 1:SEQ], MUL, ADD))
                        ins = stt(dst[:, 0:SEQ - 1], src[:, 1:SEQ], w[2], dst[:, 0:SEQ - 1], MUL, ADD)
                        ins.then_inc(hy_free, 1)
                        if part == 1:
                            dve.wait_ge(hy_free, 2 + t + 1)
                            link(tt(uh[:, c, :], uh[:, c, :], zx1[:, :], MUL))

            def gate_units(g, last):
                dve.wait_ge(acc1_red, g + 4)
                link(dve.memset(acc1[:, :], 0.0))
                for j in range(8):
                    if not (last and j == 7):
                        split_lo(32 + 8 * g + j + 1, 1 - j % 2)
                    ada_rows(4 + g, 2 * j)

            with chain.loop(0, 3, 1) as g:
                gate_units(g, False)
            gate_units(3, True)
            dve.wait_ge(acc1_red, 8)
            link(tt(mod_x[:, N_ADA0:N_ADA], ps[7][:, 0:N_ADA - N_ADA0], vecs[:, V_BADA + N_ADA0:V_BADA + N_ADA], ADD))
            link(stt(mul_f[:, :], mod_x[:, 4 * KT:5 * KT], 1.0, vecs[:, V_NF:V_NF + KT], ADD, MUL))
            for b in range(2):
                dve.wait_ge(g_st[b], 16 * 17)
            dve.wait_ge(u_fa, 10)
            for q in range(4):
                for j in range(1, 4, 2):
                    ins = dve.tensor_copy(U4[32 * j:32 * j + 32, q::4, :], u_ch[32 * q:32 * q + 32, :, j::4])
            ins.then_inc(u4d, 1)
            dve.wait_ge(s_bneg, 1)
            dve.wait_ge(u4a, 4)
            dve.wait_ge(u4d, 1)
            dve.memset(bbar[:, :, :, :], 0.0)
            for t in (BL[0], BL[1]):
                ins = dve.memset(t[:, :, :, :], 0.0)
            link(ins)
            for d in range(2):
                cols = slice(NPAIR * d, NPAIR * d + NPAIR)
                f = [pow_b[:, ri, CH - 1 if d == 0 else 0, cols].unsqueeze(2).to_broadcast([P, NPAIR, GROUP])
                     for ri in range(2)]
                m = [s5b[:, cols, ri, :] for ri in range(2)]
                tt(bt[0][:, :, :], f[0], m[0], MUL)
                tt(bt[1][:, :, :], f[1], m[1], MUL)
                tt(bt[2][:, :, :], f[0], m[1], MUL)
                link(tt(bt[3][:, :, :], f[1], m[0], MUL))
                for g in range(2):
                    r = slice(64 * g, 64 * g + 64)
                    tt(bbar[r, cols, 0, 16 * g:16 * g + 16], bt[0][r, :, :], bt[1][r, :, :], SUB)
                    ins = tt(bbar[r, cols, 1, 16 * g:16 * g + 16], bt[2][r, :, :], bt[3][r, :, :], ADD)
                link(ins)
            dve.memset(CL[0][0][:, :, :, :], 0.0)
            dve.memset(CL[0][1][:, :, :, :], 0.0).then_inc(s_zero, 1)
            dve.wait_ge(s_zero, 1)

            def table(q, dst, pows, modes, n, tP, tQ, free, ready):
                tt(tP[:, :, 0:n, :], pows, modes, MUL)
                tt(tQ[:, 0, 0:n, :], pows[:, 0], modes[:, 1], MUL)
                link(tt(tQ[:, 1, 0:n, :], pows[:, 1], modes[:, 0], MUL))
                dve.wait_ge(*free)
                for ri, (src, op) in enumerate(((tP, SUB), (tQ, ADD))):
                    for g, out in enumerate(halves(dst, ri, 0, n)):
                        r = slice(64 * g, 64 * g + 64)
                        ins = tt(out, src[r, 0, 0:n, :], src[r, 1, 0:n, :], op)
                ins.then_inc(ready, 1)
                dve.wait_ge(ready, q + 1)

            with chain.loop(0, NPAIR, 1) as q:
                table(q, BL[0], pow_b[:, :, :, q].unsqueeze(3).to_broadcast([P, 2, CH, GROUP]),
                      s5b[:, q, :, :].unsqueeze(2).to_broadcast([P, 2, CH, GROUP]), CH, prod[0], prod[1],
                      (bl_tr, 2 * q + 1), bl_rd[0])
            dve.wait_ge(xs_ev, NDQ + 2)
            with chain.loop(0, (NCH - 1) // SCAN, 3 * SCAN) as r:
                for step in range(SCAN):
                    s = SCAN * r + step + 1
                    link(tt(rec[:, :, :, :], X[:, s - 1, :, :].unsqueeze(1).to_broadcast([P, 2, 2, NDQ]),
                            lam8[:, :, :, :], MUL))
                    link(tt(X[:, s, :, :], X[:, s, :, :], rec[:, 0, :, :], ADD))
                    link(tt(X[:, s, :, :], X[:, s, :, :], rec[:, 1, ::-1, :], ADD))
            for j in range(1, 4):
                for d in range(2):
                    ins = dve.memset(CL[j][d][:, :, :, :], 0.0)
            ins.then_inc(rec_dn, 1)
            dve.wait_ge(rec_dn, 1)

            def readout_matrix(q, j):
                table(q, CL[j][0], pow_c[:, :, :, q].unsqueeze(3).to_broadcast([P, 2, CH + 1, GROUP]),
                      s5c[:, q, :, :].unsqueeze(2).to_broadcast([P, 2, CH + 1, GROUP]), CH + 1, prod[0], prod[1],
                      (y_ps, q + 1), cl_rd[0])

            def toeplitz(q, par):
                dve.wait_ge(l_ps, q + 5)
                for a in range(2):
                    o7 = 32 * (CH - 1 - 4 * a - 3)
                    ins = dve.tensor_copy(TL[par][96:128, a, :, :].rearrange("p i h -> p (i h)"),
                                          ps[4 + 2 * par][96:128, o7:o7 + 256])
                ins.then_inc(tl_d, 1)

            def outputs(q, par):
                dve.wait_ge(y_ps, q + 5)
                yq = U4[:, q, CTX // 4:].rearrange("p (c a) -> p c a", a=2)
                src = ps[5 + 2 * par][:, 0:2 * NC_LAT].rearrange("p (a c) -> p c a", a=2)
                stt(yq, yq, vecs[:, bass.ds(V_D4 + q, 1)], src, MUL, ADD).then_inc(y_ev, 1)

            for q in range(3):
                readout_matrix(q, q)
            toeplitz(0, 0)

            def step(q, j, tables):
                if tables:
                    readout_matrix(q + 3, (j + 3) % 4)
                toeplitz(q + 1, (j + 1) % 2)
                outputs(q, j % 2)

            with chain.loop(0, NPAIR // 4 - 1, 4) as i:
                for j in range(4):
                    step(4 * i + j, j, True)
            for j in range(3):
                step(NPAIR - 4 + j, j, j == 0)
            outputs(NPAIR - 1, 1)
            dve.wait_ge(y_ev, NPAIR + 2)
            for q in range(4):
                for j in range(1, 4, 2):
                    ins = dve.tensor_copy(y_ch[32 * q:32 * q + 32, :, j::4], U4[32 * j:32 * j + 32, q::4, CTX // 4:])
            ins.then_inc(ycd, 1)
            for g in range(2):
                dve.wait_ge(ygh, g + 1)
                tt(yg_lo[:, 4 * g:4 * g + 4, :], y_ch[:, 4 * g:4 * g + 4, :],
                   yg_hi[:, 4 * g:4 * g + 4, :].bitcast(F32), SUB).then_inc(ygl, 1)
            for s in range(4):
                dve.wait_ge(w_hi, U_TAB + s + 1)
                h, l = ((tf_hi, tf_lo), (tg_hi, tg_lo))[s // 2]
                tt(l[:, s % 2, :, :].rearrange("p a b -> p (a b)"), raw[s % 2][:, :],
                   h[:, s % 2, :, :].rearrange("p a b -> p (a b)").bitcast(F32), SUB).then_inc(w_lo, 1)

            def transposed_u(half):
                for t in range(4):
                    dve.wait_ge(ut_h, 4 * half + t + 1)
                    tt(uT_lo[:, t, :], ps[t % 2][:, :], uT_hi[:, t, :].bitcast(F32), SUB).then_inc(ut_l, 1)

            def spectrum(half):
                for f in range(4):
                    n = 4 * half + f
                    dve.wait_ge(pq_ps, n + 1)
                    dve.wait_ge(k_in[f % 2], 16 * (n // 2 + 1))
                    if half and f == 0:
                        dve.wait_ge(ol, 4)
                    A, B = (kfr[f % 2][:, s, :] for s in range(2))
                    pp, pq = (ps[2 + 2 * (f % 2) + s][:, :] for s in range(2))
                    tt(ct[0][:, :], A, pp, MUL)
                    link(tt(ct[1][:, :], B, pq, MUL))
                    link(tt(ct[2][:, :], ct[0][:, :], ct[1][:, :], SUB))
                    dve.sem_inc(yv, 1)
                    tt(ct[0][:, :], A, pq, MUL)
                    ins = tt(ct[1][:, :], B, pp, MUL)
                    ins.then_inc(pq_ev, 1)
                    dve.wait_ge(pq_ev, n + 1)
                    tt(ct[3][:, :], ct[0][:, :], ct[1][:, :], ADD).then_inc(yv, 1)
                    for c in range(2):
                        dve.wait_ge(yh, 8 * half + 2 * f + c + 1)
                        tt(Y_lo[:, c, f, :], ct[2 + c][:, :], Y_hi[:, c, f, :].bitcast(F32), SUB).then_inc(yl, 1)

            def conv_out(half):
                for c in range(4):
                    i = 4 * half + c
                    dve.wait_ge(cv_ps, i + 1)
                    stt(ct[0][:, :], uh[:, i, :], vecs[:, V_HB + i:V_HB + i + 1], ps[6 + i % 2][:, :],
                        MUL, ADD).then_inc(cv_free, 1)
                    dve.wait_ge(cv_free, i + 1)
                    tt(ct[1][:, :], ct[0][:, :], x0z[:, i, :], MUL).then_inc(ov, 1)
                    dve.wait_ge(oh, i + 1)
                    tt(hyo_lo[:, i, :], ct[1][:, :], hyo_hi[:, i, :].bitcast(F32), SUB).then_inc(ol, 1)

            transposed_u(0)
            spectrum(0)
            transposed_u(1)
            conv_out(0)
            spectrum(1)
            conv_out(1)
            split_lo(U_MRG, 0)
            with chain.loop(0, KT // 2, 4) as i:
                for mm in range(2):
                    m, n = 2 * i + mm, U_MRG + 4 * i + 2 * mm
                    split_lo(n + 1, 1, 1024)
                    dve.wait_ge(m_sg, m + 1)
                    link(tt(S1[mm][:, :], ps[3 * mm][:, :], S0[mm][:, :], MUL))
                    dve.wait_ge(gt_in[mm], 16 * (i + 1))
                    tt(S1[mm][:, :], S1[mm][:, :], gT[mm][:, 0, :], MUL)
                    split_lo(n + 2, 0)
                    dve.wait_ge(w_used, 2 + n + 2)
                    tt(S0[mm][:, :], ps[3 * mm + 2][:, :], gT[mm][:, 1, :], MUL).then_inc(m_free, 1)
                    dve.wait_ge(m_free, 2 + m + 1)
                    link(tt(S1[mm][:, :], S1[mm][:, :], S0[mm][:, :], ADD))
                    dve.sem_inc(m_sum, 1)
                    dve.wait_ge(m_hi, m + 1)
                    tt(mg_lo[:, m, :], S1[mm][:, :], mg_hi[:, m, :].bitcast(F32), SUB).then_inc(m_lo, 1)
            for g in range(4):
                dve.wait_ge(xa_in[g], 16)
            link(dve.memset(ct[0][:, :], 0.0))

            def add_square(m):
                link(tt(ct[1][:, :], xacc[:, m, :], xacc[:, m, :], MUL))
                link(tt(ct[0][:, :], ct[0][:, :], ct[1][:, :], ADD))

            with chain.loop(0, KT // 2, 6) as i:
                for b in range(2):
                    m = 2 * i + b
                    split_lo(U_OUT + m + 1, 1 - b)
                    dve.wait_ge(w_used, 2 + U_OUT + m + 1)
                    ins = stt(xacc[:, m, :], ps[6 + b][:, :], mod_x[:, bass.ds(2 * KT + m, 1)], xacc[:, m, :], MUL, ADD)
                    link(ins)
                    dve.sem_inc(o_free, 1)
                    add_square(m)
            dve.sem_inc(s_acc, 1)
            rstd(2, ps[4][:, :], ct[1][:, :], ct[2][:, :], ct[3][:, :], ct[0][:, :], SEQ)
            modulated(xacc, ct[0][:, :], [ct[1 + b][:, :] for b in range(2)], mul_f, mod_x, 3 * KT, KT, h2_hi, h2_lo)
            for q in range(4):
                n0, g0 = U_FFN + U_QUARTER * q, QTILES * q

                def pair(i, cols):
                    n = n0 + 2 * i
                    split_lo(n + 1, 1)
                    split_lo(n + 2, 0, cols)
                    dve.wait_ge(w_used, 2 + n + 2)
                    dve.wait_ge(fa_free, 1 + g0 + i + 1)
                    tt(f_t[:, :], f_s[:, :], ps[1][:, :], MUL).then_inc(ft_rd, 1)
                    dve.wait_ge(fh_rd, g0 + i + 1)
                    tt(a_lo[:, i, :], f_t[:, :], a_hi[:, i, :].bitcast(F32), SUB).then_inc(fl_rd, 1)
                    dve.wait_ge(fl_rd, g0 + i + 1)

                with dve.Fori(0, QTILES - 1) as i:
                    pair(i, UNIT)
                pair(QTILES - 1, UNIT2)
                n1 = n0 + 2 * QTILES
                if q == 3:
                    link(dve.memset(ct[0][:, :], 0.0))

                def down(m, b, cols):
                    if cols:
                        split_lo(n1 + m + 1, 1 - b, cols)
                    dve.wait_ge(w_used, 2 + n1 + m + 1)
                    ins = stt(xacc[:, m, :], ps[2 + b][:, :], mod_x[:, bass.ds(5 * KT + m, 1)], xacc[:, m, :], MUL, ADD)
                    link(ins)
                    dve.sem_inc(fd_free, 1)
                    if q == 3:
                        add_square(m)

                with chain.loop(0, KT // 2 - 1, 6 if q == 3 else 2) as i:
                    for b in range(2):
                        down(2 * i + b, b, UNIT2)
                down(KT - 2, 0, UNIT2)
                down(KT - 1, 1, UNIT if q < 3 else 0)
            dve.sem_inc(s_acc, 1)
            rstd(3, ps[4][:, :], ct[1][:, :], ct[2][:, :], ct[3][:, :], ct[0][:, :], SEQ)
            for m in range(KT):
                stt(xacc[:, m, :], xacc[:, m, :], vecs[:, V_NO + m:V_NO + m + 1], ct[0][:, :], MUL, MUL).then_inc(o_rd, 1)

        @block.tensor
        def _(pe):
            mm = pe.matmul

            def product(out, wh, wl, xh, xl, nk, first=True, last=True):
                for k in range(nk):
                    mm(out, wh(k), xh(k), start=first and k == 0, stop=False)
                    mm(out, wh(k), xl(k), start=False, stop=False)
                    ins = mm(out, wl(k), xh(k), start=False, stop=last and k == nk - 1)
                return ins

            def w_tile(t, k0=0):
                return lambda k: t[:, (k0 + k) * P:(k0 + k + 1) * P]

            def x_tile(t):
                return lambda k: t[:, k, :]

            pe.wait_ge(s_cmod, 1)
            pe.wait_ge(s_silu, 1)

            def scale_row(k):
                pe.wait_ge(am_in[k % 2], 16 * (k // 2 + 1))
                for j in range(4):
                    ins = mm(ps[4 + j][0:2, :], silu_c[:, k, :], ada_m[k % 2][:, 512 * j:512 * j + 512],
                             start=k == 0, stop=k == KT - 1)
                ins.then_inc(am_used, 1)

            for k in range(4):
                scale_row(k)
            pe.wait_ge(s_filt, 96)
            mm(ps[0][0:HID, :], f1w[:, :], feats[:, :], start=True, stop=True).then_inc(s_h1p, 1)
            for k in range(4, 6):
                scale_row(k)
            pe.wait_ge(s_h1, 1)
            mm(ps[0][0:HID, :], f2w[:, :], fh[2][:, :], start=True, stop=True).then_inc(s_h1p, 1)
            pe.wait_ge(s_h1, 2)
            for t in range(4):
                pe.wait_ge(f3_free, t + 1)
                for c in range(4):
                    ins = mm(ps[c][:, :], fh[3][:, P * t:P * t + P], f3w[0:HID, 512 * c:512 * c + 512],
                             start=True, stop=True)
                ins.then_inc(f3_ps, 1)
                scale_row(6 + t)
            pe.wait_ge(f3_free, 5)
            for k in range(2 * KT):
                pe.wait_ge(s_sq, k + 1)
                dst, w = (ps[2], SEQ) if k < KT else (ps[3], CTX)
                ins = mm(dst[:, 0:w], ones[:, :], sqr[k % 2][:, 0:w], start=k % KT == 0, stop=k % KT == KT - 1)
                ins.then_inc(s_squ, 1)
                if k % 4 == 3 and k // 4 < 6:
                    scale_row(10 + k // 4)
                if k % KT == KT - 1:
                    pe.wait_ge(s_squ, 2 + k + 1)
                    pe.sem_inc(s_ss, 1)
            def spectrum_of_filter(st):
                f, cs = st // 2, st % 2
                if st >= 2:
                    pe.wait_ge(kf_free, st - 1)
                for half in range(2):
                    for t in range(4):
                        ins = mm(ps[2 * (st % 2) + half][:, :], tab_f[:, cs, t, P * f:P * f + P],
                                 (taps_s, taps_d)[cs][:, t, 512 * half:512 * half + 512], start=t == 0, stop=t == 3)
                ins.then_inc(kf_ps, 1)

            def reduce_shift(half):
                pe.wait_ge(as_used, 4 + KT * (half + 1))
                for j in range(8):
                    for v in range(2):
                        ins = mm(ps[5][:, 2 * (8 * half + j) + v:2 * (8 * half + j) + v + 1],
                                 acc_s[half][:, v, P * j:P * j + P], ones[:, 0:1], start=True, stop=True)
                ins.then_inc(as_red, 1)

            pe.wait_ge(s_tabf, 32)
            pe.wait_ge(s_tap, 4)
            spectrum_of_filter(0)
            pe.wait_ge(s_sqrt, 2)
            spectrum_of_filter(1)
            pe.wait_ge(am_row, 1)
            for j in range(KT):
                ins = mm(ps[4][:, 2 * j:2 * j + 2], row_m[0:2, P * j:P * j + P], ident[0:2, 0:2], start=True, stop=True)
            ins.then_inc(am_ps, 1)
            for st in range(2, 8):
                spectrum_of_filter(st)
                if st == 5:
                    reduce_shift(0)
            reduce_shift(1)

            def ada_columns(g):
                pe.wait_ge(ada1_used, 16 * (g + 1) + 1)
                for j in range(8):
                    ins = mm(ps[7][:, bass.ds(8 * g + j, 1)], acc1[:, P * j:P * j + P], ones[:, 0:1],
                             start=True, stop=True)
                ins.then_inc(acc1_red, 1)

            pe.wait_ge(kf_free, 8)

            def u_unit(n, b, first=False):
                pe.wait_ge(w_lo, n + 1)
                pe.wait_ge(u_fa, n + 1)
                pe.wait_ge(u_fd, n + 1)
                for k in range(KT):
                    if first:
                        pe.wait_ge(s_hl, k + 1)
                        pe.wait_ge(cl_, k + 1)
                    wh, wl = w_tile(hi[b])(k), w_tile(lo[b])(k)
                    for j, (w, xt, ct_) in enumerate(((wh, h_hi, hc_hi), (wh, h_lo, hc_lo), (wl, h_hi, hc_hi))):
                        s0, s1 = k == 0 and j == 0, k == KT - 1 and j == 2
                        mm(ps[b][:, :], w, xt[:, k, :], start=s0, stop=s1)
                        ins = mm(ps[2 + b][:, 0:CTX], w, ct_[:, k, :], start=s0, stop=s1)
                ins.then_inc(w_used, 1)

            u_unit(0, 0, True)
            u_unit(1, 1)
            with pe.Fori(1, 4) as i:
                for b in range(2):
                    u_unit(2 * i + b, b)
            pe.wait_ge(u_fa, 10)

            def unit(n, b, free):
                pe.wait_ge(w_lo, n + 1)
                pe.wait_ge(*free)
                ins = product(ps[b][:, :], w_tile(hi[b]), w_tile(lo[b]), x_tile(h_hi), x_tile(h_lo), KT)
                ins.then_inc(w_used, 1)

            for part in range(3):
                ada_columns(part)
                with pe.Fori(0, 4) as i:
                    for b in range(2):
                        t = 8 * part + 2 * i + b
                        unit(8 + t, b, (hy_free, t + 1))
            pe.wait_ge(hy_free, 26)
            with pe.Fori(0, 4) as g:
                ada_columns(3 + g)
                for j in range(8):
                    unit(32 + 8 * g + j, j % 2, (g_free, 8 * g + j + 1))
            ada_columns(7)
            pe.wait_ge(g_free, 34)
            pe.wait_ge(u4a, 4)
            pe.wait_ge(u4d, 1)
            with pe.Fori(0, NPAIR) as q:
                for d in range(2):
                    pe.wait_ge(bl_rd[d], q + 1)
                    pe.wait_ge(mt_rd, 2 * q + d + 1)
                    for ri in range(2):
                        for a in range(2):
                            ins = pe.transpose(ps[d][:, (2 * ri + a) * P:(2 * ri + a + 1) * P],
                                               BL[d][:, ri, 4 * a:4 * a + 4, :].rearrange("p j h -> p (j h)"),
                                               ident[:, :])
                    ins.then_inc(bl_tr, 1)
                for d in range(2):
                    pe.wait_ge(mt_rd, 2 * q + d + 3)
                    pe.wait_ge(xs_ev, 2 * q + d + 1)
                    for ri in range(2):
                        for a in range(2):
                            ins = mm(ps[2 + d][:, NCH * ri:NCH * ri + NCH], MT[d][:, 2 * ri + a, :],
                                     U4[:, q, a::2], start=a == 0, stop=a == 1)
                    ins.then_inc(xs_ps, 1)
            pe.wait_ge(rec_dn, 1)

            def taps(q, j):
                for d in range(2):
                    pe.wait_ge(cl_rd[d], q + 1)
                pe.wait_ge(bb_rd, q + 1)
                pe.wait_ge(tl_a, q + 1)
                pe.wait_ge(tl_d, q + 1)
                par = j % 2
                jobs = [(1, 0, 256, 1), (0, 224, 256, 0), (0, 256, 480, 1)]
                for n, (d, c0, c1, i0) in enumerate(jobs):
                    for ri in range(2):
                        rhs = CL[j][d][:, ri, i0:i0 + (c1 - c0) // 32, :].rearrange("p m h -> p (m h)")
                        ins = mm(ps[4 + 2 * par][:, c0:c1], BB[j][d][:, ri, :, :].rearrange("p a b -> p (a b)"),
                                 rhs, start=n == 0 and ri == 0, stop=ri == 1 and n == 2, skip_group_check=True)
                ins.then_inc(l_ps, 1)

            def chunk_outputs(q, j):
                par, C = j % 2, CL[j]
                pe.wait_ge(tl_a, q + 3)
                pe.wait_ge(tl_d, q + 3)
                pe.wait_ge(y_ev, q + 1)
                for a in range(2):
                    out = ps[5 + 2 * par][:, NC_LAT * a:NC_LAT * a + NC_LAT]
                    for ri in range(2):
                        mm(out, C[0][:, ri, 4 * a + 1:4 * a + 5, :].rearrange("p m h -> p (m h)"),
                           X[:, NC_CTX - 1:NCH - 1, ri, q], start=ri == 0, stop=False)
                        mm(out, C[1][:, ri, 4 * a:4 * a + 4, :].rearrange("p m h -> p (m h)"),
                           XR[j][:, ri, :], start=False, stop=False)
                    for ai in range(2):
                        ins = mm(out, TL[par][:, ai, 4 * a:4 * a + 4, :].rearrange("p m h -> p (m h)"),
                                 U4[:, q, CTX // 4 + ai::2], start=False, stop=ai == 1)
                ins.then_inc(y_ps, 1)

            taps(0, 0)
            with pe.Fori(0, NPAIR // 4 - 1) as i:
                for j in range(4):
                    taps(4 * i + j + 1, (j + 1) % 4)
                    chunk_outputs(4 * i + j, j)
            for j in range(4):
                q = NPAIR - 4 + j
                if j < 3:
                    taps(q + 1, j + 1)
                chunk_outputs(q, j)
            def transpose_u(half):
                for t in range(4):
                    n = 4 * half + t
                    if n >= 2:
                        pe.wait_ge(ut_l, n - 1)
                    for c in range(4):
                        ins = pe.transpose(ps[t % 2][:, P * c:P * c + P], uh[:, 4 * half + c, P * t:P * t + P], ident[:, :])
                    ins.then_inc(ut_ps, 1)

            def spectrum(half):
                for f in range(4):
                    n = 4 * half + f
                    if n >= 2:
                        pe.wait_ge(pq_ev, n - 1)
                    for s in range(2):
                        ins = product(ps[2 + 2 * (f % 2) + s][:, :], lambda t: tf_hi[:, s, t, P * f:P * f + P],
                                      lambda t: tf_lo[:, s, t, P * f:P * f + P], x_tile(uT_hi), x_tile(uT_lo), 4)
                    ins.then_inc(pq_ps, 1)

            def inverse(half):
                for c in range(4):
                    i = 4 * half + c
                    if i >= 2:
                        pe.wait_ge(cv_free, i - 1)
                    pe.wait_ge(yl, 8 * half + 8)
                    for s in range(2):
                        ins = product(ps[6 + i % 2][:, :], lambda f: Y_hi[:, s, f, P * c:P * c + P],
                                      lambda f: Y_lo[:, s, f, P * c:P * c + P], lambda f: tg_hi[:, s, f, :],
                                      lambda f: tg_lo[:, s, f, :], 4, first=s == 0, last=s == 1)
                    ins.then_inc(cv_ps, 1)

            transpose_u(0)
            pe.wait_ge(w_lo, U_TAB + 2)
            pe.wait_ge(ut_l, 4)
            spectrum(0)
            transpose_u(1)
            pe.wait_ge(w_lo, U_TAB + 4)
            inverse(0)
            pe.wait_ge(ut_l, 8)
            spectrum(1)
            inverse(1)
            pe.wait_ge(cv_ps, 8)
            pe.sem_inc(w_used, 4)
            pe.wait_ge(ygl, 2)
            pe.wait_ge(ol, 8)
            with pe.Fori(0, KT // 2) as i:
                for b in range(2):
                    m, n = 2 * i + b, U_MRG + 4 * i + 2 * b
                    pe.wait_ge(w_lo, n + 1)
                    pe.wait_ge(m_free, m + 1)
                    product(ps[3 * b][:, :], w_tile(hi[0]), w_tile(lo[0]), x_tile(yg_hi), x_tile(yg_lo), ST)
                    ins = product(ps[3 * b + 1][:, :], w_tile(hi[0], ST), w_tile(lo[0], ST), x_tile(yg_hi), x_tile(yg_lo), ST)
                    ins.then_inc(w_used, 1)
                    pe.wait_ge(w_lo, n + 2)
                    ins = product(ps[3 * b + 2][:, :], w_tile(hi[1]), w_tile(lo[1]), x_tile(hyo_hi), x_tile(hyo_lo), ST)
                    ins.then_inc(w_used, 1)
            pe.wait_ge(m_lo, KT)
            with pe.Fori(0, KT // 2) as i:
                for b in range(2):
                    m = 2 * i + b
                    pe.wait_ge(w_lo, U_OUT + m + 1)
                    pe.wait_ge(o_free, m + 1)
                    ins = product(ps[6 + b][:, :], w_tile(hi[b]), w_tile(lo[b]), x_tile(mg_hi), x_tile(mg_lo), KT)
                    ins.then_inc(w_used, 1)
            pe.wait_ge(s_acc, 1)
            mm(ps[4][:, :], ones[:, :], ct[0][:, :], start=True, stop=True).then_inc(s_ss, 1)
            def first_unit():
                pe.wait_ge(w_lo, U_FFN + 1)
                pe.wait_ge(fa_free, 1)
                for k in range(KT):
                    pe.wait_ge(s_hl, KT + k + 1)
                    wh, wl = w_tile(hi[0])(k), w_tile(lo[0])(k)
                    mm(ps[0][:, :], wh, h2_hi[:, k, :], start=k == 0, stop=False)
                    mm(ps[0][:, :], wh, h2_lo[:, k, :], start=False, stop=False)
                    ins = mm(ps[0][:, :], wl, h2_hi[:, k, :], start=False, stop=k == KT - 1)
                ins.then_inc(w_used, 1)

            def second_unit():
                pe.wait_ge(w_lo, U_FFN + 2)
                pe.wait_ge(ft_rd, 1)
                ins = product(ps[1][:, :], w_tile(hi[1]), w_tile(lo[1]), x_tile(h2_hi), x_tile(h2_lo), KT)
                ins.then_inc(w_used, 1)

            first_unit()
            second_unit()
            for q in range(4):
                n0, g0 = U_FFN + U_QUARTER * q, QTILES * q
                with pe.Fori(1 if q == 0 else 0, QTILES) as i:
                    for b, free in enumerate((fa_free, ft_rd)):
                        n = n0 + 2 * i + b
                        pe.wait_ge(w_lo, n + 1)
                        pe.wait_ge(free, g0 + i + 1)
                        ins = product(ps[b][:, :], w_tile(hi[b]), w_tile(lo[b]), x_tile(h2_hi), x_tile(h2_lo), KT)
                        ins.then_inc(w_used, 1)
                n1 = n0 + 2 * QTILES
                pe.wait_ge(fl_rd, g0 + QTILES)
                with pe.Fori(0, KT // 2) as i:
                    for b in range(2):
                        m = 2 * i + b
                        pe.wait_ge(w_lo, n1 + m + 1)
                        pe.wait_ge(fd_free, KT * q + m + 1)
                        ins = product(ps[2 + b][:, :], w_tile(hi[b]), w_tile(lo[b]), x_tile(a_hi), x_tile(a_lo), QTILES)
                        ins.then_inc(w_used, 1)
            pe.wait_ge(s_acc, 2)
            mm(ps[4][:, :], ones[:, :], ct[0][:, :], start=True, stop=True).then_inc(s_ss, 1)


def tables():
    f32 = np.float32
    quarter = D // 4
    omega = (f32(10000.0) ** (-np.arange(quarter, dtype=f32) / f32(quarter))).astype(f32)
    rows = (np.arange(SEQ // GRID, dtype=f32)[None, :] * omega[:, None]).astype(f32)
    cols = (np.arange(GRID, dtype=f32)[None, :] * omega[:, None]).astype(f32)
    pos_r = np.concatenate([np.sin(rows), np.cos(rows)]).reshape(8, P, SEQ // GRID)
    pos_c = np.concatenate([np.sin(cols), np.cos(cols)]).reshape(8, P, GRID)
    postab = np.ascontiguousarray(np.concatenate([pos_r, pos_c], axis=2).transpose(1, 0, 2)).astype(f32)
    pos = np.arange(SEQ, dtype=f32)
    t = (pos / f32(SEQ - 1)).astype(f32)
    w = (f32(2.0 * math.pi) * pos / f32(SEQ)).astype(f32)
    bands = np.linspace(1e-4, BANDS - 1, BANDS).astype(f32)
    ang = (w[:, None] * bands).astype(f32)
    feats = np.concatenate([t[:, None], np.cos(ang), -np.sin(ang)], axis=1).astype(f32)
    negt = np.ascontiguousarray((-t).reshape(4, P).T)
    theta = np.pi * (2 * np.arange(SEQ) + 1)[:, None] * np.arange(SEQ)[None, :] / (2 * SEQ)
    cos, sin = np.cos(theta), np.sin(theta)

    def tiled(m):
        return m.reshape(4, P, SEQ).transpose(1, 0, 2).reshape(P, 4 * SEQ)

    tabs = np.stack([tiled(cos.T), tiled(sin.T), tiled(cos / SEQ), tiled(sin / SEQ)]).astype(f32)
    return postab, np.ascontiguousarray(feats.T), negt, tabs, np.eye(P, dtype=f32)


def kernel(**inputs):
    import concourse.bacc as bacc
    from concourse.bass_utils import run_bass_kernel_spmd

    a = {k: np.asarray(v) for k, v in inputs.items()}
    postab, feats, negt, tabs, ident = tables()
    cont = np.ascontiguousarray

    def units(w):
        r, c = w.shape
        return cont(w.reshape(r // P, P, c // P, P).transpose(2, 1, 0, 3).reshape(c // P, P, r))

    def by_channel(v):
        return v.reshape(-1, P).T

    w_in = units(a["w_in"][0])
    hy = [8 * part + 8 + i for part in (1, 2, 0) for i in range(ST)]
    w_in = cont(w_in[list(range(8)) + hy + list(range(32, 64))])
    conv = a["hy_conv_w"][0].reshape(3, 24, P)[:, [h - 8 for h in hy]]
    conv_b = a["hy_conv_b"][0].reshape(24, P)[[h - 8 for h in hy]]
    glu = units(a["w_glu"][0])
    w_glu = cont(np.concatenate([glu[:KT], glu[KT:]], axis=2))
    fi = units(a["w_ffn_in"][0])
    w_fi = cont(np.stack([fi[:DFF // P], fi[DFF // P:]], axis=1).reshape(2 * DFF // P, P, UNIT))
    fo = a["w_ffn_out"][0].reshape(4, QTILES, P, KT, P)
    w_fo = cont(fo.transpose(0, 3, 2, 1, 4).reshape(4 * KT, P, UNIT2))
    d4 = np.tile(a["s5_d"][0].reshape(NPAIR, 32).T, (4, 1))
    vecs = cont(np.concatenate([
        by_channel(a["norm_mix"][0]), by_channel(a["norm_ffn"][0]), by_channel(a["norm_f"]),
        by_channel(a["c"][0]), by_channel(a["c_ctx"]), by_channel(a["b_ada"][0]),
        conv.reshape(72, P).T, conv_b.T, by_channel(a["hy_bias"][0]), d4, negt], axis=1))

    def poles(v):
        return v.reshape(2, NPAIR, 2, STATE).transpose(2, 3, 0, 1).reshape(P, NDQ)

    log_dt = np.broadcast_to(a["s5_log_dt"][0][:, :, None], (2, 2 * NPAIR, STATE))
    s5a = cont(np.stack([poles(a["s5_a_re"][0]), poles(a["s5_a_im"][0]), poles(log_dt)], axis=1))

    def modes(re, im, perm):
        v = np.stack([re, im]).transpose(perm)
        v = v.reshape(2, 2, NPAIR, 2, STATE, GROUP).transpose(3, 4, 1, 2, 0, 5)
        return cont(v.reshape(P, NDQ, 2, GROUP))

    ada = a["w_ada"][0].reshape(KT, P, 6 * D)
    w_as = cont(ada[:, :, :D].reshape(KT, P, 2, 1024).transpose(2, 0, 1, 3).reshape(2 * KT, P, 1024))
    w_am = cont(ada[:, :, D:2 * D])
    w_ar = cont(a["w_ada"][0][:, N_ADA0 * P:].reshape(KT, P, 8, 1024).transpose(2, 0, 1, 3).reshape(8 * KT, P, 1024))
    data = {
        "vecs": vecs, "w_as": w_as, "w_am": w_am, "w_ar": w_ar, "w_in": w_in, "w_glu": w_glu,
        "w_hy": units(a["w_hy_out"][0]), "w_out": units(a["w_out"][0]), "w_fi": w_fi, "w_fo": w_fo,
        "x": cont(a["x"][0].T.reshape(KT, P, SEQ).transpose(1, 0, 2)),
        "ctx": cont(a["ctx"][0].T.reshape(KT, P, CTX).transpose(1, 0, 2)),
        "s5a": s5a, "s5b": modes(a["s5_b_re"][0], a["s5_b_im"][0], (0, 1, 2, 3, 4)),
        "s5c": modes(a["s5_c_re"][0], a["s5_c_im"][0], (0, 1, 2, 4, 3)),
        "f1w": cont(a["hy_f1_w"][0]), "f2w": cont(a["hy_f2_w"][0]), "f3w": cont(a["hy_f3_w"][0]),
        "fpar": cont(np.stack([a["hy_f1_b"][0], a["hy_f1_freq"][0], a["hy_f2_b"][0], a["hy_f2_freq"][0]], axis=1)),
        "decay": cont(a["hy_decay"][0].reshape(1, 2 * HYW)),
        "feats": feats, "postab": postab, "tabs": tabs, "ident": ident,
    }
    nc = bacc.Bacc("TRN2", target_bir_lowering=False, num_devices=1)
    arrays, args = {}, []
    for name, v in data.items():
        arrays[f"in_{name}"] = v
        args.append(nc.dram_tensor(f"in_{name}", v.shape, F32, kind="ExternalInput").ap())
    args.append(nc.dram_tensor("out", (KT, P, SEQ), F32, kind="ExternalOutput").ap())
    args.append(nc.dram_tensor("xp", (P, KT, SEQ), F32, kind="Internal").ap())
    args.append(nc.dram_tensor("gates", (2 * KT, P, SEQ), F32, kind="Internal").ap())
    args.append(nc.dram_tensor("kf", (4, 2, P, HYW), F32, kind="Internal").ap())
    block_kernel(nc, *args)
    got = run_bass_kernel_spmd(nc, [arrays], core_ids=[0]).results[0]["out"]
    return got.reshape(D, SEQ).T.reshape(1, SEQ, D)
```
